# Optimizing a Trainium2 kernel written in Bass

```python
import math
import functools
import jax
import jax.numpy as jnp
from jax import lax
import numpy as np

D_MODEL = 1024
BATCH = 1
SEQ = 512
DEPTH = 2
DEC_BATCH = 8
DEC_SEQ = 4
PAST_LEN = 1024
PAGE_SIZE = 128

DN_HEADS = 4
DN_DK = 128
DN_DV = 128
DN_CONV = 4
DN_QKV = 2 * DN_HEADS * DN_DK + DN_HEADS * DN_DV
RET_HEADS = 4
RET_DK = 128
RET_DV = 128
ROPE_BASE = 10000.0
ATT_HEADS = 4
ATT_DH = 128
IDX_HEADS = 4
IDX_DIM = 64
TOPK_MAX = 256
Q_BLOCK = 128
N_BUCKETS = 32
MAX_DISTANCE = 128
CHUNK = 64
N_BRANCH = 3
BRANCH_W = DN_HEADS * DN_DV
D_FF = 2816
FFN_CONV = 3
EPS = 1e-6
F32 = jnp.float32
IN_SIZES = (DN_QKV, DN_HEADS * DN_DV, DN_HEADS, DN_HEADS,
            RET_HEADS * RET_DK, RET_HEADS * RET_DK, RET_HEADS * RET_DV, RET_HEADS * RET_DV,
            ATT_HEADS * ATT_DH, ATT_HEADS * ATT_DH, ATT_HEADS * ATT_DH,
            IDX_HEADS * IDX_DIM, IDX_DIM, IDX_HEADS, N_BRANCH * D_MODEL)
IN_COLS = sum(IN_SIZES)

kernel_name = 'hybrid_delta_retention_dsa_step'

def _rms(x, g):
    xf = x.astype(F32)
    y = xf * lax.rsqrt(jnp.mean(xf * xf, axis=-1, keepdims=True) + EPS)
    return (y * g.astype(F32)).astype(x.dtype)

def _group_norm(x, g):
    xf = x.astype(F32)
    mu = jnp.mean(xf, axis=-1, keepdims=True)
    xc = xf - mu
    var = jnp.mean(xc * xc, axis=-1, keepdims=True)
    return (xc * lax.rsqrt(var + EPS) * g.astype(F32)).astype(x.dtype)

def _l2norm(x):
    xf = x.astype(F32)
    return (xf * lax.rsqrt(jnp.sum(xf * xf, axis=-1, keepdims=True) + EPS)).astype(x.dtype)

def _split_cols(z):
    offs = np.cumsum(np.array(IN_SIZES))[:-1].tolist()
    return jnp.split(z, offs, axis=-1)

def _causal_conv(x, prev, w):
    width = w.shape[0]
    L = x.shape[1]
    xc = jnp.concatenate([prev.astype(x.dtype), x], axis=1)
    y = sum(xc[:, i:i + L] * w[i] for i in range(width))
    return y, xc[:, L:]

def _rotary(x, pos):
    half = x.shape[-1] // 2
    inv = 1.0 / (ROPE_BASE ** jnp.linspace(0.0, 1.0, half, dtype=F32))
    ang = pos.astype(F32)[:, None] * inv
    cos = jnp.cos(ang)[:, None, :]
    sin = jnp.sin(ang)[:, None, :]
    xf = x.astype(F32)
    x1, x2 = xf[..., :half], xf[..., half:]
    return jnp.concatenate([x1 * cos - x2 * sin, x1 * sin + x2 * cos], axis=-1).astype(x.dtype)

def _chunked_recurrence(q, k, v, g, beta, s0):
    B, L, H, DK = q.shape
    DV = v.shape[-1]
    C = min(CHUNK, L)
    n = -(-L // C)
    pad = n * C - L

    def prep(t):
        t = t.astype(F32)
        t = jnp.pad(t, [(0, 0), (0, pad)] + [(0, 0)] * (t.ndim - 2))
        t = t.reshape((B, n, C) + t.shape[2:])
        return jnp.moveaxis(t, (1, 2), (0, 3))

    qc, kc, vc, gc = prep(q), prep(k), prep(v), prep(g)
    G = jnp.cumsum(gc, axis=-1)
    incl = jnp.tril(jnp.ones((C, C), bool))
    diff = G[..., :, None] - G[..., None, :]
    decay = jnp.where(incl, jnp.exp(jnp.where(incl, diff, 0.0)), 0.0)
    qk = jnp.einsum('nbhid,nbhjd->nbhij', qc, kc) * decay
    if beta is None:
        u, kcum = vc, None
    else:
        bc = prep(beta)
        strict = jnp.tril(jnp.ones((C, C), bool), -1)
        m = jnp.where(strict, jnp.einsum('nbhid,nbhjd->nbhij', kc, kc) * decay * bc[..., :, None], 0.0)
        a = m + jnp.eye(C, dtype=F32)
        rhs = jnp.concatenate([vc * bc[..., None], kc * (bc * jnp.exp(G))[..., None]], axis=-1)
        sol = lax.linalg.triangular_solve(a, rhs, left_side=True, lower=True, unit_diagonal=True)
        u, kcum = sol[..., :DV], sol[..., DV:]
    q_dec = qc * jnp.exp(G)[..., None]
    k_dec = kc * jnp.exp(G[..., -1:] - G)[..., None]
    g_tot = jnp.exp(G[..., -1])[..., None, None]

    def step(s, xs):
        u_c, kcum_c, qd, kd, qk_c, gt = xs
        w = u_c if kcum_c is None else u_c - jnp.einsum('bhck,bhkv->bhcv', kcum_c, s)
        o = jnp.einsum('bhck,bhkv->bhcv', qd, s) + jnp.einsum('bhij,bhjv->bhiv', qk_c, w)
        s = s * gt + jnp.einsum('bhck,bhcv->bhkv', kd, w)
        return s, o

    s_fin, o = lax.scan(step, s0.astype(F32), (u, kcum, q_dec, k_dec, qk, g_tot))
    o = jnp.moveaxis(o, (0, 3), (1, 2)).reshape(B, n * C, H, DV)[:, :L]
    return o.astype(v.dtype), s_fin.astype(s0.dtype)

def _t5_bucket(dist):
    exact = N_BUCKETS // 2
    d = dist.astype(F32)
    large = exact + (jnp.log(jnp.maximum(d, 1.0) / exact) / math.log(MAX_DISTANCE / exact)
                     * (N_BUCKETS - exact)).astype(jnp.int32)
    large = jnp.minimum(large, N_BUCKETS - 1)
    return jnp.where(dist < exact, dist, large)

def _index_select(qi, wi, ki, qpos, kpos, topk):
    s = jnp.einsum('bqhd,bld->bqhl', qi.astype(F32), ki.astype(F32)) * IDX_DIM ** -0.5
    score = jnp.einsum('bqhl,bqh->bql', jax.nn.relu(s), wi.astype(F32)) * IDX_HEADS ** -0.5
    adm = kpos[None, None, :] <= qpos[None, :, None]
    score = jnp.where(adm, score, -jnp.inf)
    _, idx = lax.top_k(score, topk)
    valid = idx <= qpos[None, :, None]
    return idx, valid

def _attend_selected(q, ksel, vsel, qpos, kpos, valid, rel_bias):
    logits = jnp.einsum('bqhd,bqkhd->bqhk', q, ksel, preferred_element_type=F32) * ATT_DH ** -0.5
    bucket = _t5_bucket(jnp.maximum(qpos[None, :, None] - kpos, 0))
    bias = jnp.moveaxis(rel_bias.astype(F32)[bucket], -1, 2)
    logits = jnp.where(valid[:, :, None, :], logits + bias, -jnp.inf)
    p = jax.nn.softmax(logits, axis=-1)
    return jnp.einsum('bqhk,bqkhd->bqhd', p.astype(vsel.dtype), vsel)

def _gather_rows(a, i):
    return jax.vmap(lambda ab, ib: ab[ib])(a, i)

def _dsa_prompt(q, k, v, qi, ki, wi, rel_bias):
    B, S, H, Dh = q.shape
    topk = min(TOPK_MAX, S // 4)
    kpos = jnp.arange(S)

    def block(i):
        st = i * Q_BLOCK
        sl = lambda t: lax.dynamic_slice_in_dim(t, st, Q_BLOCK, axis=1)
        qpos = st + jnp.arange(Q_BLOCK)
        idx, valid = _index_select(sl(qi), sl(wi), ki, qpos, kpos, topk)
        return _attend_selected(sl(q), _gather_rows(k, idx), _gather_rows(v, idx), qpos, idx, valid, rel_bias)

    o = lax.map(block, jnp.arange(S // Q_BLOCK))
    return jnp.moveaxis(o, 0, 1).reshape(B, S, H, Dh)

def _dsa_sample(q, k, v, qi, ki, wi, layer, cache_k, cache_v, cache_kidx, page_table, rel_bias):
    DB, DS, H, Dh = q.shape
    past = page_table.shape[1] * PAGE_SIZE
    L = past + DS
    topk = min(TOPK_MAX, L // 4)
    ki_past = cache_kidx[layer, page_table].reshape(DB, past, IDX_DIM)
    ki_all = jnp.concatenate([ki_past.astype(ki.dtype), ki], axis=1)
    qpos = past + jnp.arange(DS)
    idx, valid = _index_select(qi, wi, ki_all, qpos, jnp.arange(L), topk)
    pidx = jnp.minimum(idx, past - 1)
    phys = _gather_rows(page_table, pidx // PAGE_SIZE) * PAGE_SIZE + pidx % PAGE_SIZE
    nidx = jnp.clip(idx - past, 0, DS - 1)
    in_past = (idx < past)[..., None, None]

    def pick(pool, new):
        flat = pool.reshape((pool.shape[0], -1) + pool.shape[3:])
        return jnp.where(in_past, flat[layer, phys].astype(new.dtype), _gather_rows(new, nidx))

    return _attend_selected(q, pick(cache_k, k), pick(cache_v, v), qpos, idx, valid, rel_bias)

def _layer(x, pos, dn_conv0, dn_s0, ret_s0, ffn_conv0, attend,
           norm_mix, w_in, dn_conv_w, dn_a_log, dn_dt_bias, dn_norm, ret_norm,
           w_branch, w_o, norm_ffn, w_up, ffn_conv_w, w_down):
    B, L, _ = x.shape
    u = _rms(x, norm_mix)
    (dn_qkv, dn_z, dn_b, dn_a, r_q, r_k, r_v, r_g,
     a_q, a_k, a_v, i_q, i_k, i_w, gate) = _split_cols(jnp.einsum('bld,dc->blc', u, w_in))
    heads = lambda t, h: t.reshape(B, L, h, -1)

    c, dn_conv_new = _causal_conv(dn_qkv, dn_conv0, dn_conv_w)
    q, k, v = jnp.split(jax.nn.silu(c), [DN_HEADS * DN_DK, 2 * DN_HEADS * DN_DK], axis=-1)
    q = _l2norm(heads(q, DN_HEADS)) * DN_DK ** -0.5
    k = _l2norm(heads(k, DN_HEADS))
    beta = jax.nn.sigmoid(dn_b.astype(F32))
    g = -jnp.exp(dn_a_log.astype(F32)) * jax.nn.softplus(dn_a.astype(F32) + dn_dt_bias.astype(F32))
    o_a, dn_s_new = _chunked_recurrence(q, k, heads(v, DN_HEADS), g, beta, dn_s0)
    o_a = _rms(o_a, dn_norm) * jax.nn.silu(heads(dn_z, DN_HEADS))

    rq = _rotary(heads(r_q, RET_HEADS), pos) * RET_DK ** -0.5
    rk = _rotary(heads(r_k, RET_HEADS), pos)
    log_gamma = jnp.log1p(-jnp.exp2(-5.0 - jnp.arange(RET_HEADS, dtype=F32)))
    g_r = jnp.broadcast_to(log_gamma, (B, L, RET_HEADS))
    o_b, ret_s_new = _chunked_recurrence(rq, rk, heads(r_v, RET_HEADS), g_r, None, ret_s0)
    o_b = _group_norm(o_b, ret_norm) * jax.nn.silu(heads(r_g, RET_HEADS))

    k_c = heads(a_k, ATT_HEADS)
    v_c = heads(a_v, ATT_HEADS)
    o_c = attend(heads(a_q, ATT_HEADS), k_c, v_c, heads(i_q, IDX_HEADS), i_k, i_w)

    br = jnp.stack([o_a.reshape(B, L, BRANCH_W), o_b.reshape(B, L, BRANCH_W),
                    o_c.reshape(B, L, BRANCH_W)], axis=2)
    br = jnp.einsum('blnc,ncd->blnd', br, w_branch)
    gates = jax.nn.sigmoid(gate.reshape(B, L, N_BRANCH, D_MODEL))
    h = x + jnp.einsum('bld,de->ble', jnp.sum(gates * br, axis=2), w_o)

    a, ffn_conv_new = _causal_conv(jnp.einsum('bld,df->blf', _rms(h, norm_ffn), w_up), ffn_conv0, ffn_conv_w)
    a_gate, a_val = jnp.split(a, 2, axis=-1)
    y = h + jnp.einsum('blf,fd->bld', jax.nn.silu(a_gate) * a_val, w_down)
    return y, (dn_conv_new, dn_s_new, ret_s_new, k_c, v_c, i_k, ffn_conv_new)

def setup_inputs(seed: int = 0) -> dict:
    key = jax.random.key(seed)
    ks = jax.random.split(key, 32)
    nrm = lambda i, shape, scale: jax.random.normal(ks[i], shape, F32) * scale
    n_pages = PAST_LEN // PAGE_SIZE
    n_used = DEC_BATCH * n_pages
    n_phys = n_used + max(1, n_used // 4)
    page_table = jax.random.permutation(ks[0], n_phys)[:n_used].reshape(DEC_BATCH, n_pages).astype(jnp.int32)
    dt = jnp.exp(jax.random.uniform(ks[1], (DEPTH, DN_HEADS), F32, math.log(1e-3), math.log(1e-1)))
    dn_dt_bias = dt + jnp.log(-jnp.expm1(-dt))
    dn_a_log = jnp.log(jax.random.uniform(ks[2], (DEPTH, DN_HEADS), F32, 1.0, 16.0))
    return {
        'x_prompt': nrm(3, (BATCH, SEQ, D_MODEL), 1.0),
        'x_sample': nrm(4, (DEC_BATCH, DEC_SEQ, D_MODEL), 1.0),
        'cache_k': nrm(5, (DEPTH, n_phys, PAGE_SIZE, ATT_HEADS, ATT_DH), 1.0),
        'cache_v': nrm(6, (DEPTH, n_phys, PAGE_SIZE, ATT_HEADS, ATT_DH), 1.0),
        'cache_kidx': nrm(7, (DEPTH, n_phys, PAGE_SIZE, IDX_DIM), 1.0),
        'state_dn_conv': nrm(8, (DEPTH, DEC_BATCH, DN_CONV - 1, DN_QKV), 1.0),
        'state_dn': nrm(9, (DEPTH, DEC_BATCH, DN_HEADS, DN_DK, DN_DV), 0.1),
        'state_ret': nrm(10, (DEPTH, DEC_BATCH, RET_HEADS, RET_DK, RET_DV), 0.3),
        'state_ffn_conv': nrm(11, (DEPTH, DEC_BATCH, FFN_CONV - 1, 2 * D_FF), 1.0),
        'page_table': page_table,
        'norm_mix': 1.0 + nrm(12, (DEPTH, D_MODEL), 0.02),
        'w_in': nrm(13, (DEPTH, D_MODEL, IN_COLS), D_MODEL ** -0.5),
        'dn_conv_w': nrm(14, (DEPTH, DN_CONV, DN_QKV), DN_CONV ** -0.5),
        'dn_a_log': dn_a_log,
        'dn_dt_bias': dn_dt_bias,
        'dn_norm': 1.0 + nrm(15, (DEPTH, DN_DV), 0.02),
        'ret_norm': 1.0 + nrm(16, (DEPTH, RET_HEADS, RET_DV), 0.02),
        'rel_bias': nrm(17, (N_BUCKETS, ATT_HEADS), 0.5),
        'w_branch': nrm(18, (DEPTH, N_BRANCH, BRANCH_W, D_MODEL), BRANCH_W ** -0.5),
        'w_o': nrm(19, (DEPTH, D_MODEL, D_MODEL), D_MODEL ** -0.5),
        'norm_ffn': 1.0 + nrm(20, (DEPTH, D_MODEL), 0.02),
        'w_up': nrm(21, (DEPTH, D_MODEL, 2 * D_FF), D_MODEL ** -0.5),
        'ffn_conv_w': nrm(22, (DEPTH, FFN_CONV, 2 * D_FF), FFN_CONV ** -0.5),
        'w_down': nrm(23, (DEPTH, D_FF, D_MODEL), D_FF ** -0.5),
        'norm_final': 1.0 + nrm(24, (D_MODEL,), 0.02),
    }

def reference(x_prompt, x_sample, cache_k, cache_v, cache_kidx, state_dn_conv, state_dn, state_ret,
              state_ffn_conv, page_table, norm_mix, w_in, dn_conv_w, dn_a_log, dn_dt_bias, dn_norm,
              ret_norm, rel_bias, w_branch, w_o, norm_ffn, w_up, ffn_conv_w, w_down, norm_final):
    B, S, _ = x_prompt.shape
    DB, DS, _ = x_sample.shape
    pos_p = jnp.arange(S)
    pos_s = PAST_LEN + jnp.arange(DS)
    xp, xs = x_prompt, x_sample
    dt = x_prompt.dtype
    p_states, s_states = [], []
    attend_p = functools.partial(_dsa_prompt, rel_bias=rel_bias)
    for l in range(DEPTH):
        lw = (norm_mix[l], w_in[l], dn_conv_w[l], dn_a_log[l], dn_dt_bias[l], dn_norm[l], ret_norm[l],
              w_branch[l], w_o[l], norm_ffn[l], w_up[l], ffn_conv_w[l], w_down[l])
        xp, st = _layer(xp, pos_p,
                        jnp.zeros((B, DN_CONV - 1, DN_QKV), dt),
                        jnp.zeros((B, DN_HEADS, DN_DK, DN_DV), dt),
                        jnp.zeros((B, RET_HEADS, RET_DK, RET_DV), dt),
                        jnp.zeros((B, FFN_CONV - 1, 2 * D_FF), dt),
                        attend_p, *lw)
        p_states.append(st)
        attend_s = functools.partial(_dsa_sample, layer=l, cache_k=cache_k, cache_v=cache_v,
                                     cache_kidx=cache_kidx, page_table=page_table, rel_bias=rel_bias)
        xs, st = _layer(xs, pos_s, state_dn_conv[l], state_dn[l], state_ret[l], state_ffn_conv[l],
                        attend_s, *lw)
        s_states.append(st)
    y_prompt = _rms(xp, norm_final)
    y_sample = _rms(xs, norm_final)
    stk = lambda states, i: jnp.stack([st[i] for st in states])
    p_dn_conv, p_dn, p_ret = stk(p_states, 0), stk(p_states, 1), stk(p_states, 2)
    p_k, p_v, p_kidx, p_ffn_conv = stk(p_states, 3), stk(p_states, 4), stk(p_states, 5), stk(p_states, 6)
    s_dn_conv, s_dn, s_ret = stk(s_states, 0), stk(s_states, 1), stk(s_states, 2)
    s_k, s_v, s_kidx, s_ffn_conv = stk(s_states, 3), stk(s_states, 4), stk(s_states, 5), stk(s_states, 6)
    return (y_prompt, y_sample, p_dn_conv, p_dn, p_ret, p_k, p_v, p_kidx, p_ffn_conv,
            s_dn_conv, s_dn, s_ret, s_k, s_v, s_kidx, s_ffn_conv)


_drawn_inputs = setup_inputs


def setup_inputs(seed=0):
    import zlib

    import numpy as np

    out = dict(_drawn_inputs(seed))
    spreads = {}
    factors = {'dn_norm': 4.786, 'ret_norm': 4.598, 'norm_final': 2.847}
    for name, (base, spread) in spreads.items():
        noise = np.random.default_rng([zlib.crc32(name.encode()), seed]).standard_normal(out[name].shape)
        drawn = base * np.exp(spread * noise) if base else spread * noise
        out[name] = jnp.asarray(drawn.astype(out[name].dtype))
    for name, factor in factors.items():
        out[name] = (out[name] * factor).astype(out[name].dtype)
    return out
```

```python
from contextlib import ExitStack

import numpy as np

import concourse.bass as bass
from concourse import mybir

F32 = mybir.dt.float32
F32R = mybir.dt.float32r
I32 = mybir.dt.int32
ALU = mybir.AluOpType
ACT = mybir.ActivationFunctionType
AX = mybir.AxisListType

P = 128
D = 1024
KD = D // P
SEQ, DB, DS = 512, 8, 4
NS = DB * DS
NT = SEQ + NS
HT = NT // 2
DEPTH = 2
H = 4
PAST, PAGE = 1024, 128
NPG = PAST // PAGE
NEWK = PAST + NS
DFF = 2816
FT = DFF // P
FH = FT // 2
NBUCKET = 32
TOPK_P, TOPK_S = 128, 256
EPS = 1e-6
SCALE = float(P) ** -0.5
NEG, TAKEN = -1.0e30, -3.0e38
DW, SW = 515 + DB * 7, 514 + DB * 6
COL = {}
_o = 0
for _n, _w in (('dn', 1536), ('z', 512), ('b', 4), ('a', 4), ('rq', 512), ('rk', 512), ('rv', 512), ('rg', 512),
               ('aq', 512), ('ak', 512), ('av', 512), ('iq', 256), ('ik', 64), ('iw', 4), ('gate', 3072)):
    COL[_n] = _o
    _o += _w



def bucket(d):
    d = np.asarray(d)
    f = np.maximum(d.astype(np.float32), np.float32(1.0)) / np.float32(16)
    large = 16 + (np.log(f) / np.float32(np.log(128 / 16)) * np.float32(16)).astype(np.int32)
    return np.where(d < 16, d, np.minimum(large, 31))


def one_hot(d):
    return ((bucket(np.maximum(d, 0))[None] == np.arange(NBUCKET)[:, None]) & (d >= 0)[None]).astype(np.float32)


def const_arrays():
    a = {}
    i, j = np.arange(P)[None, :], np.arange(P)[:, None]
    a['ident'] = (i == j)
    a['triu'] = (i >= j)
    a['level'] = np.concatenate([(i // (2 * s) == j // (2 * s)) & (i // s % 2 == 1) & (j // s % 2 == 0)
                                 for s in (1, 2, 4, 8, 16, 32, 64)], 1)
    a['causal'] = np.where(i > j, NEG, 0.0)
    lg = np.log1p(-np.exp2(-5.0 - np.arange(H)))
    a['r_decay'] = np.concatenate([np.where(i >= j, np.exp(lg[h] * np.maximum(i - j, 0)), 0.0) for h in range(H)], 1)
    a['r_q'] = np.concatenate([np.exp(lg[h] * (i + 1)) + 0.0 * j for h in range(H)], 1)
    a['r_k'] = np.exp(lg[None, :] * (P - 1 - j))
    s, t = np.arange(NS)[None, :], np.arange(NS)[:, None]
    same = (s // DS == t // DS)
    pad = lambda x: np.concatenate([x, np.zeros((P - x.shape[0], x.shape[1]))], 0)
    a['rs_decay'] = pad(np.concatenate([np.where(same & (s >= t), np.exp(lg[h] * np.maximum(s - t, 0)), 0.0)
                                        for h in range(H)], 1))
    a['rs_q'] = np.concatenate([np.exp(lg[h] * (s % DS + 1)) + 0.0 * j for h in range(H)], 1)
    a['rs_k'] = pad(np.exp(lg[None, :] * (DS - 1 - t % DS)))
    a['seq_of'] = pad((t // DS == np.arange(DB)[None, :]))
    a['triu_s'] = pad(same & (s >= t))
    a['after'] = (j > i)
    a['after_s'] = pad(same & (t > s))
    a['eps'] = np.full((P, 1), EPS)
    a['rep'] = pad((i % NS == t))
    a['causal_s'] = pad(np.where(same & (s <= t), 0.0, NEG))
    a['ones'] = np.ones((P, P))
    pos = np.concatenate([np.arange(SEQ), PAST + np.arange(NS) % DS]).astype(np.float32)
    inv = (np.float32(1.0) / (np.float32(10000.0) ** np.linspace(0.0, 1.0, 64, dtype=np.float32))).astype(np.float32)
    ang = inv[:, None] * pos[None, :]
    a['cos'] = np.concatenate([np.cos(ang)] * 2, 0)
    a['sin'] = np.concatenate([-np.sin(ang), np.sin(ang)], 0)
    return {k: np.asarray(v, np.float32) for k, v in a.items()}


def onehot_arrays():
    a = {'oh': one_hot(255 - np.arange(384))}
    c = np.arange(P)
    n = np.arange(NS)
    for t in range(DS):
        a[f'oh{t}'] = np.concatenate([one_hot(P + t - c), one_hot(t - n % DS)], 1)
        a[f'row{t}'] = np.broadcast_to((np.arange(P) % DS == t), (NBUCKET, P))
    return {k: np.asarray(v, np.float32) for k, v in a.items()}


class Counter:

    def __init__(self, sem, known):
        self.sem, self.known, self.count, self.values = sem, known, 0, {}

    def fresh(self):
        self.count = 0

    def next(self, key=None, by=1):
        self.count += by
        if key is not None:
            assert key not in self.values, key
            self.values[key] = self.count
        return by

    def at(self, key):
        return self.known[key] if self.known is not None else 1


class Bank:

    def __init__(self, ap, filled, drained, known):
        self.ap, self.filled, self.drained, self.known = ap, filled, drained, known
        self.uses, self.values = 0, {}

    def fresh(self):
        self.uses = 0

    def claim(self, key):
        assert key not in self.values, key
        self.uses += 1
        self.values[key] = self.uses
        return self.uses - 1

    def at(self, key):
        return self.known[key] if self.known is not None else 1


class Known:

    def __init__(self):
        self.tables = None
        self.made = {}

    def table(self, name):
        return None if self.tables is None else self.tables[name]

    def learned(self):
        k = Known()
        k.tables = {n: dict(s.values) for n, s in self.made.items()}
        return k


IN_NAMES = ['x_prompt', 'x_sample', 'cache_k', 'cache_v', 'cache_kidx', 'state_dn_conv', 'state_dn', 'state_ret',
            'state_ffn_conv', 'page_table', 'norm_mix', 'w_in', 'dn_conv_w', 'dn_a_log', 'dn_dt_bias', 'dn_norm',
            'ret_norm', 'rel_bias', 'w_branch', 'w_o', 'norm_ffn', 'w_up', 'ffn_conv_w', 'w_down', 'norm_final']
OUT_SHAPES = [
    ('y_prompt', (1, SEQ, D)), ('y_sample', (DB, DS, D)),
    ('p_dn_conv', (DEPTH, 1, 3, 1536)), ('p_dn', (DEPTH, 1, H, P, P)), ('p_ret', (DEPTH, 1, H, P, P)),
    ('p_k', (DEPTH, 1, SEQ, H, P)), ('p_v', (DEPTH, 1, SEQ, H, P)), ('p_kidx', (DEPTH, 1, SEQ, 64)),
    ('p_ffn_conv', (DEPTH, 1, 2, 2 * DFF)),
    ('s_dn_conv', (DEPTH, DB, 3, 1536)), ('s_dn', (DEPTH, DB, H, P, P)), ('s_ret', (DEPTH, DB, H, P, P)),
    ('s_k', (DEPTH, DB, DS, H, P)), ('s_v', (DEPTH, DB, DS, H, P)), ('s_kidx', (DEPTH, DB, DS, 64)),
    ('s_ffn_conv', (DEPTH, DB, 2, 2 * DFF))]

UNITS = ['iq', 'ik'] + [f'{n}{i}' for n in ('rq', 'rk', 'rv', 'rg', 'aq', 'ak', 'av') for i in range(2)] \
    + [f'dn{i}' for i in range(6)] + ['z0', 'z1'] \
    + [f'{w}{n}{d}' for n in range(3) for d in range(4) for w in ('gate', 'br')] \
    + [f'wo{i}' for i in range(4)] \
    + [x for f in range(2) for x in [f'up{f}_{j}' for j in range(FH)] + [f'down{f}_{c}' for c in range(KD)]]
UIDX = {u: i for i, u in enumerate(UNITS)}
NRAW, NSPLIT = 3, 3
TILES = []
for _u in UNITS:
    if _u.startswith('gate'):
        TILES += [(_u, 0), ('br' + _u[4:], 0), (_u, 1), ('br' + _u[4:], 1)]
    elif not _u.startswith('br'):
        TILES += [(_u, 0), (_u, 1)]
TIDX = {t: i for i, t in enumerate(TILES)}
UP_K = 6
KPAGES, VPAGES = 6, 4
NPAGES = DB * NPG
LEVELS = (1, 2, 4, 8, 16, 32, 64)
PAR0 = dict(f0=0, f1=FT * 2, mix=FT * 4, ffn=FT * 4 + 8, dnn=FT * 4 + 16, retn=FT * 4 + 17)
PAR0_N = FT * 4 + 21
PAR1 = dict(f2=0, dc=FT * 2, fin=FT * 2 + 48)
PAR1_N = FT * 2 + 56


def flat(ap):
    return ap.rearrange("p a b -> p (a b)")


class Program:

    def __init__(self, nc, io, consts, onehots, scratch_x, scratch_b, known):
        self.nc, self.io, self.known, self.learn = nc, io, known, Known()
        self.scratch_x, self.scratch_b = scratch_x, scratch_b
        self.consts, self.onehots = consts, onehots
        self.ctx = ExitStack()
        self.sems = []

    def sb(self, name, shape, dt=F32, ctx=None):
        return (ctx or self.ctx).enter_context(self.nc.sbuf_tensor(name, shape, dt))

    def sem(self, name):
        s = self.ctx.enter_context(self.nc.semaphore(name))
        self.sems.append(s)
        return s

    def counter(self, name):
        s = Counter(self.sem(name), self.known.table(name))
        self.learn.made[name] = s
        return s

    def bank(self, name, ap):
        s = Bank(ap, self.sem(name + "_filled"), self.sem(name + "_drained"), self.known.table(name))
        self.learn.made[name] = s
        return s

    def eps(self):
        return self.const('eps')

    def clear_semaphores(self):
        self.nc.all_engine_barrier()
        for s in self.sems:
            self.nc.sync.sem_clear(s)
        self.nc.all_engine_barrier()


def allocate(g, layout):
    sb, c = g.sb, g.ctx
    g.C = sb("consts", [P, layout['_n']])
    g.const = lambda n, p=P: g.C[0:p, layout[n][0]:layout[n][0] + layout[n][1]]
    g.PJ = [g.bank(f"big{i}", c.enter_context(g.nc.psum_tensor(f"big{i}", [P, 2, 512], F32))) for i in range(2)]
    g.X = [g.bank(f"aux{i}", c.enter_context(g.nc.psum_tensor(f"aux{i}", [P, 512], F32))) for i in range(4)]
    g.bias_near = sb("bias_near", [P, H, 2 * P])
    g.bias_s = sb("bias_s", [P, P + NS])
    g.uhi, g.ulo = sb("uhi", [P, KD, NT], F32R), sb("ulo", [P, KD, NT], F32R)
    g.w_raw = [sb(f"w_raw{i}", [P, 2048]) for i in range(NRAW)]
    g.w_hi = [sb(f"w_hi{i}", [P, KD * P], F32R) for i in range(NSPLIT)]
    g.w_lo = [sb(f"w_lo{i}", [P, KD * P], F32R) for i in range(NSPLIT)]
    g.par = sb("par", [P, PAR0_N + PAR1_N])
    g.dn_prev, g.dn_last = sb("dn_prev", [P, 12, DB * 3]), sb("dn_last", [P, 12, 3 + DB * 3])
    g.ffn_prev, g.ffn_last = sb("ffn_prev", [P, 2 * FT, DB * 2]), sb("ffn_last", [P, 2 * FT, 2 + DB * 2])
    g.small = sb("small", [P, 5, 12])
    g.lrow = sb("lrow", [P, 2, H])
    g.gate = sb("gate", [P, 8, 5, H])
    g.stat = sb("stat", [P, 64])
    g.mx = sb("mx", [P, 8])
    g.ptab = sb("ptab", [1, DB * NPG], I32)
    with ExitStack() as r:
        g.xload = sb("xload", [P, KD, NT], ctx=r)
        g.xsq = [sb(f"xsq{i}", [P, NT], ctx=r) for i in range(2)]
        g.par_rows = [sb(f"par_rows{i}", [P, P], ctx=r) for i in range(2)]
        g.dn_rows = sb("dn_rows", [DB * 3, 1536], ctx=r)
        g.ffn_rows = sb("ffn_rows", [DB * 2, 2 * DFF], ctx=r)
        g.rstd0 = sb("rstd0", [P, NT], ctx=r)
        g.ytok = [sb(f"ytok{i}", [P, D], ctx=r) for i in range(2)]
    with ExitStack() as r:
        g.oh_sb = sb("oh_sb", [NBUCKET, 384 + 4 * 160 + 4 * P], ctx=r)
        g.rb = sb("rb", [NBUCKET, 3, H], ctx=r)
        g.rbrow = sb("rbrow", [NBUCKET, 4, P], ctx=r)
        g.brow = sb("brow", [P, H, 383], ctx=r)
        g.xtok = sb("xtok", [P, 5, D], ctx=r)
        g.xset = sb("xset", [P, KD, NT], ctx=r)
    outs = c.enter_context(ExitStack())
    g.out_dn, g.out_ret, g.out_att = (sb(n, [P, H, NT], ctx=outs) for n in ("out_dn", "out_ret", "out_att"))
    att = c.enter_context(ExitStack())
    g.s_pT = sb("s_pT", [P, NPG + 1, P], ctx=att)
    g.sel_s = flat(g.s_pT[0:NS, :, :])[:, 0:NEWK]
    g.s_ak = sb("s_ak", [P, H, NS], ctx=att)
    g.s_v = sb("s_v", [NS, 512], ctx=att)
    sel = c.enter_context(ExitStack())
    g.sel = sb("sel", [P, 128 + 256 + 384 + 512], ctx=sel)
    g.selat = [0, 128, 384, 768]
    with ExitStack() as r:
        g.iq, g.ik = sb("iq", [P, 2, NT], ctx=r), sb("ik", [P, NT], ctx=r)
        g.iqs = sb("iqs", [64, H, NS], ctx=r)
        g.kidx = [sb(f"kidx{i}", [P, NPG, 64], ctx=r) for i in range(2)]
        g.kidxT = sb("kidxT", [64, PAST], ctx=r)
        g.wrow = sb("wrow", [P, DB, H * DS], ctx=r)
        g.relu_p = [sb(f"relu_p{i}", [P, 512], ctx=r) for i in range(2)]
        g.sprod = sb("sprod", [P, NPG, H * DS], ctx=r)
        g.scoreT = sb("scoreT", [P, NPG, NS], ctx=r)
        g.relu_s = sb("relu_s", [NS, H * NS], ctx=r)
        g.kidx_tok = sb("kidx_tok", [P, 5, 64], ctx=r)
    with ExitStack() as r:
        g.rqk = sb("rqk", [P, 8, NT], ctx=r)
        g.rv = sb("rv", [P, H, NT], ctx=r)
        g.rraw = sb("rraw", [P, NT], ctx=r)
        g.rswap = sb("rswap", [P, NT], ctx=r)
        g.r_kd, g.r_v, g.r_qk, g.r_qd, g.r_S = (sb(f"r_{n}", [P, 512], ctx=r) for n in ("kd", "v", "qk", "qd", "S"))
        g.r_sin = [sb(f"r_sin{i}", [P, 512], ctx=r) for i in range(2)]
        g.r_sout = sb("r_sout", [P, 512], ctx=r)
        g.r_kdm = sb("r_kdm", [NS, 512], ctx=r)
    with ExitStack() as r:
        g.akv = sb("akv", [P, 8, NT], ctx=r)
        g.vtok = sb("vtok", [P, 5, 512], ctx=r)
        g.ktok = [sb(f"ktok{i}", [P, 512], ctx=r) for i in range(2)]
        g.logit = [sb(f"logit{i}", [P, 512], ctx=r) for i in range(2)]
        g.prob = [sb(f"prob{i}", [P, 512], ctx=r) for i in range(2)]
        g.probT = [sb(f"probT{i}", [P, 512], ctx=r) for i in range(2)]
    sel.close()
    with ExitStack() as r:
        g.qkv = sb("qkv", [P, 12, NT], ctx=r)
        g.d_pad = [sb(f"d_pad{i}", [P, DW], ctx=r) for i in range(2)]
        g.d_conv = [sb(f"d_conv{i}", [P, DW], ctx=r) for i in range(2)]
        with ExitStack() as r2:
            g.kpage = [sb(f"kpage{i}", [P, 512], ctx=r2) for i in range(KPAGES)]
            g.kT = [sb(f"kT{i}", [P, 512], ctx=r2) for i in range(2)]
            g.s_lT = sb("s_lT", [P, NPG, H, DB, DS], ctx=r2)
            g.s_log = sb("s_log", [P, NEWK], ctx=r2)
        g.d_dec, g.d_eg, g.d_mt, g.d_lm, g.d_t, g.d_tt, g.d_y, g.d_kd, g.d_vb, g.d_kb, g.d_S = (
            sb("d_" + n, [P, 512], ctx=r) for n in ("dec", "eg", "mt", "lm", "t", "tt", "y", "kd", "vb", "kb", "S"))
    att.close()
    g.vpage = [t[:, 0:512] for t in (*g.d_conv, *g.d_pad)]
    g.d_kc, g.d_qd, g.d_w = g.d_mt, g.d_y, g.d_lm
    g.d_sq, g.d_rs = g.d_pad[0][:, 0:NT], g.d_pad[1][:, 0:NT]
    g.d_sin = [g.d_pad[0][:, 0:512], g.d_pad[1][:, 0:512]]
    g.d_sout, g.d_kdm = g.d_conv[0][:, 0:512], g.d_conv[1][0:NS, 0:512]
    with ExitStack() as r:
        g.bhi = [sb(f"bhi{i}", [P, H, NT], F32R, ctx=r) for i in range(2)]
        g.blo = [sb(f"blo{i}", [P, H, NT], F32R, ctx=r) for i in range(2)]
        g.m = sb("m", [P, KD, NT], ctx=r)
        g.sig = [sb(f"sig{i}", [P, NT], ctx=r) for i in range(2)]
    outs.close()
    g.x = sb("x", [P, KD, NT])
    g.hhi, g.hlo = (sb(n, [P, FH, NT], F32R) for n in ("hhi", "hlo"))
    g.f_pad = [sb(f"f_pad{i}", [P, SW]) for i in range(2)]
    g.f_conv = [sb(f"f_conv{i}", [P, SW]) for i in range(2)]
    g.f_act = sb("f_act", [P, NT])
    g.f_sq, g.f_rs = g.f_pad[0][:, 0:NT], g.f_pad[1][:, 0:NT]


def setup(g, oh_at):
    nc, io = g.nc, g.io
    const, ident = g.const, g.const('ident')
    in_ready, steps_a, steps_v = (g.counter(n) for n in ("set_in", "set_act", "set_vec"))
    x_in, wr = g.counter("set_x"), g.counter("set_wr")
    oh = lambda n: g.oh_sb[:, oh_at[n][0]:oh_at[n][0] + oh_at[n][1]]
    with nc.Block() as block:
        @block.sync
        def _(sp):
            sp.dma_start(g.C[:, :], g.consts).then_inc(in_ready.sem, in_ready.next(by=16))
            sp.dma_start(g.oh_sb[:, :], g.onehots).then_inc(in_ready.sem, in_ready.next(by=16))
            sp.dma_start(g.rb[:, 0, :], io['rel_bias']).then_inc(in_ready.sem, in_ready.next(by=16))
            sp.dma_start(g.rb[:, 1, :], io['rel_bias'][31:32, :].to_broadcast([NBUCKET, H])).then_inc(
                    in_ready.sem, in_ready.next(by=16))
            sp.dma_start(g.ptab[:, :], io['page_table'].rearrange("b n -> (b n)").unsqueeze(0)).then_inc(
                    in_ready.sem, in_ready.next('all', 16))
            sp.dma_start(g.xtok[:, 0:4, :], io['x_prompt'].rearrange("a (c p) n -> p (a c) n", p=P)).then_inc(
                    x_in.sem, x_in.next(by=16))
            sp.dma_start(g.xtok[0:NS, 4, :], io['x_sample'].rearrange("b t n -> (b t) n")).then_inc(
                    x_in.sem, x_in.next('all', 16))
            sp.wait_ge(steps_a.sem, steps_a.at('brow'))
            sp.dma_start(g.scratch_b[0:P * H * 383].rearrange("(h p n) -> p h n", h=H, p=P), g.brow[:, :, :]).then_inc(
                    wr.sem, wr.next('brow', 16))
            sp.wait_ge(wr.sem, wr.at('brow'))
            for h in range(H):
                src = bass.AP(g.scratch_b.tensor, h * P * 383 + 127, [[382, P], [1, 2 * P]])
                sp.dma_start(g.bias_near[:, h, :], src).then_inc(wr.sem, wr.next(by=16))
            sp.wait_ge(steps_a.sem, steps_a.at('xset'))
            sp.dma_start(g.scratch_x, flat(g.xset[:, :, :])).then_inc(wr.sem, wr.next('end', 16))
            sp.wait_ge(wr.sem, wr.at('end'))

        @block.vector
        def _(ve):
            ve.wait_ge(in_ready.sem, in_ready.at('all'))
            ve.tensor_tensor(g.rb[:, 2, :], g.rb[:, 0, :], g.rb[:, 1, :], ALU.subtract).then_inc(
                    steps_v.sem, steps_v.next())
            ve.wait_ge(steps_v.sem, steps_v.count)
            ve.tensor_copy(g.rbrow[:, :, :], g.rb[:, 2, :].unsqueeze(2).to_broadcast([NBUCKET, H, P])).then_inc(
                    steps_v.sem, steps_v.next('rb'))
            ve.wait_ge(steps_v.sem, steps_v.count)
            ve.wait_ge(g.X[3].filled, g.X[3].at(('brow', 3)))
            rows = [oh(f'row{t}') for t in range(DS)]
            for t in range(DS):
                ve.tensor_tensor(g.rbrow[:, t, :].rearrange("p (h n) -> p h n", h=H),
                                      g.rb[:, 2, :].unsqueeze(2).to_broadcast([NBUCKET, H, NS]),
                                      rows[t].rearrange("p (h n) -> p h n", h=H), ALU.mult).then_inc(
                        steps_v.sem, steps_v.next(('row', t)))
                ve.wait_ge(steps_v.sem, steps_v.count)

        @block.tensor
        def _(pe):
            pe.wait_ge(steps_v.sem, steps_v.at('rb'))
            for h in range(H):
                pe.wait_ge(g.X[h].drained, g.X[h].claim(('brow', h)))
                x = g.X[h].ap
                mm = pe.matmul(x[:, 0:383], g.rbrow[:, h, :], oh('oh')[:, 0:383], start=True, stop=True)
                mm.then_inc(g.X[h].filled, 1)
            pe.wait_ge(g.X[0].drained, g.X[0].claim('bias_s'))
            x = g.X[0].ap
            for t in range(DS):
                pe.wait_ge(steps_v.sem, steps_v.at(('row', t)))
                mm = pe.matmul(x[:, 0:160], g.rbrow[:, t, :], oh(f'oh{t}'), start=(t == 0), stop=(t == DS - 1))
            mm.then_inc(g.X[0].filled, 1)
            pe.wait_ge(x_in.sem, x_in.at('all'))
            for c in range(5):
                n = P if c < 4 else NS
                for half in range(2):
                    b = g.X[2 + half]
                    pe.wait_ge(b.drained, b.claim(('x', c, half)))
                    x = b.ap
                    for k in range(4):
                        mm = pe.transpose(x[:, k * P:k * P + n], g.xtok[0:n, c, (half * 4 + k) * P:(half * 4 + k + 1) * P],
                                          ident[0:n, 0:n])
                    mm.then_inc(b.filled, 1)

        @block.scalar
        def _(ac):
            for h in range(H):
                ac.wait_ge(g.X[h].filled, g.X[h].at(('brow', h)))
                x = g.X[h].ap
                ac.activation(g.brow[:, h, :], x[:, 0:383], ACT.Copy).then_inc(g.X[h].drained, 1)
                ac.wait_ge(g.X[h].drained, g.X[h].at(('brow', h)))
            ac.activation(g.stat[:, 0:1], g.eps(), ACT.Copy).then_inc(steps_a.sem, steps_a.next('brow'))
            ac.wait_ge(steps_a.sem, steps_a.count)
            ac.wait_ge(g.X[0].filled, g.X[0].at('bias_s'))
            x = g.X[0].ap
            ac.activation(g.bias_s[:, :], x[:, 0:160], ACT.Copy).then_inc(g.X[0].drained, 1)
            ac.wait_ge(g.X[0].drained, g.X[0].at('bias_s'))
            for c in range(5):
                n = P if c < 4 else NS
                for half in range(2):
                    b = g.X[2 + half]
                    ac.wait_ge(b.filled, b.at(('x', c, half)))
                    x = b.ap
                    ac.activation(g.xset[:, half * 4:half * 4 + 4, c * P:c * P + n],
                                          x[:, :].rearrange("p (k n) -> p k n", k=4)[:, :, 0:n], ACT.Copy).then_inc(
                            b.drained, 1)
                    ac.wait_ge(b.drained, b.at(('x', c, half)))
            ac.activation(g.stat[:, 1:2], g.eps(), ACT.Copy).then_inc(steps_a.sem, steps_a.next('xset'))
            ac.wait_ge(steps_a.sem, steps_a.count)


def halves(ap):
    return ap.rearrange("p (a b) -> p a b", a=2)


def head_view(ap, n):
    return ap[:, 0:H * n].rearrange("p (h n) -> p h n", h=H)


def chunk_of(c):
    return (slice(c * P, c * P + P), P) if c < 4 else (slice(SEQ, NT), NS)


def layer_program(g, layer):
    nc, io, const = g.nc, g.io, g.const
    ident, ones = const('ident'), const('ones')
    S = lambda n: g.counter(n)
    w_in_raw = [S(f"w_loaded{i}") for i in range(NRAW)]
    w_hi, w_lo = S("w_hi_made"), S("w_lo_made")
    x_in, rows_in, state_in = S("x_loaded"), S("rows_loaded"), S("conv_states_loaded")
    kidx_in = [S(f"kidx_loaded{i}") for i in range(2)]
    rs_in = [S(f"ret_state_loaded{i}") for i in range(2)]
    ds_in = [S(f"dn_state_loaded{i}") for i in range(2)]
    k_in = [S(f"k_page_loaded{i}") for i in range(KPAGES)]
    v_in = [S(f"v_page_loaded{i}") for i in range(VPAGES)]
    act_steps, vec_steps, pool_steps = S("act_steps"), S("vec_steps"), S("pool_steps")
    act_out, vec_out, pe_out, pool_out = S("act_made"), S("vec_made"), S("pe_made"), S("pool_made")
    st_idx, st_kv, st_k = S("kidx_stored"), S("v_stored"), [S(f"ktok_stored{i}") for i in range(2)]
    st_state, st_ss, st_dn = S("state_stored"), [S(f"sample_state_stored{i}") for i in range(2)], S("dn_rows_stored")
    st_ffn = [S(f"ffn_rows_stored{i}") for i in range(4)]
    PJ, X = g.PJ, g.X
    at_layer = lambda name: io[name][bass.ds(layer, 1)]

    def last_use(t):
        u, i = t
        if u.startswith('down') and i == 0:
            return pe_out.sem, pe_out.at(('used', u))
        bank, key = PJ[1], None
        if u == 'ik':
            bank, key = (PJ[0], 'ik') if i == 0 else (X[1], 'small')
        elif u.startswith('gate'):
            bank, key = PJ[0], ('gate', int(u[4]), int(u[5]), i)
        elif u.startswith('br'):
            key = ('br', int(u[2]), int(u[3]), i)
        elif u.startswith('up'):
            bank, key = PJ[i], ('up', *map(int, u[2:].split('_')), i)
        elif u.startswith('down'):
            f, c = map(int, u[4:].split('_'))
            bank, key = PJ[c % 2], ('down', f, c)
        elif u == 'iq':
            bank, key = PJ[i], f'iq{i}'
        else:
            bank, key = PJ[i], (u[:-1], 2 * int(u[-1]) + i)
        return bank.filled, bank.at(key)
    raw, hi, lo = g.w_raw, g.w_hi, g.w_lo
    gC, gG, gBeta, gEK, gBE, gTmp, gA, gB = (g.gate[:, i] for i in range(8))

    def unit_pieces(u):
        t = raw[UIDX[u] % NRAW]
        win = at_layer('w_in').rearrange("a (k p) n -> p (a k) n", p=P)

        def cols(src, w, n_k=KD, at=0, width=256):
            return (t[:, 0:n_k * width].rearrange("p (k n) -> p k n", k=n_k)[:, :, at:at + w], src)
        if u == 'ik':
            ik = win[:, :, COL['ik']:COL['ik'] + 64]
            return [cols(ik, 64), cols(ik, 64, at=64), cols(win[:, :, COL['b']:COL['b'] + 8], 8, at=128),
                    cols(win[:, :, COL['iw']:COL['iw'] + 4], 4, at=136)]
        if u == 'iq':
            return [cols(win[:, :, COL['iq']:COL['iq'] + 256], 256)]
        if u.startswith('gate'):
            c = COL['gate'] + int(u[4]) * D + int(u[5]) * 256
            return [cols(win[:, :, c:c + 256], 256)]
        if u.startswith('br'):
            n, d = int(u[2]), int(u[3])
            src = at_layer('w_branch').rearrange("a n (k p) m -> p (a n k) m", p=P)
            return [cols(src[:, n * H:n * H + H, d * 256:d * 256 + 256], 256, n_k=H)]
        if u.startswith('wo'):
            c = int(u[2]) * 256
            return [cols(at_layer('w_o').rearrange("a (k p) m -> p (a k) m", p=P)[:, :, c:c + 256], 256)]
        if u.startswith('up'):
            f, j = map(int, u[2:].split('_'))
            c = (f * FH + j) * P
            src = at_layer('w_up').rearrange("a (k p) m -> p (a k) m", p=P)
            return [cols(src[:, :, c:c + P], P), cols(src[:, :, DFF + c:DFF + c + P], P, at=P)]
        if u.startswith('down'):
            f, c = map(int, u[4:].split('_'))
            src = at_layer('w_down').rearrange("a (k p) m -> p (a k) m", p=P)
            return [cols(src[:, f * FH:f * FH + FH, c * P:c * P + P], P, n_k=FH, width=P)]
        name, i = (u[:-1], int(u[-1]))
        return [cols(win[:, :, COL[name] + i * 256:COL[name] + i * 256 + 256], 256)]

    def unit_size(u):
        return 1024 if u.startswith('br') else FH * P if u.startswith('down') else 2048

    def tile_of(t):
        u, i = t
        x = raw[UIDX[u] % NRAW]
        if u.startswith('down'):
            return x[:, 0:FH * P].rearrange("p (k n) -> p k n", n=P)[:, UP_K:FH] if i \
                else x[:, 0:UP_K * P].rearrange("p (k n) -> p k n", n=P)
        x = x[:, 0:unit_size(u)].rearrange("p (k n) -> p k n", n=256)
        return x[:, :, P:P + 12] if t == ('ik', 1) else x[:, :, i * P:i * P + P]

    def split_view(bufs, t):
        n_k, n = tile_of(t).shape[1:]
        return bufs[TIDX[t] % NSPLIT][:, 0:n_k * n].rearrange("p (k n) -> p k n", n=n)

    def load_unit(q, i):
        if i >= len(UNITS):
            return
        u = UNITS[i]
        if i >= NRAW:
            q.wait_ge(w_lo.sem, w_lo.at((UNITS[i - NRAW], 1)))
        loaded = w_in_raw[i % NRAW]
        pieces = unit_pieces(u)
        for n, (dst, src) in enumerate(pieces):
            q.dma_start(dst, src).then_inc(loaded.sem, loaded.next(u if n == len(pieces) - 1 else None, 16))

    @g.block.sync
    def _(sp):
        sp.dma_start(flat(g.xload[:, :, :]), g.scratch_x).then_inc(x_in.sem, x_in.next('start', 16))
        r0, r1 = g.par_rows
        fw = at_layer('ffn_conv_w').rearrange("a i (t p) -> (a i t) p", p=P)
        for i in range(NRAW):
            load_unit(sp, i)
        for t, base, n, src in (
                (r0, PAR0['f0'], 4 * FT, fw[0:4 * FT]), (r1, PAR1['f2'], 2 * FT, fw[4 * FT:6 * FT]),
                (r0, PAR0['mix'], 8, at_layer('norm_mix').rearrange("a (k p) -> (a k) p", p=P)),
                (r0, PAR0['ffn'], 8, at_layer('norm_ffn').rearrange("a (k p) -> (a k) p", p=P)),
                (r0, PAR0['dnn'], 1, at_layer('dn_norm')),
                (r0, PAR0['retn'], 4, at_layer('ret_norm').rearrange("a h p -> (a h) p")),
                (r1, PAR1['dc'], 48, at_layer('dn_conv_w').rearrange("a i (t p) -> (a i t) p", p=P)),
                (r1, PAR1['fin'], 8, io['norm_final'].rearrange("(k p) -> k p", p=P))):
            sp.dma_start(t[base:base + n, :], src).then_inc(rows_in.sem, rows_in.next(by=16))
        sp.dma_start(g.lrow[:, 0, :], at_layer('dn_a_log').to_broadcast([P, H])).then_inc(
                rows_in.sem, rows_in.next(by=16))
        sp.dma_start(g.lrow[:, 1, :], at_layer('dn_dt_bias').to_broadcast([P, H])).then_inc(
                rows_in.sem, rows_in.next('all', 16))
        sp.dma_start(g.dn_rows[:, :], at_layer('state_dn_conv').rearrange("a b i n -> (a b i) n")).then_inc(
                state_in.sem, state_in.next(by=16))
        sp.dma_start(g.ffn_rows[:, :], at_layer('state_ffn_conv').rearrange("a b i n -> (a b i) n")).then_inc(
                state_in.sem, state_in.next('all', 16))
        n_phys = io['cache_k'].shape[1]
        pools = {n: io[n].rearrange("l n p h d -> (l n) p (h d)") for n in ('cache_k', 'cache_v')}
        pools['cache_kidx'] = io['cache_kidx'].rearrange("l n p d -> (l n) p d")

        def page(pool, b, pg):
            e = b * NPG + pg
            phys = sp.value_load(g.ptab[0:1, e:e + 1], min_val=0, max_val=n_phys - 1)
            return pools[pool][bass.ds(phys + layer * n_phys, 1)].rearrange("a p n -> (a p) n")
        for b in range(DB):
            if b >= 2:
                sp.wait_ge(X[1].filled, X[1].at(('kidxT', b - 2)))
            elif b == 0:
                sp.wait_ge(act_out.sem, act_out.at('states'))
                sp.wait_ge(vec_out.sem, vec_out.at(('u', KD - 1)))
            for pg in range(NPG):
                sp.dma_start(g.kidx[b % 2][:, pg, :], page('cache_kidx', b, pg)).then_inc(
                        kidx_in[b % 2].sem, kidx_in[b % 2].next(b if pg == NPG - 1 else None, 16))
        for b in range(DB):
            if b >= 2:
                sp.wait_ge(vec_out.sem, vec_out.at(('rs', b - 2)))
            elif b == 0:
                sp.wait_ge(vec_out.sem, vec_out.at(('rk', 3)))
            sp.dma_start(head_view(g.r_sin[b % 2], P), at_layer('state_ret').rearrange(
                "a b h k v -> k (a b) h v")[:, b]).then_inc(rs_in[b % 2].sem, rs_in[b % 2].next(b, 16))
        sp.wait_ge(PJ[1].drained, PJ[1].at(('ao', 3)))
        sp.wait_ge(st_kv.sem, st_kv.at('v'))
        sp.wait_ge(st_k[0].sem, st_k[0].at(4))
        sp.wait_ge(st_k[1].sem, st_k[1].at(3))
        for i in range(NPAGES):
            if i >= KPAGES:
                m = i - KPAGES
                sp.wait_ge(X[m % 2].filled, X[m % 2].at(('sk', m)))
            sp.dma_start(g.kpage[i % KPAGES][:, :], page('cache_k', *divmod(i, NPG))).then_inc(
                k_in[i % KPAGES].sem, k_in[i % KPAGES].next(i, 16))
        sp.wait_ge(act_out.sem, act_out.at(('silu', 11)))
        for i in range(NPAGES):
            if i == 2:
                sp.wait_ge(vec_out.sem, vec_out.at(('l2', 7)))
            if i >= VPAGES:
                sp.wait_ge(pe_out.sem, pe_out.at(('v', i - VPAGES)))
            sp.dma_start(g.vpage[i % VPAGES], page('cache_v', *divmod(i, NPG))).then_inc(
                v_in[i % VPAGES].sem, v_in[i % VPAGES].next(i, 16))
        for ps in range(2):
            for b in range(DB):
                n = ps * DB + b
                if n >= 2:
                    user = pe_out if n < DB + 2 else vec_out
                    sp.wait_ge(user.sem, user.at(('ds', n - 2)))
                else:
                    sp.wait_ge(PJ[0].filled, PJ[0].at('so'))
                sp.dma_start(head_view(g.d_sin[n % 2], P), at_layer('state_dn').rearrange(
                    "a b h k v -> k (a b) h v")[:, b]).then_inc(ds_in[n % 2].sem, ds_in[n % 2].next(n, 16))
        sp.wait_ge(act_out.sem, act_out.at(('bsplit', 2)))
        sp.wait_ge(vec_out.sem, vec_out.at(('bsplit', 2)))
        sp.dma_start(flat(g.x[:, :, :]), g.scratch_x).then_inc(x_in.sem, x_in.next('again', 16))
        sp.wait_ge(vec_out.sem, vec_out.at('x_final'))
        sp.dma_start(g.scratch_x, flat(g.x[:, :, :])).then_inc(x_in.sem, x_in.next('stored', 16))
        sp.wait_ge(x_in.sem, x_in.at('stored'))

    @g.block.gpsimd
    def _(po):

        for t in TILES:
            po.wait_ge(w_hi.sem, w_hi.at(t))
            po.tensor_tensor(split_view(lo, t), tile_of(t), split_view(hi, t).bitcast(F32), ALU.subtract).then_inc(
                w_lo.sem, w_lo.next(t))

    @g.block.tensor
    def _(pe):
        def mm3(out, wh, wl, xh, xl, start, stop):
            pe.matmul(out, wh, xh, start=start, stop=False)
            pe.matmul(out, wh, xl, start=False, stop=False)
            return pe.matmul(out, wl, xh, start=False, stop=stop)

        def dense_tile(key, slot, u, i, ah, al, ready=None, between=None):
            pe.wait_ge(w_lo.sem, w_lo.at((u, i)))
            wh, wl = split_view(hi, (u, i)), split_view(lo, (u, i))
            n_k = wh.shape[1]
            pe.wait_ge(PJ[slot].drained, PJ[slot].claim(key))
            out = PJ[slot].ap
            for half in range(2):
                if half == 1 and between is not None:
                    between()
                for k in range(n_k):
                    if half == 0 and ready is not None:
                        ready(k)
                    cs = slice(half * HT, half * HT + HT)
                    mm = mm3(out[:, half, 0:HT], wh[:, k, :], wl[:, k, :], ah[:, k, cs], al[:, k, cs],
                             k == 0, k == n_k - 1)
            mm.then_inc(PJ[slot].filled, 1)

        def column_sums(key, slot, sources):
            pe.wait_ge(PJ[slot].drained, PJ[slot].claim(key))
            out = PJ[slot].ap
            n = len(sources)
            for k, (wait, ap) in enumerate(sources):
                wait()
                for half in range(2):
                    mm = pe.matmul(out[:, half, 0:HT], ones, ap[:, half * HT:half * HT + HT],
                                   start=(k == 0), stop=(k == n - 1))
                if k < n - 1:
                    mm.then_inc(pe_out.sem, pe_out.next((key, k)))
            mm.then_inc(PJ[slot].filled, 1)

        def turn(bank, key, n, m, srcs, pitch):
            pe.wait_ge(bank.drained, bank.claim(key))
            x = bank.ap
            for i, s in enumerate(srcs):
                mm = pe.transpose(x[0:m, i * pitch:i * pitch + n], s, ident[0:n, 0:n])
            mm.then_inc(bank.filled, 1)

        pe.wait_ge(rows_in.sem, rows_in.at('all'))
        turn(X[0], 'par0', PAR0_N, P, [g.par_rows[0][0:PAR0_N, :]], PAR0_N)
        turn(X[1], 'par1', PAR1_N, P, [g.par_rows[1][0:PAR1_N, :]], PAR1_N)
        column_sums('rms0', 0, [((lambda k=k: pe.wait_ge(act_out.sem, act_out.at(('sq', k)))), g.xsq[k % 2]) for k in range(KD)])
        pe.wait_ge(state_in.sem, state_in.at('all'))
        turn(X[2], 'dn_prev', 24, P, [g.dn_rows[:, t * P:t * P + P] for t in range(12)], 24)
        turn(X[3], 'ffn_prev0', 16, P, [g.ffn_rows[:, t * P:t * P + P] for t in range(FT)], 16)
        turn(X[0], 'ffn_prev1', 16, P, [g.ffn_rows[:, t * P:t * P + P] for t in range(FT, 2 * FT)], 16)

        def dense_unit(u, keys, first_ready=None):
            for i, key in enumerate(keys):
                dense_tile(key, i, u, i, g.uhi, g.ulo, first_ready if i == 0 else None)

        def u_ready(k):
            pe.wait_ge(vec_out.sem, vec_out.at(('u', k)))
        dense_unit('iq', ['iq0', 'iq1'], u_ready)
        dense_tile('ik', 0, 'ik', 0, g.uhi, g.ulo)
        pe.wait_ge(w_lo.sem, w_lo.at(('ik', 1)))
        wh, wl = split_view(hi, ('ik', 1)), split_view(lo, ('ik', 1))
        pe.wait_ge(X[1].drained, X[1].claim('small'))
        x = X[1].ap
        for c in range(5):
            cs, n = chunk_of(c)
            for k in range(KD):
                a, b = g.uhi[:, k, cs], g.ulo[:, k, cs]
                w1, w2 = wh[:, k, :], wl[:, k, :]
                if c == 4:
                    a, b, w1, w2 = (t.bitcast(F32) for t in (a, b, w1, w2))
                mm = mm3(x[0:n, c * 12:c * 12 + 12], a, b, w1, w2, k == 0, k == KD - 1)
        mm.then_inc(X[1].filled, 1)
        pe.wait_ge(PJ[0].drained, PJ[0].at('ik'))
        pe.wait_ge(X[0].drained, X[0].claim('kidx_tok'))
        x = X[0].ap
        for c in range(5):
            cs, n = chunk_of(c)
            mm = pe.transpose(x[0:n, c * 64:c * 64 + 64], g.ik[0:64, cs], ident[0:64, 0:64])
        mm.then_inc(X[0].filled, 1)
        i = 0
        for qb in range(1, 4):
            n = (qb + 1) * P
            for h in range(H):
                b0 = 64 * (h % 2)
                bank = X[2 + i % 2]
                pe.wait_ge(bank.drained, bank.claim(('is', qb, h)))
                x = bank.ap
                mm = pe.matmul(x[:, 0:n], g.iq[b0:b0 + 64, h // 2, qb * P:qb * P + P], g.ik[b0:b0 + 64, 0:n],
                               start=True, stop=True)
                mm.then_inc(bank.filled, 1)
                i += 1
        pe.wait_ge(X[1].drained, X[1].at('small'))
        pe.wait_ge(X[2].drained, X[2].claim('wrow'))
        x = X[2].ap
        for h in range(H):
            mm = pe.matmul(x[:, h * NS:h * NS + NS], g.small[0:NS, 4, 8 + h:9 + h].to_broadcast([NS, P]),
                           ident[0:NS, 0:NS], start=True, stop=True)
        mm.then_inc(X[2].filled, 1)
        pe.wait_ge(act_out.sem, act_out.at('iqs'))
        for b in range(DB):
            pe.wait_ge(kidx_in[b % 2].sem, kidx_in[b % 2].at(b))
            for q in range(2):
                turn(X[q], ('kidxT' if q else 'kidxT0', b), P, 64, [g.kidx[b % 2][:, q * 4 + j, :] for j in range(4)], P)
            pe.wait_ge(X[1].drained, X[1].at(('kidxT', b)))
            bank = X[2 + b % 2]
            pe.wait_ge(bank.drained, bank.claim(('sT', b)))
            x = bank.ap
            for pg in range(NPG):
                mm = pe.matmul(x[:, pg * 16:pg * 16 + 16].rearrange("p (h t) -> p h t", h=H),
                               g.kidxT[:, pg * P:pg * P + P], g.iqs[:, :, b * DS:b * DS + DS], start=True, stop=True)
            mm.then_inc(bank.filled, 1)
        pe.wait_ge(X[0].drained, X[0].claim('s_new'))
        x = X[0].ap
        for h in range(H):
            mm = pe.matmul(x[0:NS, h * NS:h * NS + NS], g.iqs[:, h, :], g.ik[0:64, SEQ:NT], start=True, stop=True)
        mm.then_inc(X[0].filled, 1)
        pe.wait_ge(vec_out.sem, vec_out.at('scoreT'))
        for q in range(2):
            turn(X[1 + q], ('s_score', q), P, NS, [g.scoreT[:, q * 4 + j, :] for j in range(4)], P)

        for nm in ('rq', 'rk', 'rv', 'rg'):
            for i in range(2):
                dense_unit(f'{nm}{i}', [(nm, 2 * i), (nm, 2 * i + 1)])
        for c in range(5):
            cs, n = chunk_of(c)
            if c == 0:
                pe.wait_ge(vec_out.sem, vec_out.at(('rk', 3)))
                pe.wait_ge(PJ[1].drained, PJ[1].at(('rv', 3)))
            turn(X[0], ('rkT', c), P, n, [g.rqk[:, 4 + h, cs] for h in range(H)], P)
            turn(X[1], ('rvT', c), P, n, [g.rv[:, h, cs] for h in range(H)], P)
            pe.wait_ge(X[2].drained, X[2].claim(('rqk', c)))
            x = X[2].ap
            for h in range(H):
                mm = pe.matmul(x[0:n, h * n:h * n + n], g.rqk[:, 4 + h, cs], g.rqk[:, h, cs], start=True, stop=True)
            mm.then_inc(X[2].filled, 1)
            pe.wait_ge(vec_out.sem, vec_out.at(('r_in', c)))
            pe.wait_ge(X[1].drained, X[1].at(('rvT', c)))
            pe.wait_ge(X[3].drained, X[3].claim(('ro', c)))
            x = X[3].ap
            kd, v, qk, qd = g.r_kd, g.r_v, g.r_qk, g.r_qd
            if c < 4:
                for h in range(H):
                    hs = slice(h * P, h * P + P)
                    pe.matmul(x[:, hs], g.r_S[:, hs], qd[:, hs], start=True, stop=False)
                    mm = pe.matmul(x[:, hs], v[:, hs], qk[:, hs], start=False, stop=True)
                mm.then_inc(X[3].filled, 1)
                pe.wait_ge(X[0].drained, X[0].claim(('rS', c)))
                x = X[0].ap
                for h in range(H):
                    hs = slice(h * P, h * P + P)
                    mm = pe.matmul(x[:, hs], kd[:, hs], v[:, hs], start=True, stop=True)
                mm.then_inc(X[0].filled, 1)
            else:
                for h in range(H):
                    pe.matmul(x[:, h * n:h * n + n], v[0:n, h * P:h * P + P], qk[0:n, h * n:h * n + n],
                              start=(h == 0), stop=False, skip_group_check=True)
                for b in range(DB):
                    pe.wait_ge(rs_in[b % 2].sem, rs_in[b % 2].at(b))
                    for h in range(H):
                        o = h * n + b * DS
                        mm = pe.matmul(x[:, o:o + DS], g.r_sin[b % 2][:, h * P:h * P + P], qd[:, o:o + DS],
                                       start=False, stop=(b == DB - 1), skip_group_check=True)
                    if b == DB - 1:
                        mm.then_inc(X[3].filled, 1)
                    pe.wait_ge(vec_out.sem, vec_out.at(('kdm', b)))
                    bank = X[b % 2]
                    pe.wait_ge(bank.drained, bank.claim(('rS', c, b)))
                    y = bank.ap
                    for h in range(H):
                        hs = slice(h * P, h * P + P)
                        mm = pe.matmul(y[:, hs], g.r_kdm[:, hs], v[0:n, hs], start=True, stop=True)
                    mm.then_inc(bank.filled, 1)
        pe.wait_ge(X[3].drained, X[3].at(('ro', 4)))
        for h in range(H):
            column_sums(('rmean', h), 0, [((lambda: None), g.rv[:, h, :])])
            column_sums(('rvar', h), 1, [((lambda h=h: pe.wait_ge(act_out.sem, act_out.at(('rsq', h)))), g.rswap)])

        for nm in ('aq', 'ak', 'av'):
            for i in range(2):
                dense_unit(f'{nm}{i}', [(nm, 2 * i), (nm, 2 * i + 1)])
        pe.wait_ge(PJ[1].drained, PJ[1].at(('av', 3)))
        for c in range(5):
            cs, n = chunk_of(c)
            turn(X[0], ('kT', c), P, n, [g.akv[:, h, cs] for h in range(H)], P)
            turn(X[1], ('vT', c), P, n, [g.akv[:, 4 + h, cs] for h in range(H)], P)
        steps = [(qb, h) for qb in range(4) for h in range(H)]
        for i in range(len(steps) + 1):
            if i < len(steps):
                qb, h = steps[i]
                n = (qb + 1) * P
                pe.wait_ge(X[i % 2].drained, X[i % 2].claim(('qk', i)))
                x = X[i % 2].ap
                mm = pe.matmul(x[:, 0:n], g.out_att[:, h, qb * P:qb * P + P], g.akv[:, h, 0:n], start=True, stop=True)
                mm.then_inc(X[i % 2].filled, 1)
            if i:
                j = i - 1
                qb, h = steps[j]
                pe.wait_ge(vec_out.sem, vec_out.at(('prob', j)))
                turn(X[2 + j % 2], ('pT', j), P, P, [g.prob[j % 2][:, t * P:t * P + P] for t in range(qb + 1)], P)
                pe.wait_ge(X[2 + j % 2].drained, X[2 + j % 2].at(('pT', j)))
                if j == 0:
                    pe.wait_ge(X[1].drained, X[1].at(('vT', 4)))
                if h == 0:
                    pe.wait_ge(PJ[qb % 2].drained, PJ[qb % 2].claim(('ao', qb)))
                o = PJ[qb % 2].ap
                for t in range(qb + 1):
                    mm = pe.matmul(o[:, 0, h * P:h * P + P], g.vtok[:, t, h * P:h * P + P],
                                   g.probT[j % 2][:, t * P:t * P + P], start=(t == 0), stop=(t == qb))
                if h == H - 1:
                    mm.then_inc(PJ[qb % 2].filled, 1)

        def turn_keys(i):
            pe.wait_ge(k_in[i % KPAGES].sem, k_in[i % KPAGES].at(i))
            turn(X[i % 2], ('sk', i), P, P, [g.kpage[i % KPAGES][:, h * P:h * P + P] for h in range(H)], P)

        def key_page(i):
            b, pg = divmod(i, NPG)
            if i + 1 < NPAGES:
                turn_keys(i + 1)
            bank = X[2 + b % 2]
            if pg == 0:
                pe.wait_ge(bank.drained, bank.claim(('slT', b)))
            pe.wait_ge(X[i % 2].drained, X[i % 2].at(('sk', i)))
            for h in range(H):
                mm = pe.matmul(bank.ap[:, pg * 16 + h * DS:pg * 16 + h * DS + DS], g.kT[i % 2][:, h * P:h * P + P],
                               g.out_att[:, h, SEQ + b * DS:SEQ + b * DS + DS], start=True, stop=True)
            if pg == NPG - 1:
                mm.then_inc(bank.filled, 1)

        turn_keys(0)
        for t in range(16):
            def keys(at):
                key_page(4 * t + at)
                key_page(4 * t + at + 1)
            u, key = (f'dn{t // 2}', ('dn', t)) if t < 12 else (f'z{t // 2 - 6}', ('z', t - 12))
            dense_tile(key, t % 2, u, t % 2, g.uhi, g.ulo, between=lambda: keys(0))
            keys(2)

        pe.wait_ge(X[0].drained, X[0].claim(('srep', 0)))
        x = X[0].ap
        mm = pe.matmul(x[:, 0:512], const('rep', NS), g.sel_s[:, 0:512], start=True, stop=True)
        mm.then_inc(X[0].filled, 1)
        pe.wait_ge(X[1].drained, X[1].claim(('srep', 1)))
        x = X[1].ap
        mm = pe.matmul(x[:, 0:512], const('rep', NS), g.sel_s[:, 512:1024], start=True, stop=True)
        mm.then_inc(X[1].filled, 1)
        pe.wait_ge(X[0].drained, X[0].claim(('srep', 2)))
        x = X[0].ap
        mm = pe.matmul(x[:, 0:NS], const('rep', NS), g.sel_s[:, 1024:NEWK], start=True, stop=True)
        mm.then_inc(X[0].filled, 1)
        pe.wait_ge(X[2 + (DB - 1) % 2].drained, X[2 + (DB - 1) % 2].at(('slT', DB - 1)))
        for q in range(2):
            turn(X[2 + q], ('slog', q), P, P, [g.s_lT[:, q * 4 + j].rearrange("p h b t -> p (h b t)") for j in range(4)], P)
        pe.wait_ge(X[1].drained, X[1].claim('snew'))
        x = X[1].ap
        for h in range(H):
            mm = pe.matmul(x[h * NS:h * NS + NS, 0:NS], g.out_att[:, h, SEQ:NT], g.s_ak[:, h, :], start=True, stop=True)
        mm.then_inc(X[1].filled, 1)
        for t in range(8):
            column_sums(('l2', t), t % 2, [((lambda t=t: pe.wait_ge(act_out.sem, act_out.at(('l2sq', t)))), g.d_sq)])
        pe.wait_ge(X[3].drained, X[3].claim('gsum'))
        x = X[3].ap
        pe.wait_ge(act_out.sem, act_out.at('conv_done'))
        pe.wait_ge(vec_out.sem, vec_out.at('g'))
        G16 = gG[:, 0:4, :].rearrange("p c h -> p (c h)")
        pe.matmul(x[:, 0:16], const('triu'), G16, start=True, stop=True)
        pe.matmul(x[0:NS, 16:20], const('triu_s', NS)[:, 0:NS], gG[0:NS, 4, :], start=True, stop=True)
        pe.matmul(x[:, 20:36], const('after'), G16, start=True, stop=True)
        mm = pe.matmul(x[0:NS, 36:40], const('after_s', NS)[:, 0:NS], gG[0:NS, 4, :], start=True, stop=True)
        mm.then_inc(X[3].filled, 1)
        pe.wait_ge(vec_out.sem, vec_out.at('s_prob'))
        for q in range(2):
            turn(X[2 + q], ('spT', q), P, P, [g.s_log[:, (q * 4 + j) * P:(q * 4 + j + 1) * P] for j in range(4)], P)
        turn(X[0], 'spT_new', P, NS, [g.s_log[:, PAST:NEWK]], P)
        pe.wait_ge(X[0].drained, X[0].at('spT_new'))
        pe.wait_ge(PJ[0].drained, PJ[0].claim('so'))
        x = PJ[0].ap
        o = x[:, 0, 0:P]
        for h in range(H):
            pe.matmul(o[:, h * NS:h * NS + NS], g.s_v[:, h * P:h * P + P], g.s_pT[0:NS, NPG, h * NS:h * NS + NS],
                      start=(h == 0), stop=False, skip_group_check=True)

        def value_page(i):
            b, pg = divmod(i, NPG)
            pe.wait_ge(v_in[i % VPAGES].sem, v_in[i % VPAGES].at(i))
            for h in range(H):
                c0 = h * NS + b * DS
                mm = pe.matmul(o[:, c0:c0 + DS], g.vpage[i % VPAGES][:, h * P:h * P + P], g.s_pT[:, pg, c0:c0 + DS],
                               start=False, stop=(pg == NPG - 1), skip_group_check=True)
            if i == NPAGES - 1:
                mm.then_inc(PJ[0].filled, 1)
            else:
                mm.then_inc(pe_out.sem, pe_out.next(('v', i)))

        for c in range(5):
            cs, n = chunk_of(c)
            tri = const('triu') if c < 4 else const('triu_s', NS)[:, 0:NS]
            q, k, v = (g.qkv[:, 4 * i:4 * i + 4, cs] for i in range(3))
            for bank, key, src, rhs in ((X[0], 'grow', gG, tri), (X[1], 'betarow', gBeta, ident[0:n, 0:n])):
                pe.wait_ge(bank.drained, bank.claim((key, c)))
                x = bank.ap
                for h in range(H):
                    mm = pe.matmul(x[:, h * n:h * n + n], src[0:n, c, h:h + 1].to_broadcast([n, P]), rhs,
                                   start=True, stop=True)
                mm.then_inc(bank.filled, 1)
            if c == 0:
                pe.wait_ge(vec_out.sem, vec_out.at(('l2', 7)))
            for bank, key, a, b in ((X[2], 'kk', k, k), (X[3], 'kq', k, q)):
                pe.wait_ge(bank.drained, bank.claim((key, c)))
                x = bank.ap
                for h in range(H):
                    mm = pe.matmul(x[0:n, h * n:h * n + n], a[:, h, :], b[:, h, :], start=True, stop=True)
                mm.then_inc(bank.filled, 1)
            turn(X[0], ('dkT', c), P, n, [k[:, h, :] for h in range(H)], P)
            turn(X[1], ('dvT', c), P, n, [v[:, h, :] for h in range(H)], P)
            levels = LEVELS if c < 4 else LEVELS[:2]
            pages = iter(range(c * 16, c * 16 + 16 if c < 4 else 0))
            if c < 4:
                value_page(next(pages))
                value_page(next(pages))
            for s in levels:
                pe.wait_ge(vec_out.sem, vec_out.at(('lm', c, s)))
                pe.wait_ge(X[2].drained, X[2].claim(('Y', c, s)))
                x = X[2].ap
                for h in range(H):
                    hs = slice(h * n, h * n + n)
                    mm = pe.matmul(x[0:n, hs], g.d_lm[0:n, hs], g.d_t[0:n, hs], start=True, stop=True)
                mm.then_inc(X[2].filled, 1)
                if c < 4:
                    value_page(next(pages))
                pe.wait_ge(X[2].drained, X[2].at(('Y', c, s)))
                if s != levels[-1]:
                    pe.wait_ge(X[3].drained, X[3].claim(('TY', c, s)))
                    x = X[3].ap
                    for h in range(H):
                        hs = slice(h * n, h * n + n)
                        mm = pe.matmul(x[0:n, hs], g.d_tt[0:n, hs], g.d_y[0:n, hs], start=True, stop=True)
                    mm.then_inc(X[3].filled, 1)
                pe.wait_ge(X[0].drained, X[0].claim(('YT', c, s)))
                x = X[0].ap
                for h in range(H):
                    hs = slice(h * n, h * n + n)
                    mm = pe.matmul(x[0:n, hs], g.d_y[0:n, hs], g.d_tt[0:n, hs], start=True, stop=True)
                mm.then_inc(X[0].filled, 1)
                if c < 4:
                    value_page(next(pages))
            pe.wait_ge(X[0].drained, X[0].at(('YT', c, levels[-1])))
            pe.wait_ge(X[1].drained, X[1].claim(('kc', c)))
            x = X[1].ap
            for h in range(H):
                mm = pe.matmul(x[:, h * n:h * n + n], g.d_kb[0:n, h * P:h * P + P], g.d_tt[0:n, h * n:h * n + n],
                               start=True, stop=True)
            mm.then_inc(X[1].filled, 1)
            pe.wait_ge(X[1].drained, X[1].at(('kc', c)))
            pe.wait_ge(vec_out.sem, vec_out.at(('qd', c)))
            qk = g.d_dec
            if c < 4:
                pe.wait_ge(X[2].drained, X[2].claim(('dw', c)))
                x = X[2].ap
                for h in range(H):
                    hs = slice(h * P, h * P + P)
                    pe.matmul(x[:, hs], g.d_tt[:, hs], g.d_vb[:, hs], start=True, stop=False)
                    mm = pe.matmul(x[:, hs], g.d_kc[:, hs], g.d_S[:, hs], start=False, stop=True)
                mm.then_inc(X[2].filled, 1)
                pe.wait_ge(X[2].drained, X[2].at(('dw', c)))
                pe.wait_ge(X[3].drained, X[3].claim(('do', c)))
                x = X[3].ap
                for h in range(H):
                    hs = slice(h * P, h * P + P)
                    pe.matmul(x[:, hs], g.d_S[:, hs], g.d_qd[:, hs], start=True, stop=False)
                    mm = pe.matmul(x[:, hs], g.d_w[:, hs], qk[:, hs], start=False, stop=True)
                mm.then_inc(X[3].filled, 1)
                pe.wait_ge(X[0].drained, X[0].claim(('dS', c)))
                x = X[0].ap
                for h in range(H):
                    hs = slice(h * P, h * P + P)
                    mm = pe.matmul(x[:, hs], g.d_kd[:, hs], g.d_w[:, hs], start=True, stop=True)
                mm.then_inc(X[0].filled, 1)
            else:
                pe.wait_ge(X[2].drained, X[2].claim(('dw', c)))
                x = X[2].ap
                for h in range(H):
                    pe.matmul(x[:, h * n:h * n + n], g.d_vb[0:n, h * P:h * P + P], g.d_tt[0:n, h * n:h * n + n],
                              start=(h == 0), stop=False, skip_group_check=True)
                pe.wait_ge(X[3].drained, X[3].claim(('do', c)))
                y = X[3].ap
                for b in range(DB):
                    pe.wait_ge(ds_in[b % 2].sem, ds_in[b % 2].at(b))
                    for h in range(H):
                        o = h * n + b * DS
                        mm = pe.matmul(x[:, o:o + DS], g.d_sin[b % 2][:, h * P:h * P + P], g.d_kc[:, o:o + DS],
                                       start=False, stop=(b == DB - 1), skip_group_check=True)
                    if b == DB - 1:
                        mm.then_inc(X[2].filled, 1)
                    for h in range(H):
                        o = h * n + b * DS
                        mm = pe.matmul(y[:, o:o + DS], g.d_sin[b % 2][:, h * P:h * P + P], g.d_qd[:, o:o + DS],
                                       start=(b == 0 and h == 0), stop=False, skip_group_check=True)
                    mm.then_inc(pe_out.sem, pe_out.next(('ds', b)))
                pe.wait_ge(X[2].drained, X[2].at(('dw', c)))
                turn(X[1], 'dwT', P, n, [g.d_eg[:, 128 + h * n:128 + h * n + n] for h in range(H)], P)
                pe.wait_ge(X[1].drained, X[1].at('dwT'))
                for h in range(H):
                    mm = pe.matmul(y[:, h * n:h * n + n], g.d_w[0:n, h * P:h * P + P], qk[0:n, h * n:h * n + n],
                                   start=False, stop=True, skip_group_check=True)
                mm.then_inc(X[3].filled, 1)
                for b in range(DB):
                    pe.wait_ge(vec_out.sem, vec_out.at(('dkdm', b)))
                    pe.wait_ge(X[b % 2].drained, X[b % 2].claim(('dS', c, b)))
                    x = X[b % 2].ap
                    for h in range(H):
                        hs = slice(h * P, h * P + P)
                        mm = pe.matmul(x[:, hs], g.d_kdm[:, hs], g.d_w[0:n, hs], start=True, stop=True)
                    mm.then_inc(X[b % 2].filled, 1)
        pe.wait_ge(X[3].drained, X[3].at(('do', 4)))
        for h in range(H):
            column_sums(('dvar', h), h % 2, [((lambda h=h: pe.wait_ge(act_out.sem, act_out.at(('dsq', h)))), g.d_sq)])
        for i in range(3):
            turn(X[i], ('dn_last', i), P, 27, [g.dn_last[:, 4 * i + j, :] for j in range(4)], P)

        for n in range(3):
            pe.wait_ge(act_out.sem, act_out.at(('bsplit', n)))
            pe.wait_ge(vec_out.sem, vec_out.at(('bsplit', n)))
            for d in range(4):
                ug, ub = f'gate{n}{d}', f'br{n}{d}'
                for i in range(2):
                    dense_tile(('gate', n, d, i), 0, ug, i, g.uhi, g.ulo)
                    dense_tile(('br', n, d, i), 1, ub, i, g.bhi[n % 2], g.blo[n % 2])

        def m_ready(k):
            pe.wait_ge(act_out.sem, act_out.at(('msplit', k)))
            pe.wait_ge(vec_out.sem, vec_out.at(('msplit', k)))
        for i in range(4):
            dense_unit(f'wo{i}', [('wo', 2 * i), ('wo', 2 * i + 1)], m_ready if i == 0 else None)
        column_sums('rms1', 0, [((lambda k=k: pe.wait_ge(act_out.sem, act_out.at(('hsq', k)))), g.f_sq if k % 2 == 0 else g.f_rs)
                                for k in range(KD)])

        for f in range(2):
            for j in range(FH):
                for i in range(2):
                    dense_tile(('up', f, j, i), i, f'up{f}_{j}', i, g.uhi, g.ulo,
                               (lambda k: pe.wait_ge(vec_out.sem, vec_out.at(('hn', k)))) if (f, j, i) == (0, 0, 0)
                               else None)
            for c in range(KD):
                u, slot = f'down{f}_{c}', PJ[c % 2]
                pe.wait_ge(slot.drained, slot.claim(('down', f, c)))
                for i in range(2):
                    pe.wait_ge(w_lo.sem, w_lo.at((u, i)))
                    wh, wl = split_view(hi, (u, i)), split_view(lo, (u, i))
                    for k in range(i * UP_K, FH if i else UP_K):
                        if c == 0:
                            pe.wait_ge(vec_out.sem, vec_out.at(('hff', f, k)))
                        for half in range(2):
                            cs = slice(half * HT, half * HT + HT)
                            mm = mm3(slot.ap[:, half, 0:HT], wh[:, k - i * UP_K, :], wl[:, k - i * UP_K, :],
                                     g.hhi[:, k, cs], g.hlo[:, k, cs], k == 0, k == FH - 1)
                    if i == 0:
                        mm.then_inc(pe_out.sem, pe_out.next(('used', u)))
                    else:
                        mm.then_inc(slot.filled, 1)
        for i in range(11):
            turn(X[i % 4], ('ffn_last', i), P, 18, [g.ffn_last[:, 4 * i + j, :] for j in range(4)], P)

    @g.block.scalar
    def _(ac):
        C = ACT.Copy

        def act(out, in_, f=C, **kw):
            return ac.activation(out, in_, f, **kw)

        def prep(n):
            if n >= len(TILES):
                return
            u, i = TILES[n]
            if n >= NSPLIT:
                ac.wait_ge(*last_use(TILES[n - NSPLIT]))
            if i == 0:
                ac.wait_ge(w_in_raw[UIDX[u] % NRAW].sem, w_in_raw[UIDX[u] % NRAW].at(u))
            act(split_view(hi, (u, i)), tile_of((u, i))).then_inc(w_hi.sem, w_hi.next((u, i)))
            if n and TILES[n - 1][1] == 1:
                load_unit(ac, UIDX[TILES[n - 1][0]] + NRAW)

        def next_tile(u, i):
            prep(TIDX[u, i] + NSPLIT)

        def rsqrt(out, bank, key, scale, made):
            ac.wait_ge(bank.filled, bank.at(key))
            x = bank.ap
            act(halves(out), x[:, :, 0:HT], ACT.Ln, scale=scale, bias=g.eps()).then_inc(bank.drained, 1)
            ac.wait_ge(bank.drained, bank.at(key))
            act(out, out, ACT.Exp, scale=-0.5).then_inc(act_out.sem, act_out.next(made))
            ac.wait_ge(act_out.sem, act_out.count)

        def copy_out(bank, key, pairs, **kw):
            ac.wait_ge(bank.filled, bank.at(key))
            x = bank.ap
            pairs = pairs(x)
            for dst, src in pairs[:-1]:
                act(dst, src, **kw).then_inc(act_steps.sem, act_steps.next())
                ac.wait_ge(act_steps.sem, act_steps.count)
            act(*pairs[-1], **kw).then_inc(bank.drained, 1)
            ac.wait_ge(bank.drained, bank.at(key))

        prep(0)
        prep(1)
        ac.wait_ge(x_in.sem, x_in.at('start'))
        for k in range(KD):
            if k >= 2:
                ac.wait_ge(pe_out.sem, pe_out.at(('rms0', k - 2)))
            act(g.xsq[k % 2][:, :], g.xload[:, k, :], ACT.Square).then_inc(act_out.sem, act_out.next(('sq', k)))
            ac.wait_ge(act_out.sem, act_out.count)
        prep(2)
        copy_out(X[0], 'par0', lambda x: [(g.par[:, 0:PAR0_N], x[:, 0:PAR0_N])])
        copy_out(X[1], 'par1', lambda x: [(g.par[:, PAR0_N:PAR0_N + PAR1_N], x[:, 0:PAR1_N])])
        rsqrt(g.rstd0[:, :], PJ[0], 'rms0', 1.0 / D, 'rstd0')
        copy_out(X[2], 'dn_prev', lambda x: [(g.dn_prev[:, :, :], x[:, 0:288].rearrange("p (t n) -> p t n", t=12))])
        for i, b in ((0, X[3]), (1, X[0])):
            copy_out(b, f'ffn_prev{i}', lambda x: [(g.ffn_prev[:, i * FT:i * FT + FT, :],
                                                    x[:, 0:FT * 16].rearrange("p (t n) -> p t n", t=FT))])
        act(g.gate[:, 7, 0, :], g.lrow[:, 0, :], ACT.Exp).then_inc(act_out.sem, act_out.next('states'))
        ac.wait_ge(act_out.sem, act_out.count)
        for k in range(KD):
            ac.wait_ge(vec_out.sem, vec_out.at(('uf', k)))
            act(g.uhi[:, k, :], g.xload[:, k, :]).then_inc(act_out.sem, act_out.next(('uh', k)))
            ac.wait_ge(act_out.sem, act_out.count)

        ac.wait_ge(vec_out.sem, vec_out.at(('u', KD - 1)))
        for i in range(2):
            copy_out(PJ[i], f'iq{i}', lambda x: [(halves(g.iq[:, i, :]), x[:, :, 0:HT])])
            next_tile('iq', i)
        copy_out(PJ[0], 'ik', lambda x: [(halves(g.ik[:, :]), x[:, :, 0:HT])])
        next_tile('ik', 0)
        ac.wait_ge(vec_out.sem, vec_out.at('small_zero'))
        copy_out(X[1], 'small', lambda x: [(g.small[:, 0:4, :], x[:, 0:48].rearrange("p (c n) -> p c n", c=4)),
                                           (g.small[0:NS, 4, :], x[0:NS, 48:60])])
        next_tile('ik', 1)
        for h in range(H):
            act(g.iqs[:, h, :], g.iq[64 * (h % 2):64 * (h % 2) + 64, h // 2, SEQ:NT]).then_inc(
                    act_out.sem, act_out.next('iqs' if h == H - 1 else None))
            ac.wait_ge(act_out.sem, act_out.count)
        copy_out(X[0], 'kidx_tok', lambda x: [(g.kidx_tok[:, 0:4, :], x[:, 0:256].rearrange("p (c n) -> p c n", c=4)),
                                              (g.kidx_tok[0:NS, 4, :], x[0:NS, 256:320])])
        ac.dma_start(at_layer('p_kidx').rearrange("a b (c p) n -> p (a b c) n", p=P), g.kidx_tok[:, 0:4, :]).then_inc(
                st_idx.sem, st_idx.next(by=16))
        ac.dma_start(at_layer('s_kidx').rearrange("a b t n -> (a b t) n"), g.kidx_tok[0:NS, 4, :]).then_inc(
                st_idx.sem, st_idx.next('all', 16))
        i = 0
        for qb in range(1, 4):
            n = (qb + 1) * P
            for h in range(H):
                if i >= 2:
                    ac.wait_ge(vec_out.sem, vec_out.at(('score', i - 2)))
                copy_out(X[2 + i % 2], ('is', qb, h), lambda x: [(g.relu_p[i % 2][:, 0:n], x[:, 0:n])], f=ACT.Relu)
                i += 1
        copy_out(X[2], 'wrow', lambda x: [(g.wrow[:, :, :].rearrange("p b (h t) -> p b h t", h=H),
                                           x[:, 0:P].rearrange("p (h b t) -> p b h t", h=H, b=DB))])
        for b in range(DB):
            if b:
                ac.wait_ge(X[2 + (b - 1) % 2].filled, X[2 + (b - 1) % 2].at(('sT', b - 1)))
            copy_out(X[0], ('kidxT0', b), lambda x: [(g.kidxT[:, 0:512], x[0:64, :])])
            copy_out(X[1], ('kidxT', b), lambda x: [(g.kidxT[:, 512:1024], x[0:64, :])])
        copy_out(X[0], 's_new', lambda x: [(g.relu_s[:, :], x[0:NS, 0:P])], f=ACT.Relu)
        for q in range(2):
            copy_out(X[1 + q], ('s_score', q), lambda x: [(g.sel_s[:, q * 512:q * 512 + 512], x[0:NS, :])])

        ac.wait_ge(vec_out.sem, vec_out.at('index_done'))
        ac.wait_ge(st_idx.sem, st_idx.at('all'))
        prev = None
        for nm in ('rq', 'rk', 'rv', 'rg'):
            for h in range(H):
                b, key = PJ[h % 2], (nm, h)
                if nm in ('rq', 'rk'):
                    if prev is not None:
                        ac.wait_ge(vec_out.sem, vec_out.at(prev))
                    sc = SCALE if nm == 'rq' else 1.0
                    copy_out(b, key, lambda x: [(halves(g.rraw[:, :]), x[:, :, 0:HT]),
                                                (halves(g.rswap[0:64, :]), x[64:P, :, 0:HT]),
                                                (halves(g.rswap[64:P, :]), x[0:64, :, 0:HT])], scale=sc)
                    prev = key
                elif nm == 'rv':
                    copy_out(b, key, lambda x: [(halves(g.rv[:, h, :]), x[:, :, 0:HT])])
                else:
                    copy_out(b, key, lambda x: [(halves(g.out_ret[:, h, :]), x[:, :, 0:HT])], f=ACT.Silu)
                next_tile(f'{nm}{h // 2}', h % 2)
        for c in range(5):
            cs, n = chunk_of(c)
            if c:
                ac.wait_ge(X[0].filled, X[0].at(('rS', c - 1)))
            copy_out(X[1], ('rvT', c), lambda x: [(g.r_v[0:n, :], x[0:n, :])])
            if c == 4:
                for b in range(DB):
                    ac.wait_ge(vec_out.sem, vec_out.at(('rs', b)))
                    ac.dma_start(at_layer('s_ret').rearrange("a b h k v -> k (a b) h v")[:, b],
                                              head_view(g.r_sout, P)).then_inc(
                            st_ss[0].sem, st_ss[0].next(('ret', b), 16))
            copy_out(X[3], ('ro', c), lambda x: [(g.rv[:, :, cs], head_view(x, n))])
            if c == 3:
                ac.wait_ge(vec_out.sem, vec_out.at(('r_state', 3)))
                ac.dma_start(at_layer('p_ret').rearrange("a b h k v -> k (a b h) v"),
                                          head_view(g.r_S, P)).then_inc(st_state.sem, st_state.next('ret', 16))
        for h in range(H):
            ac.wait_ge(vec_out.sem, vec_out.at(('rxc', h)))
            if h:
                ac.wait_ge(PJ[1].filled, PJ[1].at(('rvar', h - 1)))
            act(g.rswap[:, :], g.rraw[:, :], ACT.Square).then_inc(act_out.sem, act_out.next(('rsq', h)))
            ac.wait_ge(act_out.sem, act_out.count)
            rsqrt(g.rswap[:, :], PJ[1], ('rvar', h), 1.0 / P, ('rrs', h))
            ac.wait_ge(vec_out.sem, vec_out.at(('rout', h)))

        for nm in ('aq', 'ak', 'av'):
            if nm == 'ak':
                ac.wait_ge(st_state.sem, st_state.at('ret'))
                ac.wait_ge(st_ss[0].sem, st_ss[0].at(('ret', DB - 1)))
            for h in range(H):
                dst = g.out_att[:, h, :] if nm == 'aq' else g.akv[:, h + (4 if nm == 'av' else 0), :]
                copy_out(PJ[h % 2], (nm, h), lambda x: [(halves(dst), x[:, :, 0:HT])],
                         scale=SCALE if nm == 'aq' else 1.0)
                next_tile(f'{nm}{h // 2}', h % 2)
        for c in range(5):
            cs, n = chunk_of(c)
            if c >= 2:
                ac.wait_ge(st_k[c % 2].sem, st_k[c % 2].at(c - 2))
            copy_out(X[0], ('kT', c), lambda x: [(g.ktok[c % 2][0:n, :], x[0:n, :])])
            copy_out(X[1], ('vT', c), lambda x: [(g.vtok[0:n, c, :], x[0:n, :])])
            for nm, sig, src, key in (('k', st_k[c % 2], g.ktok[c % 2][0:n, :], c),
                                      ('v', st_kv, g.vtok[0:n, c, :], 'v' if c == 4 else None)):
                if c < 4:
                    dst = at_layer(f'p_{nm}').rearrange("a b (c p) h d -> (a b c) p (h d)", p=P)[c]
                else:
                    dst = at_layer(f's_{nm}').rearrange("a b t h d -> (a b t) (h d)")
                ac.dma_start(dst, src).then_inc(sig.sem, sig.next(key, 16))
        act(g.s_ak[:, :, :], g.akv[:, 0:4, SEQ:NT]).then_inc(act_steps.sem, act_steps.next())
        ac.wait_ge(act_steps.sem, act_steps.count)
        act(g.s_v[:, :], g.vtok[0:NS, 4, :]).then_inc(act_out.sem, act_out.next('s_kv'))
        ac.wait_ge(act_out.sem, act_out.count)
        steps = [(qb, h) for qb in range(4) for h in range(H)]
        for i in range(len(steps) + 1):
            if i < len(steps):
                n = (steps[i][0] + 1) * P
                ac.wait_ge(vec_out.sem, vec_out.at(('nmax', i)))
                if i >= 2:
                    ac.wait_ge(X[2 + i % 2].filled, X[2 + i % 2].at(('pT', i - 2)))
                act(g.prob[i % 2][:, 0:n], g.logit[i % 2][:, 0:n], ACT.Exp, bias=g.stat[:, 4 + i % 2:5 + i % 2],
                         accum_out=g.stat[:, 6 + i % 2:7 + i % 2]).then_inc(act_out.sem, act_out.next(('exp', i)))
                ac.wait_ge(act_out.sem, act_out.count)
            if i:
                j = i - 1
                qb, h = steps[j]
                n = (qb + 1) * P
                copy_out(X[2 + j % 2], ('pT', j), lambda x: [(g.probT[j % 2][:, 0:n], x[:, 0:n])])
                if h == H - 1:
                    copy_out(PJ[qb % 2], ('ao', qb), lambda x: [(g.out_att[:, :, qb * P:qb * P + P],
                                                                 head_view(x[:, 0, :], P))])

        ac.wait_ge(st_kv.sem, st_kv.at('v'))
        ac.wait_ge(st_k[0].sem, st_k[0].at(4))
        ac.wait_ge(st_k[1].sem, st_k[1].at(3))

        def even_page(i):
            if i < NPAGES:
                copy_out(X[0], ('sk', i), lambda x: [(g.kT[0][:, :], x[:, :])])

        def past_logits(b):
            copy_out(X[2 + b % 2], ('slT', b), lambda x: [(g.s_lT[:, :, :, b, :],
                                                           x[:, 0:P].rearrange("p (g h t) -> p g h t", h=H, t=DS))])

        def seqs(ap, base, w):
            return ap[:, base:base + DB * w].rearrange("p (b w) -> p b w", b=DB)

        def silu_of(t):
            ac.wait_ge(vec_out.sem, vec_out.at(('conv', t)))
            y = g.d_conv[t % 2]
            act(g.qkv[:, t, 0:SEQ], y[:, 0:SEQ], ACT.Silu).then_inc(act_steps.sem, act_steps.next())
            ac.wait_ge(act_steps.sem, act_steps.count)
            act(g.qkv[:, t, SEQ:NT].rearrange("p (b t) -> p b t", b=DB), seqs(y, 515, 7)[:, :, 0:4], ACT.Silu).then_inc(
                    act_out.sem, act_out.next(('silu', t)))
            ac.wait_ge(act_out.sem, act_out.count)
        ac.wait_ge(vec_out.sem, vec_out.at('d_pads'))
        even_page(0)
        for t in range(12):
            even_page(4 * t + 2)
            pad = g.d_pad[t % 2]
            if t >= 2:
                ac.wait_ge(vec_out.sem, vec_out.at(('conv', t - 2)))
            copy_out(PJ[t % 2], ('dn', t), lambda x: [
                (pad[:, 3:3 + HT], x[:, 0, 0:HT]), (pad[:, 3 + HT:3 + SEQ], x[:, 1, 0:SEQ - HT]),
                (seqs(pad, 515, 7)[:, :, 3:7], x[:, 1, SEQ - HT:HT].rearrange("p (b t) -> p b t", b=DB))])
            act(seqs(pad, 515, 7)[:, :, 0:3], g.dn_prev[:, t, :].rearrange("p (b i) -> p b i", b=DB)).then_inc(
                    act_out.sem, act_out.next(('pad', t)))
            ac.wait_ge(act_out.sem, act_out.count)
            act(g.dn_last[:, t, 0:3], pad[:, SEQ:SEQ + 3]).then_inc(act_steps.sem, act_steps.next())
            ac.wait_ge(act_steps.sem, act_steps.count)
            act(g.dn_last[:, t, 3:27].rearrange("p (b i) -> p b i", b=DB), seqs(pad, 515, 7)[:, :, 4:7]).then_inc(
                    act_steps.sem, act_steps.next())
            ac.wait_ge(act_steps.sem, act_steps.count)
            even_page(4 * t + 4)
            if t % 2:
                past_logits(t // 2)
            next_tile(f'dn{t // 2}', t % 2)
            if t:
                silu_of(t - 1)
        silu_of(11)
        for h in range(H):
            even_page(4 * (12 + h) + 2)
            copy_out(PJ[h % 2], ('z', h), lambda x: [(halves(g.out_dn[:, h, :]), x[:, :, 0:HT])], f=ACT.Silu)
            even_page(4 * (12 + h) + 4)
            if h % 2:
                past_logits((12 + h) // 2)
            next_tile(f'z{h // 2}', h % 2)
        for q in range(2):
            copy_out(X[q], ('srep', q), lambda x: [(g.s_log[:, q * 512:q * 512 + 512], x[:, :])])
        copy_out(X[0], ('srep', 2), lambda x: [(g.s_log[:, PAST:NEWK], x[:, 0:NS])])
        ac.wait_ge(vec_out.sem, vec_out.at('g_arg'))
        act(gBeta, g.small[:, :, 0:4], ACT.Sigmoid).then_inc(act_out.sem, act_out.next('beta'))
        ac.wait_ge(act_out.sem, act_out.count)
        act(gA, gTmp, ACT.Abs).then_inc(act_steps.sem, act_steps.next())
        ac.wait_ge(act_steps.sem, act_steps.count)
        act(gA, gA, ACT.Exp, scale=-1.0).then_inc(act_steps.sem, act_steps.next())
        ac.wait_ge(act_steps.sem, act_steps.count)
        act(gA, gA, ACT.Ln, bias=1.0).then_inc(act_out.sem, act_out.next('conv_done'))
        ac.wait_ge(act_out.sem, act_out.count)
        for t in range(8):
            if t == 2:
                ac.wait_ge(vec_out.sem, vec_out.at('s_nmax'))
                act(g.s_log[:, :], g.s_log[:, :], ACT.Exp, bias=g.stat[:, 8:9], accum_out=g.stat[:, 9:10]).then_inc(
                        act_out.sem, act_out.next('s_exp'))
                ac.wait_ge(act_out.sem, act_out.count)
            if t:
                ac.wait_ge(PJ[(t - 1) % 2].filled, PJ[(t - 1) % 2].at(('l2', t - 1)))
                ac.wait_ge(vec_out.sem, vec_out.at(('l2', t - 1)))
            act(g.d_sq, g.qkv[:, t, :], ACT.Square).then_inc(act_out.sem, act_out.next(('l2sq', t)))
            ac.wait_ge(act_out.sem, act_out.count)
            rsqrt(g.d_rs, PJ[t % 2], ('l2', t), 1.0, ('l2rs', t))
        ac.wait_ge(X[3].filled, X[3].at('gsum'))
        x = X[3].ap
        v16 = lambda at: x[:, at:at + 16].rearrange("p (c h) -> p c h", c=4)
        act(gC[:, 0:4, :], v16(0)).then_inc(act_steps.sem, act_steps.next())
        ac.wait_ge(act_steps.sem, act_steps.count)
        act(gC[0:NS, 4, :], x[0:NS, 16:20]).then_inc(act_steps.sem, act_steps.next())
        ac.wait_ge(act_steps.sem, act_steps.count)
        act(gEK[:, 0:4, :], v16(20), ACT.Exp).then_inc(act_steps.sem, act_steps.next())
        ac.wait_ge(act_steps.sem, act_steps.count)
        act(gEK[0:NS, 4, :], x[0:NS, 36:40], ACT.Exp).then_inc(X[3].drained, 1)
        ac.wait_ge(X[3].drained, X[3].at('gsum'))
        act(gBE[:, 0:4, :], gC[:, 0:4, :], ACT.Exp).then_inc(act_steps.sem, act_steps.next())
        ac.wait_ge(act_steps.sem, act_steps.count)
        act(gBE[0:NS, 4, :], gC[0:NS, 4, :], ACT.Exp).then_inc(act_out.sem, act_out.next('gexp'))
        ac.wait_ge(act_out.sem, act_out.count)
        for q in range(2):
            copy_out(X[2 + q], ('spT', q), lambda x: [(g.s_pT[:, q * 4:q * 4 + 4, :],
                                                       x[:, :].rearrange("p (g n) -> p g n", g=4))])
        copy_out(X[0], 'spT_new', lambda x: [(g.s_pT[0:NS, NPG, :], x[0:NS, 0:P])])
        for c in range(5):
            cs, n = chunk_of(c)
            ac.wait_ge(vec_out.sem, vec_out.at(('dif', c)))
            act(g.d_dec[0:n, 0:4 * n], g.d_dec[0:n, 0:4 * n], ACT.Exp).then_inc(act_out.sem, act_out.next(('dec', c)))
            ac.wait_ge(act_out.sem, act_out.count)
            copy_out(X[0], ('grow', c), lambda x: [(g.d_eg[:, 0:4 * n], x[:, 0:4 * n])], f=ACT.Exp)
            for s in (LEVELS if c < 4 else LEVELS[:2]):
                copy_out(X[2], ('Y', c, s), lambda x: [(g.d_y[0:n, 0:4 * n], x[0:n, 0:4 * n])])
            copy_out(X[1], ('kc', c), lambda x: [(g.d_kc[:, 0:4 * n], x[:, 0:4 * n])])
            if c < 4:
                copy_out(X[2], ('dw', c), lambda x: [(g.d_w[:, :], x[:, :])])
            else:
                copy_out(X[2], ('dw', c), lambda x: [(g.d_eg[:, 128:256], x[:, 0:P])])
                copy_out(X[1], 'dwT', lambda x: [(g.d_w[0:NS, :], x[0:NS, :])])
            copy_out(X[3], ('do', c), lambda x: [(g.qkv[:, 8:12, cs], head_view(x, n))])
            if c == 3:
                copy_out(PJ[0], 'so', lambda x: [(g.out_att[:, :, SEQ:NT], head_view(x[:, 0, :], NS))])
                ac.wait_ge(vec_out.sem, vec_out.at(('d_state', 3)))
                ac.dma_start(at_layer('p_dn').rearrange("a b h k v -> k (a b h) v"),
                                          head_view(g.d_S, P)).then_inc(st_state.sem, st_state.next('dn', 16))
        for b in range(DB):
            ac.wait_ge(vec_out.sem, vec_out.at(('ds', DB + b)))
            ac.dma_start(at_layer('s_dn').rearrange("a b h k v -> k (a b) h v")[:, b],
                                      head_view(g.d_sout, P)).then_inc(st_ss[1].sem, st_ss[1].next(b, 16))
        for h in range(H):
            if h:
                ac.wait_ge(vec_out.sem, vec_out.at(('dout', h - 1)))
            act(g.d_sq, g.qkv[:, 8 + h, :], ACT.Square).then_inc(act_out.sem, act_out.next(('dsq', h)))
            ac.wait_ge(act_out.sem, act_out.count)
            rsqrt(g.d_rs, PJ[h % 2], ('dvar', h), 1.0 / P, ('drs', h))
        for i, st in enumerate((g.d_t, g.d_tt, g.d_y)):
            copy_out(X[i], ('dn_last', i), lambda x: [(st[0:27, :], x[0:27, :])])
            ac.dma_start(at_layer('p_dn_conv').rearrange("a b i n -> (a b i) n")[:, i * 512:i * 512 + 512],
                                   st[0:3, :]).then_inc(st_dn.sem, st_dn.next(by=16))
            ac.dma_start(at_layer('s_dn_conv').rearrange("a b i n -> (a b i) n")[:, i * 512:i * 512 + 512],
                                   st[3:27, :]).then_inc(st_dn.sem, st_dn.next(i, 16))

        ac.wait_ge(vec_out.sem, vec_out.at(('dout', 3)))
        ac.wait_ge(st_state.sem, st_state.at('dn'))
        ac.wait_ge(st_ss[1].sem, st_ss[1].at(DB - 1))
        ac.wait_ge(st_dn.sem, st_dn.at(2))
        outs = (g.out_dn, g.out_ret, g.out_att)

        def bsplit(n):
            if n == 2:
                ac.wait_ge(PJ[1].filled, PJ[1].at(('br', 0, 3, 1)))
            act(g.bhi[n % 2][:, :, :], outs[n][:, :, :]).then_inc(act_out.sem, act_out.next(('bsplit', n)))
            ac.wait_ge(act_out.sem, act_out.count)
        bsplit(0)
        bsplit(1)
        i = 0
        for n in range(3):
            if n == 1:
                bsplit(2)
            for d in range(4):
                for j in range(2):
                    if i >= 2:
                        ac.wait_ge(vec_out.sem, vec_out.at(('mul', i - 2)))
                    copy_out(PJ[0], ('gate', n, d, j), lambda x: [(halves(g.sig[i % 2][:, :]), x[:, :, 0:HT])],
                             f=ACT.Sigmoid)
                    i += 1
                    next_tile(f'gate{n}{d}', j)
                    next_tile(f'br{n}{d}', j)
        for k in range(KD):
            ac.wait_ge(vec_out.sem, vec_out.at(('m', k)))
            act(g.uhi[:, k, :], g.m[:, k, :]).then_inc(act_out.sem, act_out.next(('msplit', k)))
            ac.wait_ge(act_out.sem, act_out.count)
        for i in range(4):
            next_tile(f'wo{i}', 0)
            next_tile(f'wo{i}', 1)
        for k in range(KD):
            ac.wait_ge(vec_out.sem, vec_out.at(('h', k)))
            if k >= 2:
                ac.wait_ge(pe_out.sem, pe_out.at(('rms1', k - 2)))
            act(g.f_sq if k % 2 == 0 else g.f_rs, g.x[:, k, :], ACT.Square).then_inc(
                    act_out.sem, act_out.next(('hsq', k)))
            ac.wait_ge(act_out.sem, act_out.count)
        rsqrt(g.f_act[:, :], PJ[0], 'rms1', 1.0 / D, 'rstd1')
        for k in range(KD):
            ac.wait_ge(vec_out.sem, vec_out.at(('hf', k)))
            act(g.uhi[:, k, :], g.f_conv[k % 2][:, 0:NT]).then_inc(act_out.sem, act_out.next(('hh', k)))
            ac.wait_ge(act_out.sem, act_out.count)

        ac.wait_ge(vec_out.sem, vec_out.at('f_pads'))
        for f in range(2):
            for j in range(FH):
                for i in range(2):
                    pad, t = g.f_pad[i], f * FH + j + i * FT
                    if (f, j) != (0, 0):
                        ac.wait_ge(vec_out.sem, vec_out.at(('fconv', *divmod(f * FH + j - 1, FH), i)))
                    copy_out(PJ[i], ('up', f, j, i), lambda x: [
                        (pad[:, 2:2 + HT], x[:, 0, 0:HT]), (pad[:, 2 + HT:2 + SEQ], x[:, 1, 0:SEQ - HT]),
                        (seqs(pad, 514, 6)[:, :, 2:6], x[:, 1, SEQ - HT:HT].rearrange("p (b t) -> p b t", b=DB))])
                    act(seqs(pad, 514, 6)[:, :, 0:2], g.ffn_prev[:, t, :].rearrange("p (b i) -> p b i", b=DB)).then_inc(
                            act_out.sem, act_out.next(('fpad', f, j, i)))
                    ac.wait_ge(act_out.sem, act_out.count)
                    act(g.ffn_last[:, t, 0:2], pad[:, SEQ:SEQ + 2]).then_inc(act_steps.sem, act_steps.next())
                    ac.wait_ge(act_steps.sem, act_steps.count)
                    act(g.ffn_last[:, t, 2:18].rearrange("p (b i) -> p b i", b=DB), seqs(pad, 514, 6)[:, :, 4:6]).then_inc(
                            act_steps.sem, act_steps.next())
                    ac.wait_ge(act_steps.sem, act_steps.count)
                    next_tile(f'up{f}_{j}', i)
                ac.wait_ge(vec_out.sem, vec_out.at(('fconv', f, j, 0)))
                if (f, j) != (0, 0):
                    ac.wait_ge(vec_out.sem, vec_out.at(('hff', *divmod(f * FH + j - 1, FH))))
                y = g.f_conv[0]
                act(g.f_act[:, 0:SEQ], y[:, 0:SEQ], ACT.Silu).then_inc(act_steps.sem, act_steps.next())
                ac.wait_ge(act_steps.sem, act_steps.count)
                act(g.f_act[:, SEQ:NT].rearrange("p (b t) -> p b t", b=DB), seqs(y, 514, 6)[:, :, 0:4], ACT.Silu).then_inc(
                        act_out.sem, act_out.next(('fsilu', f, j)))
                ac.wait_ge(act_out.sem, act_out.count)
                ac.wait_ge(vec_out.sem, vec_out.at(('hprod', f, j)))
                if f == 1 and j == 0:
                    ac.wait_ge(PJ[1].filled, PJ[1].at(('down', 0, 7)))
                act(g.hhi[:, j, :], g.f_act[:, :]).then_inc(act_out.sem, act_out.next(('hhi', f, j)))
                ac.wait_ge(act_out.sem, act_out.count)
            for c in range(KD):
                next_tile(f'down{f}_{c}', 0)
                next_tile(f'down{f}_{c}', 1)
        stage = [g.f_pad[0], g.f_pad[1], g.f_conv[0], g.f_conv[1]]
        for i in range(11):
            st = stage[i % 4]
            if i >= 4:
                ac.wait_ge(st_ffn[i % 4].sem, st_ffn[i % 4].at(i - 4))
            copy_out(X[i % 4], ('ffn_last', i), lambda x: [(st[0:18, 0:512], x[0:18, :])])
            for nm, lo_, hi_ in (('p_ffn_conv', 0, 2), ('s_ffn_conv', 2, 18)):
                ac.dma_start(at_layer(nm).rearrange("a b i n -> (a b i) n")[:, i * 512:i * 512 + 512],
                                               st[lo_:hi_, 0:512]).then_inc(
                        st_ffn[i % 4].sem, st_ffn[i % 4].next(i if hi_ == 18 else None, 16))
        for i in range(7, 11):
            ac.wait_ge(st_ffn[i % 4].sem, st_ffn[i % 4].at(i))

    @g.block.vector
    def _(ve):
        tt, stt, ts = ve.tensor_tensor, ve.scalar_tensor_tensor, ve.tensor_scalar
        par = lambda n, i=0: g.par[:, (PAR0[n] if n in PAR0 else PAR0_N + PAR1[n]) + i:][:, 0:1]

        def bcast(ap, n):
            return ap.unsqueeze(2).to_broadcast([ap.shape[0], ap.shape[1], n])

        def over_heads(ap):
            return ap.unsqueeze(1).to_broadcast([ap.shape[0], H, ap.shape[1]])

        ve.memset(g.small[:, 4, :], 0.0).then_inc(vec_out.sem, vec_out.next('small_zero'))
        ve.wait_ge(vec_out.sem, vec_out.count)
        ve.wait_ge(X[0].drained, X[0].at('par0'))
        ve.wait_ge(x_in.sem, x_in.at('start'))
        ve.wait_ge(act_out.sem, act_out.at('rstd0'))
        for k in range(KD):
            stt(g.xload[:, k, :], g.xload[:, k, :], par('mix', k), g.rstd0[:, :], ALU.mult, ALU.mult).then_inc(
                    vec_out.sem, vec_out.next(('uf', k)))
            ve.wait_ge(vec_out.sem, vec_out.count)
            if k:
                ve.wait_ge(act_out.sem, act_out.at(('uh', k - 1)))
                tt(g.ulo[:, k - 1, :], g.xload[:, k - 1, :], g.uhi[:, k - 1, :].bitcast(F32), ALU.subtract).then_inc(
                        vec_out.sem, vec_out.next(('u', k - 1)))
                ve.wait_ge(vec_out.sem, vec_out.count)
        ve.wait_ge(act_out.sem, act_out.at(('uh', KD - 1)))
        tt(g.ulo[:, KD - 1, :], g.xload[:, KD - 1, :], g.uhi[:, KD - 1, :].bitcast(F32), ALU.subtract).then_inc(
                vec_out.sem, vec_out.next(('u', KD - 1)))
        ve.wait_ge(vec_out.sem, vec_out.count)

        ve.wait_ge(X[1].drained, X[1].at('small'))
        w = g.gate[:, 6]
        ts(w, g.small[:, :, 8:12], 1.0 / 16.0, None, ALU.mult).then_inc(vec_steps.sem, vec_steps.next())
        ve.wait_ge(vec_steps.sem, vec_steps.count)
        ve.tensor_copy(g.sel[:, 0:P], const('causal')).then_inc(vec_steps.sem, vec_steps.next())
        ve.wait_ge(vec_steps.sem, vec_steps.count)
        i = 0
        for qb in range(1, 4):
            n = (qb + 1) * P
            sc = g.sel[:, g.selat[qb]:g.selat[qb] + n]
            for h in range(H):
                ve.wait_ge(X[2 + i % 2].drained, X[2 + i % 2].at(('is', qb, h)))
                r = g.relu_p[i % 2][:, 0:n]
                if h == 0:
                    ts(sc, r, w[:, qb, h:h + 1], None, ALU.mult).then_inc(vec_out.sem, vec_out.next(('score', i)))
                    ve.wait_ge(vec_out.sem, vec_out.count)
                else:
                    stt(sc, r, w[:, qb, h:h + 1], sc, ALU.mult, ALU.add).then_inc(
                            vec_out.sem, vec_out.next(('score', i)))
                    ve.wait_ge(vec_out.sem, vec_out.count)
                i += 1
            tt(sc[:, n - P:n], sc[:, n - P:n], const('causal'), ALU.add).then_inc(vec_steps.sem, vec_steps.next())
            ve.wait_ge(vec_steps.sem, vec_steps.count)
        for b in range(DB):
            if b == 0:
                ve.wait_ge(X[2].drained, X[2].at('wrow'))
            bank = X[2 + b % 2]
            ve.wait_ge(bank.filled, bank.at(('sT', b)))
            x = bank.ap
            stt(g.sprod[:, :, :], x[:, 0:P].rearrange("p (g n) -> p g n", g=NPG), 0.0,
                        g.wrow[:, b, :].unsqueeze(1).to_broadcast([P, NPG, 16]), ALU.max, ALU.mult).then_inc(
                    bank.drained, 1)
            ve.wait_ge(bank.drained, bank.at(('sT', b)))
            ve.tensor_reduce(g.scoreT[:, :, b * DS:b * DS + DS],
                                  g.sprod[:, :, :].rearrange("p g (h t) -> p g t h", h=H), AX.X, ALU.add).then_inc(
                    vec_out.sem, vec_out.next('scoreT' if b == DB - 1 else None))
            ve.wait_ge(vec_out.sem, vec_out.count)
        ve.wait_ge(X[0].drained, X[0].at('s_new'))
        new = g.sel_s[:, PAST:NEWK]
        ws = g.small[0:NS, 4, 8:12]
        for h in range(H):
            r = g.relu_s[:, h * NS:h * NS + NS]
            if h == 0:
                ts(new, r, ws[:, h:h + 1], None, ALU.mult).then_inc(vec_steps.sem, vec_steps.next())
                ve.wait_ge(vec_steps.sem, vec_steps.count)
            else:
                stt(new, r, ws[:, h:h + 1], new, ALU.mult, ALU.add).then_inc(vec_steps.sem, vec_steps.next())
                ve.wait_ge(vec_steps.sem, vec_steps.count)
        tt(new, new, const('causal_s', NS)[:, 0:NS], ALU.add).then_inc(vec_out.sem, vec_out.next('index_done'))
        ve.wait_ge(vec_out.sem, vec_out.count)

        def rounds():
            for qb in range(1, 4):
                n = (qb + 1) * P
                sc = g.sel[:, g.selat[qb]:g.selat[qb] + n]
                yield sc, TOPK_P // 8, None
            yield g.sel_s[:, :], TOPK_S // 8, 'sel_s'

        def choose(sc, n_rounds, key):
            p = sc.shape[0]
            if key:
                ve.wait_ge(X[2].drained, X[2].at(('s_score', 1)))
            for _ in range(n_rounds):
                ve.max(g.mx[0:p, :], sc).then_inc(vec_steps.sem, vec_steps.next())
                ve.wait_ge(vec_steps.sem, vec_steps.count)
                ve.match_replace(sc, g.mx[0:p, :], sc, TAKEN).then_inc(vec_steps.sem, vec_steps.next())
                ve.wait_ge(vec_steps.sem, vec_steps.count)
            ts(sc, sc, TAKEN / 1.5, NEG, ALU.is_gt, ALU.mult).then_inc(vec_out.sem, vec_out.next(key))
            ve.wait_ge(vec_out.sem, vec_out.count)
        todo = list(rounds())

        for nm in ('rq', 'rk'):
            for h in range(H):
                ve.wait_ge(PJ[h % 2].drained, PJ[h % 2].at((nm, h)))
                dst = g.rqk[:, h + (4 if nm == 'rk' else 0), :]
                tt(dst, g.rraw[:, :], const('cos'), ALU.mult).then_inc(vec_steps.sem, vec_steps.next())
                ve.wait_ge(vec_steps.sem, vec_steps.count)
                tt(g.rswap[:, :], g.rswap[:, :], const('sin'), ALU.mult).then_inc(vec_steps.sem, vec_steps.next())
                ve.wait_ge(vec_steps.sem, vec_steps.count)
                tt(dst, dst, g.rswap[:, :], ALU.add).then_inc(vec_out.sem, vec_out.next((nm, h)))
                ve.wait_ge(vec_out.sem, vec_out.count)
        for t in todo[:3]:
            choose(*t)
        ve.memset(g.r_S[:, :], 0.0).then_inc(vec_steps.sem, vec_steps.next())
        ve.wait_ge(vec_steps.sem, vec_steps.count)
        gt = [float(np.exp(np.log1p(-2.0 ** (-5.0 - h)) * P)) for h in range(H)]
        gt_s = [float(np.exp(np.log1p(-2.0 ** (-5.0 - h)) * DS)) for h in range(H)]
        for c in range(5):
            cs, n = chunk_of(c)
            rk_, rq_, dc = ('r_k', 'r_q', 'r_decay') if c < 4 else ('rs_k', 'rs_q', 'rs_decay')
            ve.wait_ge(X[0].filled, X[0].at(('rkT', c)))
            x = X[0].ap
            tt(head_view(g.r_kd[0:n, :], P), head_view(x[0:n, :], P), bcast(const(rk_, n), P), ALU.mult).then_inc(
                    X[0].drained, 1)
            ve.wait_ge(X[0].drained, X[0].at(('rkT', c)))
            tt(head_view(g.r_qd, n), g.rqk[:, 0:4, cs], head_view(const(rq_), n), ALU.mult).then_inc(
                    vec_steps.sem, vec_steps.next())
            ve.wait_ge(vec_steps.sem, vec_steps.count)
            ve.wait_ge(X[2].filled, X[2].at(('rqk', c)))
            x = X[2].ap
            tt(g.r_qk[0:n, 0:4 * n], x[0:n, 0:4 * n], const(dc, n), ALU.mult).then_inc(X[2].drained, 1)
            ve.wait_ge(X[2].drained, X[2].at(('rqk', c)))
            ve.engine_nop().then_inc(vec_out.sem, vec_out.next(('r_in', c)))
            ve.wait_ge(vec_out.sem, vec_out.count)
            if c < 4:
                ve.wait_ge(X[0].filled, X[0].at(('rS', c)))
                x = X[0].ap
                for h in range(H):
                    hs = slice(h * P, h * P + P)
                    ins = stt(g.r_S[:, hs], g.r_S[:, hs], gt[h], x[:, hs], ALU.mult, ALU.add)
                    if h < H - 1:
                        ins.then_inc(vec_steps.sem, vec_steps.next())
                        ve.wait_ge(vec_steps.sem, vec_steps.count)
                    else:
                        ins.then_inc(X[0].drained, 1)
                        ve.wait_ge(X[0].drained, X[0].at(('rS', c)))
                ve.engine_nop().then_inc(vec_out.sem, vec_out.next(('r_state', c)))
                ve.wait_ge(vec_out.sem, vec_out.count)
            else:
                for b in range(DB):
                    if b:
                        ve.wait_ge(X[(b - 1) % 2].filled, X[(b - 1) % 2].at(('rS', c, b - 1)))
                    ts(g.r_kdm[:, :], g.r_kd[0:NS, :], const('seq_of', NS)[:, b:b + 1], None, ALU.mult).then_inc(
                            vec_out.sem, vec_out.next(('kdm', b)))
                    ve.wait_ge(vec_out.sem, vec_out.count)
                    if b:
                        ve.wait_ge(st_ss[0].sem, st_ss[0].at(('ret', b - 1)))
                    ve.wait_ge(X[b % 2].filled, X[b % 2].at(('rS', c, b)))
                    x = X[b % 2].ap
                    for h in range(H):
                        hs = slice(h * P, h * P + P)
                        ins = stt(g.r_sout[:, hs], g.r_sin[b % 2][:, hs], gt_s[h], x[:, hs], ALU.mult, ALU.add)
                        if h < H - 1:
                            ins.then_inc(vec_steps.sem, vec_steps.next())
                            ve.wait_ge(vec_steps.sem, vec_steps.count)
                        else:
                            ins.then_inc(X[b % 2].drained, 1)
                            ve.wait_ge(X[b % 2].drained, X[b % 2].at(('rS', c, b)))
                    ve.engine_nop().then_inc(vec_out.sem, vec_out.next(('rs', b)))
                    ve.wait_ge(vec_out.sem, vec_out.count)
        for h in range(H):
            ve.wait_ge(PJ[0].filled, PJ[0].at(('rmean', h)))
            x = PJ[0].ap
            stt(halves(g.rraw[:, :]), x[:, :, 0:HT], -1.0 / P, halves(g.rv[:, h, :]), ALU.mult, ALU.add).then_inc(
                    PJ[0].drained, 1)
            ve.wait_ge(PJ[0].drained, PJ[0].at(('rmean', h)))
            ve.engine_nop().then_inc(vec_out.sem, vec_out.next(('rxc', h)))
            ve.wait_ge(vec_out.sem, vec_out.count)
            ve.wait_ge(act_out.sem, act_out.at(('rrs', h)))
            stt(g.rraw[:, :], g.rraw[:, :], par('retn', h), g.rswap[:, :], ALU.mult, ALU.mult).then_inc(
                    vec_steps.sem, vec_steps.next())
            ve.wait_ge(vec_steps.sem, vec_steps.count)
            tt(g.out_ret[:, h, :], g.out_ret[:, h, :], g.rraw[:, :], ALU.mult).then_inc(
                    vec_out.sem, vec_out.next(('rout', h)))
            ve.wait_ge(vec_out.sem, vec_out.count)

        choose(*todo[3])
        steps = [(qb, h) for qb in range(4) for h in range(H)]
        for i in range(len(steps) + 1):
            if i < len(steps):
                qb, h = steps[i]
                n = (qb + 1) * P
                ve.wait_ge(X[i % 2].filled, X[i % 2].at(('qk', i)))
                x = X[i % 2].ap
                L = g.logit[i % 2]
                tt(L[:, 0:n], x[:, 0:n], g.sel[:, g.selat[qb]:g.selat[qb] + n], ALU.add).then_inc(X[i % 2].drained, 1)
                ve.wait_ge(X[i % 2].drained, X[i % 2].at(('qk', i)))
                m = min(n, 2 * P)
                tt(L[:, n - m:n], L[:, n - m:n], g.bias_near[:, h, 2 * P - m:2 * P], ALU.add).then_inc(
                        vec_steps.sem, vec_steps.next())
                ve.wait_ge(vec_steps.sem, vec_steps.count)
                ve.tensor_reduce(g.stat[:, 4 + i % 2:5 + i % 2], L[:, 0:n], AX.X, ALU.max, negate=True).then_inc(
                        vec_out.sem, vec_out.next(('nmax', i)))
                ve.wait_ge(vec_out.sem, vec_out.count)
            if i:
                j = i - 1
                n = (steps[j][0] + 1) * P
                ve.wait_ge(act_out.sem, act_out.at(('exp', j)))
                r = g.stat[:, 10 + j % 2:11 + j % 2]
                ve.reciprocal(r, g.stat[:, 6 + j % 2:7 + j % 2]).then_inc(vec_steps.sem, vec_steps.next())
                ve.wait_ge(vec_steps.sem, vec_steps.count)
                ts(g.prob[j % 2][:, 0:n], g.prob[j % 2][:, 0:n], r, None, ALU.mult).then_inc(
                        vec_out.sem, vec_out.next(('prob', j)))
                ve.wait_ge(vec_out.sem, vec_out.count)

        ve.wait_ge(PJ[1].drained, PJ[1].at(('ao', 3)))
        ve.wait_ge(st_kv.sem, st_kv.at('v'))
        ve.wait_ge(st_k[0].sem, st_k[0].at(4))
        ve.wait_ge(st_k[1].sem, st_k[1].at(3))

        def odd_page(i):
            ve.wait_ge(X[1].filled, X[1].at(('sk', i)))
            ve.tensor_copy(g.kT[1][:, :], X[1].ap[:, :]).then_inc(X[1].drained, 1)
            ve.wait_ge(X[1].drained, X[1].at(('sk', i)))

        ve.memset(g.d_pad[0][:, 0:3], 0.0).then_inc(vec_steps.sem, vec_steps.next())
        ve.wait_ge(vec_steps.sem, vec_steps.count)
        ve.memset(g.d_pad[1][:, 0:3], 0.0).then_inc(vec_out.sem, vec_out.next('d_pads'))
        ve.wait_ge(vec_out.sem, vec_out.count)
        for t in range(12):
            odd_page(4 * t + 1)
            odd_page(4 * t + 3)
            ve.wait_ge(act_out.sem, act_out.at(('pad', t)))
            if t >= 2:
                ve.wait_ge(act_out.sem, act_out.at(('silu', t - 2)))
            src, y = g.d_pad[t % 2], g.d_conv[t % 2][:, 0:DW - 3]
            ts(y, src[:, 0:DW - 3], par('dc', t), None, ALU.mult).then_inc(vec_steps.sem, vec_steps.next())
            ve.wait_ge(vec_steps.sem, vec_steps.count)
            for i in range(1, 4):
                stt(y, src[:, i:i + DW - 3], par('dc', i * 12 + t), y, ALU.mult, ALU.add).then_inc(
                        vec_out.sem, vec_out.next(('conv', t) if i == 3 else None))
                ve.wait_ge(vec_out.sem, vec_out.count)
        for t in range(12, 16):
            odd_page(4 * t + 1)
            odd_page(4 * t + 3)
        ve.wait_ge(X[0].drained, X[0].at(('srep', 2)))
        ve.wait_ge(X[1].drained, X[1].at(('srep', 1)))
        L = g.s_log
        for q in range(2):
            ve.wait_ge(X[2 + q].filled, X[2 + q].at(('slog', q)))
            x = X[2 + q].ap
            tt(L[:, q * 512:q * 512 + 512], L[:, q * 512:q * 512 + 512], x[:, :], ALU.add).then_inc(
                    X[2 + q].drained, 1)
            ve.wait_ge(X[2 + q].drained, X[2 + q].at(('slog', q)))
        ve.wait_ge(X[1].filled, X[1].at('snew'))
        x = X[1].ap
        tt(L[:, PAST:NEWK], L[:, PAST:NEWK], x[:, 0:NS], ALU.add).then_inc(X[1].drained, 1)
        ve.wait_ge(X[1].drained, X[1].at('snew'))
        tt(L[:, PAST - P:NEWK], L[:, PAST - P:NEWK], g.bias_s[:, :], ALU.add).then_inc(
                vec_steps.sem, vec_steps.next())
        ve.wait_ge(vec_steps.sem, vec_steps.count)
        ve.tensor_reduce(g.stat[:, 8:9], L[:, :], AX.X, ALU.max, negate=True).then_inc(
                vec_out.sem, vec_out.next('s_nmax'))
        ve.wait_ge(vec_out.sem, vec_out.count)
        tt(gTmp, g.small[:, :, 4:8], g.lrow[:, 1, :].unsqueeze(1).to_broadcast([P, 5, H]), ALU.add).then_inc(
                vec_out.sem, vec_out.next('g_arg'))
        ve.wait_ge(vec_out.sem, vec_out.count)
        ve.wait_ge(act_out.sem, act_out.at('conv_done'))
        stt(gTmp, gTmp, 0.0, gA, ALU.max, ALU.add).then_inc(vec_steps.sem, vec_steps.next())
        ve.wait_ge(vec_steps.sem, vec_steps.count)
        stt(gG, gTmp, -1.0, g.gate[:, 7, 0, :].unsqueeze(1).to_broadcast([P, 5, H]), ALU.mult, ALU.mult).then_inc(
                vec_out.sem, vec_out.next('g'))
        ve.wait_ge(vec_out.sem, vec_out.count)
        for t in range(8):
            if t == 4:
                ve.wait_ge(act_out.sem, act_out.at('s_exp'))
                ve.reciprocal(g.stat[:, 12:13], g.stat[:, 9:10]).then_inc(vec_steps.sem, vec_steps.next())
                ve.wait_ge(vec_steps.sem, vec_steps.count)
                ts(L[:, :], L[:, :], g.stat[:, 12:13], None, ALU.mult).then_inc(vec_out.sem, vec_out.next('s_prob'))
                ve.wait_ge(vec_out.sem, vec_out.count)
            ve.wait_ge(act_out.sem, act_out.at(('l2rs', t)))
            q = g.qkv[:, t, :]
            stt(q, q, SCALE if t < 4 else 1.0, g.d_rs, ALU.mult, ALU.mult).then_inc(
                    vec_out.sem, vec_out.next(('l2', t)))
            ve.wait_ge(vec_out.sem, vec_out.count)
        ve.wait_ge(act_out.sem, act_out.at('gexp'))
        ve.wait_ge(X[0].filled, X[0].at('spT_new'))
        stt(gBE[:, 0:4, :], gBE[:, 0:4, :], -1.0, gBeta[:, 0:4, :], ALU.mult, ALU.mult).then_inc(
                vec_steps.sem, vec_steps.next())
        ve.wait_ge(vec_steps.sem, vec_steps.count)
        stt(gBE[0:NS, 4, :], gBE[0:NS, 4, :], -1.0, gBeta[0:NS, 4, :], ALU.mult, ALU.mult).then_inc(
                vec_steps.sem, vec_steps.next())
        ve.wait_ge(vec_steps.sem, vec_steps.count)
        ve.memset(g.d_S[:, :], 0.0).then_inc(vec_steps.sem, vec_steps.next())
        ve.wait_ge(vec_steps.sem, vec_steps.count)
        for c in range(5):
            cs, n = chunk_of(c)
            tri = const('triu') if c < 4 else const('triu_s', NS)[:, 0:NS]
            ve.wait_ge(X[0].filled, X[0].at(('grow', c)))
            x = X[0].ap
            for h in range(H):
                ts(g.d_dec[0:n, h * n:h * n + n], x[0:n, h * n:h * n + n], gC[0:n, c, h:h + 1], 0.0,
                        ALU.subtract, ALU.min).then_inc(vec_out.sem, vec_out.next(('dif', c) if h == 3 else None))
                ve.wait_ge(vec_out.sem, vec_out.count)
            ve.wait_ge(act_out.sem, act_out.at(('dec', c)))
            dec = head_view(g.d_dec[0:n, :], n)
            tt(dec, dec, over_heads(tri), ALU.mult).then_inc(vec_steps.sem, vec_steps.next())
            ve.wait_ge(vec_steps.sem, vec_steps.count)
            mt = g.d_mt[0:n, 0:4 * n]
            ve.wait_ge(X[2].filled, X[2].at(('kk', c)))
            x = X[2].ap
            tt(mt, g.d_dec[0:n, 0:4 * n], x[0:n, 0:4 * n], ALU.mult).then_inc(X[2].drained, 1)
            ve.wait_ge(X[2].drained, X[2].at(('kk', c)))
            ve.wait_ge(X[1].filled, X[1].at(('betarow', c)))
            x = X[1].ap
            tt(mt, mt, x[0:n, 0:4 * n], ALU.mult).then_inc(X[1].drained, 1)
            ve.wait_ge(X[1].drained, X[1].at(('betarow', c)))
            ve.wait_ge(X[3].filled, X[3].at(('kq', c)))
            x = X[3].ap
            tt(g.d_dec[0:n, 0:4 * n], g.d_dec[0:n, 0:4 * n], x[0:n, 0:4 * n], ALU.mult).then_inc(X[3].drained, 1)
            ve.wait_ge(X[3].drained, X[3].at(('kq', c)))
            ve.wait_ge(X[0].filled, X[0].at(('dkT', c)))
            x = X[0].ap
            tt(head_view(g.d_kd[0:n, :], P), head_view(x[0:n, :], P), bcast(gEK[0:n, c, :], P), ALU.mult).then_inc(
                    vec_steps.sem, vec_steps.next())
            ve.wait_ge(vec_steps.sem, vec_steps.count)
            tt(head_view(g.d_kb[0:n, :], P), head_view(x[0:n, :], P), bcast(gBE[0:n, c, :], P), ALU.mult).then_inc(
                    X[0].drained, 1)
            ve.wait_ge(X[0].drained, X[0].at(('dkT', c)))
            ve.wait_ge(X[1].filled, X[1].at(('dvT', c)))
            x = X[1].ap
            tt(head_view(g.d_vb[0:n, :], P), head_view(x[0:n, :], P), bcast(gBeta[0:n, c, :], P), ALU.mult).then_inc(
                    X[1].drained, 1)
            ve.wait_ge(X[1].drained, X[1].at(('dvT', c)))
            t_, tT = g.d_t[0:n, 0:4 * n], g.d_tt[0:n, 0:4 * n]
            for y in (t_, tT):
                ve.tensor_copy(head_view(y, n), over_heads(ident[0:n, 0:n])).then_inc(vec_steps.sem, vec_steps.next())
                ve.wait_ge(vec_steps.sem, vec_steps.count)
            levels = LEVELS if c < 4 else LEVELS[:2]
            for li, s in enumerate(levels):
                lv = const('level', n)[:, li * P:li * P + n]
                tt(head_view(g.d_lm[0:n, :], n), head_view(mt, n), over_heads(lv), ALU.mult).then_inc(
                        vec_out.sem, vec_out.next(('lm', c, s)))
                ve.wait_ge(vec_out.sem, vec_out.count)
                if s != levels[-1]:
                    ve.wait_ge(X[3].filled, X[3].at(('TY', c, s)))
                    x = X[3].ap
                    tt(t_, t_, x[0:n, 0:4 * n], ALU.subtract).then_inc(X[3].drained, 1)
                    ve.wait_ge(X[3].drained, X[3].at(('TY', c, s)))
                ve.wait_ge(X[0].filled, X[0].at(('YT', c, s)))
                x = X[0].ap
                tt(tT, tT, x[0:n, 0:4 * n], ALU.subtract).then_inc(X[0].drained, 1)
                ve.wait_ge(X[0].drained, X[0].at(('YT', c, s)))
            ve.wait_ge(X[1].drained, X[1].at(('kc', c)))
            tt(head_view(g.d_qd, n), g.qkv[:, 0:4, cs], head_view(g.d_eg, n), ALU.mult).then_inc(
                    vec_out.sem, vec_out.next(('qd', c)))
            ve.wait_ge(vec_out.sem, vec_out.count)
            if c < 4:
                ve.wait_ge(X[0].filled, X[0].at(('dS', c)))
                x = X[0].ap
                for h in range(H):
                    hs = slice(h * P, h * P + P)
                    ins = stt(g.d_S[:, hs], g.d_S[:, hs], g.d_eg[:, h * P + P - 1:h * P + P], x[:, hs],
                              ALU.mult, ALU.add)
                    if h < H - 1:
                        ins.then_inc(vec_steps.sem, vec_steps.next())
                        ve.wait_ge(vec_steps.sem, vec_steps.count)
                    else:
                        ins.then_inc(X[0].drained, 1)
                        ve.wait_ge(X[0].drained, X[0].at(('dS', c)))
                ve.engine_nop().then_inc(vec_out.sem, vec_out.next(('d_state', c)))
                ve.wait_ge(vec_out.sem, vec_out.count)
            else:
                ve.wait_ge(X[1].drained, X[1].at('dwT'))
                ve.wait_ge(PJ[0].filled, PJ[0].at('so'))
                for b in range(DB):
                    if b:
                        ve.wait_ge(X[(b - 1) % 2].filled, X[(b - 1) % 2].at(('dS', c, b - 1)))
                    ts(g.d_kdm, g.d_kd[0:NS, :], const('seq_of', NS)[:, b:b + 1], None, ALU.mult).then_inc(
                            vec_out.sem, vec_out.next(('dkdm', b)))
                    ve.wait_ge(vec_out.sem, vec_out.count)
                    if b:
                        ve.wait_ge(st_ss[1].sem, st_ss[1].at(b - 1))
                    ve.wait_ge(ds_in[b % 2].sem, ds_in[b % 2].at(DB + b))
                    ve.wait_ge(X[b % 2].filled, X[b % 2].at(('dS', c, b)))
                    x = X[b % 2].ap
                    for h in range(H):
                        hs = slice(h * P, h * P + P)
                        e = h * NS + b * DS + DS - 1
                        ins = stt(g.d_sout[:, hs], g.d_sin[b % 2][:, hs], g.d_eg[:, e:e + 1], x[:, hs],
                                  ALU.mult, ALU.add)
                        if h < H - 1:
                            ins.then_inc(vec_steps.sem, vec_steps.next())
                            ve.wait_ge(vec_steps.sem, vec_steps.count)
                        else:
                            ins.then_inc(X[b % 2].drained, 1)
                            ve.wait_ge(X[b % 2].drained, X[b % 2].at(('dS', c, b)))
                    ve.engine_nop().then_inc(vec_out.sem, vec_out.next(('ds', DB + b)))
                    ve.wait_ge(vec_out.sem, vec_out.count)
        for h in range(H):
            ve.wait_ge(act_out.sem, act_out.at(('drs', h)))
            o = g.qkv[:, 8 + h, :]
            stt(o, o, par('dnn'), g.d_rs, ALU.mult, ALU.mult).then_inc(vec_steps.sem, vec_steps.next())
            ve.wait_ge(vec_steps.sem, vec_steps.count)
            tt(g.out_dn[:, h, :], g.out_dn[:, h, :], o, ALU.mult).then_inc(vec_out.sem, vec_out.next(('dout', h)))
            ve.wait_ge(vec_out.sem, vec_out.count)

        outs = (g.out_dn, g.out_ret, g.out_att)

        def bsplit(n):
            ve.wait_ge(act_out.sem, act_out.at(('bsplit', n)))
            tt(g.blo[n % 2][:, :, :], outs[n][:, :, :], g.bhi[n % 2][:, :, :].bitcast(F32), ALU.subtract).then_inc(
                    vec_out.sem, vec_out.next(('bsplit', n)))
            ve.wait_ge(vec_out.sem, vec_out.count)
        bsplit(0)
        bsplit(1)
        i = 0
        for n in range(3):
            if n == 1:
                bsplit(2)
            for d in range(4):
                for j in range(2):
                    k = 2 * d + j
                    ve.wait_ge(PJ[0].drained, PJ[0].at(('gate', n, d, j)))
                    ve.wait_ge(PJ[1].filled, PJ[1].at(('br', n, d, j)))
                    x = PJ[1].ap
                    s = g.sig[i % 2]
                    dst = g.m[:, k, :] if n == 0 else s[:, :]
                    tt(halves(dst), halves(s[:, :]), x[:, :, 0:HT], ALU.mult).then_inc(PJ[1].drained, 1)
                    ve.wait_ge(PJ[1].drained, PJ[1].at(('br', n, d, j)))
                    if n:
                        tt(g.m[:, k, :], g.m[:, k, :], s[:, :], ALU.add).then_inc(
                                vec_out.sem, vec_out.next(('mul', i)))
                        ve.wait_ge(vec_out.sem, vec_out.count)
                    else:
                        ve.engine_nop().then_inc(vec_out.sem, vec_out.next(('mul', i)))
                        ve.wait_ge(vec_out.sem, vec_out.count)
                    if n == 2:
                        ve.engine_nop().then_inc(vec_out.sem, vec_out.next(('m', k)))
                        ve.wait_ge(vec_out.sem, vec_out.count)
                    i += 1
        for k in range(KD):
            ve.wait_ge(act_out.sem, act_out.at(('msplit', k)))
            tt(g.ulo[:, k, :], g.m[:, k, :], g.uhi[:, k, :].bitcast(F32), ALU.subtract).then_inc(
                    vec_out.sem, vec_out.next(('msplit', k)))
            ve.wait_ge(vec_out.sem, vec_out.count)
        ve.wait_ge(x_in.sem, x_in.at('again'))
        for k in range(KD):
            ve.wait_ge(PJ[k % 2].filled, PJ[k % 2].at(('wo', k)))
            x = PJ[k % 2].ap
            tt(halves(g.x[:, k, :]), halves(g.x[:, k, :]), x[:, :, 0:HT], ALU.add).then_inc(PJ[k % 2].drained, 1)
            ve.wait_ge(PJ[k % 2].drained, PJ[k % 2].at(('wo', k)))
            ve.engine_nop().then_inc(vec_out.sem, vec_out.next(('h', k)))
            ve.wait_ge(vec_out.sem, vec_out.count)
        ve.wait_ge(act_out.sem, act_out.at('rstd1'))
        for k in range(KD + 1):
            if k < KD:
                stt(g.f_conv[k % 2][:, 0:NT], g.x[:, k, :], par('ffn', k), g.f_act[:, :], ALU.mult, ALU.mult).then_inc(
                        vec_out.sem, vec_out.next(('hf', k)))
                ve.wait_ge(vec_out.sem, vec_out.count)
            if k:
                j = k - 1
                ve.wait_ge(act_out.sem, act_out.at(('hh', j)))
                tt(g.ulo[:, j, :], g.f_conv[j % 2][:, 0:NT], g.uhi[:, j, :].bitcast(F32), ALU.subtract).then_inc(
                        vec_out.sem, vec_out.next(('hn', j)))
                ve.wait_ge(vec_out.sem, vec_out.count)
        ve.memset(g.f_pad[0][:, 0:2], 0.0).then_inc(vec_steps.sem, vec_steps.next())
        ve.wait_ge(vec_steps.sem, vec_steps.count)
        ve.memset(g.f_pad[1][:, 0:2], 0.0).then_inc(vec_out.sem, vec_out.next('f_pads'))
        ve.wait_ge(vec_out.sem, vec_out.count)

        for f in range(2):
            for j in range(FH):
                for i in range(2):
                    ve.wait_ge(act_out.sem, act_out.at(('fpad', f, j, i)))
                    src, y, t = g.f_pad[i], g.f_conv[i][:, 0:SW - 2], f * FH + j + i * FT
                    ts(y, src[:, 0:SW - 2], par('f0', t), None, ALU.mult).then_inc(vec_steps.sem, vec_steps.next())
                    ve.wait_ge(vec_steps.sem, vec_steps.count)
                    stt(y, src[:, 1:SW - 1], par('f0', 2 * FT + t), y, ALU.mult, ALU.add).then_inc(
                            vec_steps.sem, vec_steps.next())
                    ve.wait_ge(vec_steps.sem, vec_steps.count)
                    stt(y, src[:, 2:SW], par('f2', t), y, ALU.mult, ALU.add).then_inc(
                            vec_out.sem, vec_out.next(('fconv', f, j, i)))
                    ve.wait_ge(vec_out.sem, vec_out.count)
                ve.wait_ge(act_out.sem, act_out.at(('fsilu', f, j)))
                y = g.f_conv[1]
                tt(g.f_act[:, 0:SEQ], g.f_act[:, 0:SEQ], y[:, 0:SEQ], ALU.mult).then_inc(
                        vec_steps.sem, vec_steps.next())
                ve.wait_ge(vec_steps.sem, vec_steps.count)
                fs = g.f_act[:, SEQ:NT].rearrange("p (b t) -> p b t", b=DB)
                tt(fs, fs, y[:, 514:514 + 48].rearrange("p (b t) -> p b t", b=DB)[:, :, 0:4], ALU.mult).then_inc(
                        vec_out.sem, vec_out.next(('hprod', f, j)))
                ve.wait_ge(vec_out.sem, vec_out.count)
                ve.wait_ge(act_out.sem, act_out.at(('hhi', f, j)))
                tt(g.hlo[:, j, :], g.f_act[:, :], g.hhi[:, j, :].bitcast(F32), ALU.subtract).then_inc(
                        vec_out.sem, vec_out.next(('hff', f, j)))
                ve.wait_ge(vec_out.sem, vec_out.count)
            for c in range(KD):
                ve.wait_ge(PJ[c % 2].filled, PJ[c % 2].at(('down', f, c)))
                x = PJ[c % 2].ap
                tt(halves(g.x[:, c, :]), halves(g.x[:, c, :]), x[:, :, 0:HT], ALU.add).then_inc(PJ[c % 2].drained, 1)
                ve.wait_ge(PJ[c % 2].drained, PJ[c % 2].at(('down', f, c)))
        ve.engine_nop().then_inc(vec_out.sem, vec_out.next('x_final'))
        ve.wait_ge(vec_out.sem, vec_out.count)


def final(g):
    nc, io = g.nc, g.io
    ones, ident = g.const('ones'), g.const('ident')
    x_in, made, normed, squares = (g.counter(n) for n in ("fin_x", "fin_act", "fin_vec", "fin_pe"))
    stored = [g.counter(f"fin_stored{i}") for i in range(2)]
    PJ, X = g.PJ, g.X
    with nc.Block() as block:
        @block.sync
        def _(sp):
            sp.dma_start(flat(g.xload[:, :, :]), g.scratch_x).then_inc(x_in.sem, x_in.next('x', 16))
            for c in range(5):
                sp.wait_ge(made.sem, made.at(('y', c)))
                if c < 4:
                    dst = io['y_prompt'].rearrange("a (c p) n -> (a c) p n", p=P)[c]
                else:
                    dst = io['y_sample'].rearrange("b t n -> (b t) n")
                sp.dma_start(dst, g.ytok[c % 2][0:P if c < 4 else NS, :]).then_inc(
                        stored[c % 2].sem, stored[c % 2].next(c, 16))
            sp.wait_ge(stored[0].sem, stored[0].at(4))
            sp.wait_ge(stored[1].sem, stored[1].at(3))

        @block.scalar
        def _(ac):
            ac.wait_ge(x_in.sem, x_in.at('x'))
            for k in range(KD):
                if k >= 2:
                    ac.wait_ge(squares.sem, squares.at(k - 2))
                ac.activation(g.xsq[k % 2][:, :], g.xload[:, k, :], ACT.Square).then_inc(
                        made.sem, made.next(('sq', k)))
                ac.wait_ge(made.sem, made.count)
            ac.wait_ge(PJ[0].filled, PJ[0].at('rms_fin'))
            x = PJ[0].ap
            ac.activation(halves(g.rstd0[:, :]), x[:, :, 0:HT], ACT.Ln, scale=1.0 / D, bias=g.eps()).then_inc(
                    PJ[0].drained, 1)
            ac.wait_ge(PJ[0].drained, PJ[0].at('rms_fin'))
            ac.activation(g.rstd0[:, :], g.rstd0[:, :], ACT.Exp, scale=-0.5).then_inc(made.sem, made.next('rstd'))
            ac.wait_ge(made.sem, made.count)
            for c in range(5):
                n = P if c < 4 else NS
                if c >= 2:
                    ac.wait_ge(stored[c % 2].sem, stored[c % 2].at(c - 2))
                for half in range(2):
                    b = X[half]
                    ac.wait_ge(b.filled, b.at(('y', c, half)))
                    x = b.ap
                    ac.activation(g.ytok[c % 2][0:n, half * 512:half * 512 + 512], x[0:n, :], ACT.Copy).then_inc(
                            b.drained, 1)
                    ac.wait_ge(b.drained, b.at(('y', c, half)))
                ac.activation(g.stat[:, 0:1], g.eps(), ACT.Copy).then_inc(made.sem, made.next(('y', c)))
                ac.wait_ge(made.sem, made.count)

        @block.vector
        def _(ve):
            ve.wait_ge(made.sem, made.at('rstd'))
            for k in range(KD):
                gain = g.par[:, PAR0_N + PAR1['fin'] + k:PAR0_N + PAR1['fin'] + k + 1]
                ve.scalar_tensor_tensor(g.xload[:, k, :], g.xload[:, k, :], gain, g.rstd0[:, :], ALU.mult, ALU.mult).then_inc(
                        normed.sem, normed.next(k))
                ve.wait_ge(normed.sem, normed.count)

        @block.tensor
        def _(pe):
            pe.wait_ge(PJ[0].drained, PJ[0].claim('rms_fin'))
            out = PJ[0].ap
            for k in range(KD):
                pe.wait_ge(made.sem, made.at(('sq', k)))
                for half in range(2):
                    mm = pe.matmul(out[:, half, 0:HT], ones, g.xsq[k % 2][:, half * HT:half * HT + HT],
                                   start=(k == 0), stop=(k == KD - 1))
                if k < KD - 1:
                    mm.then_inc(squares.sem, squares.next(k))
            mm.then_inc(PJ[0].filled, 1)
            pe.wait_ge(normed.sem, normed.at(KD - 1))
            for c in range(5):
                cs, n = chunk_of(c)
                for half in range(2):
                    pe.wait_ge(X[half].drained, X[half].claim(('y', c, half)))
                    x = X[half].ap
                    for k in range(4):
                        mm = pe.transpose(x[0:n, k * P:k * P + P], g.xload[:, half * 4 + k, cs], ident)
                    mm.then_inc(X[half].filled, 1)


def build(nc, io, consts, onehots, scratch_x, scratch_b, layout, onehot_at, known):
    g = Program(nc, io, consts, onehots, scratch_x, scratch_b, known)
    with g.ctx:
        allocate(g, layout)
        setup(g, onehot_at)
        g.clear_semaphores()
        for s in g.learn.made.values():
            s.fresh()
        with nc.Fori(0, DEPTH) as layer:
            with nc.Block() as g.block:
                layer_program(g, layer)
            g.clear_semaphores()
        for s in g.learn.made.values():
            s.fresh()
        final(g)
    return g.learn.learned()



def packed(arrays, rows):
    at, o = {}, 0
    for k, v in arrays.items():
        at[k] = (o, v.shape[1])
        o += v.shape[1]
    at['_n'] = o
    return np.concatenate([v[0:rows] for v in arrays.values()], 1), at


def kernel(**inputs):
    from concourse import bacc
    from concourse.bass_utils import run_bass_kernel_spmd

    consts, layout = packed(const_arrays(), P)
    onehots, onehot_at = packed(onehot_arrays(), NBUCKET)
    arrays = {f"in_{n}": np.ascontiguousarray(inputs[n]) for n in IN_NAMES}
    arrays["in_consts"], arrays["in_onehots"] = consts, onehots

    def program(known):
        nc = bacc.Bacc("TRN2", target_bir_lowering=False, num_devices=1)
        dram = {n: nc.dram_tensor(n, a.shape, mybir.dt.from_np(a.dtype), kind="ExternalInput").ap()
                for n, a in arrays.items()}
        io = {n: dram[f"in_{n}"] for n in IN_NAMES}
        for n, shape in OUT_SHAPES:
            io[n] = nc.dram_tensor(f"out_{n}", shape, F32, kind="ExternalOutput").ap()
        scratch_x = nc.dram_tensor("scratch_x", (P, KD * NT), F32, kind="Internal").ap()
        scratch_b = nc.dram_tensor("scratch_b", (P * H * 383,), F32, kind="Internal").ap()
        return nc, build(nc, io, dram["in_consts"], dram["in_onehots"], scratch_x, scratch_b, layout, onehot_at, known)

    _, counted = program(Known())
    nc, _ = program(counted)
    r = run_bass_kernel_spmd(nc, [arrays], core_ids=[0])
    return tuple(r.results[0][f"out_{n}"] for n, _ in OUT_SHAPES)
```

```python
from contextlib import ExitStack

import numpy as np

import concourse.bass as bass
from concourse import mybir

F32 = mybir.dt.float32
F32R = mybir.dt.float32r
I32 = mybir.dt.int32
ALU = mybir.AluOpType
ACT = mybir.ActivationFunctionType
AX = mybir.AxisListType

P = 128
D = 1024
KD = D // P
SEQ, DB, DS = 512, 8, 4
NS = DB * DS
NT = SEQ + NS
HT = NT // 2
DEPTH = 2
H = 4
PAST, PAGE = 1024, 128
NPG = PAST // PAGE
NEWK = PAST + NS
DFF = 2816
FT = DFF // P
FH = FT // 2
NBUCKET = 32
TOPK_P, TOPK_S = 128, 256
EPS = 1e-6
SCALE = float(P) ** -0.5
NEG, TAKEN = -1.0e30, -3.0e38
DW, SW = 515 + DB * 7, 514 + DB * 6
COL = {}
_o = 0
for _n, _w in (('dn', 1536), ('z', 512), ('b', 4), ('a', 4), ('rq', 512), ('rk', 512), ('rv', 512), ('rg', 512),
               ('aq', 512), ('ak', 512), ('av', 512), ('iq', 256), ('ik', 64), ('iw', 4), ('gate', 3072)):
    COL[_n] = _o
    _o += _w



def bucket(d):
    d = np.asarray(d)
    f = np.maximum(d.astype(np.float32), np.float32(1.0)) / np.float32(16)
    large = 16 + (np.log(f) / np.float32(np.log(128 / 16)) * np.float32(16)).astype(np.int32)
    return np.where(d < 16, d, np.minimum(large, 31))


def one_hot(d):
    return ((bucket(np.maximum(d, 0))[None] == np.arange(NBUCKET)[:, None]) & (d >= 0)[None]).astype(np.float32)


def const_arrays():
    a = {}
    i, j = np.arange(P)[None, :], np.arange(P)[:, None]
    a['ident'] = (i == j)
    a['triu'] = (i >= j)
    a['level'] = np.concatenate([(i // (2 * s) == j // (2 * s)) & (i // s % 2 == 1) & (j // s % 2 == 0)
                                 for s in (1, 2, 4, 8, 16, 32, 64)], 1)
    a['causal'] = np.where(i > j, NEG, 0.0)
    lg = np.log1p(-np.exp2(-5.0 - np.arange(H)))
    a['r_decay'] = np.concatenate([np.where(i >= j, np.exp(lg[h] * np.maximum(i - j, 0)), 0.0) for h in range(H)], 1)
    a['r_q'] = np.concatenate([np.exp(lg[h] * (i + 1)) + 0.0 * j for h in range(H)], 1)
    a['r_k'] = np.exp(lg[None, :] * (P - 1 - j))
    s, t = np.arange(NS)[None, :], np.arange(NS)[:, None]
    same = (s // DS == t // DS)
    pad = lambda x: np.concatenate([x, np.zeros((P - x.shape[0], x.shape[1]))], 0)
    a['rs_decay'] = pad(np.concatenate([np.where(same & (s >= t), np.exp(lg[h] * np.maximum(s - t, 0)), 0.0)
                                        for h in range(H)], 1))
    a['rs_q'] = np.concatenate([np.exp(lg[h] * (s % DS + 1)) + 0.0 * j for h in range(H)], 1)
    a['rs_k'] = pad(np.exp(lg[None, :] * (DS - 1 - t % DS)))
    a['seq_of'] = pad((t // DS == np.arange(DB)[None, :]))
    a['triu_s'] = pad(same & (s >= t))
    a['after'] = (j > i)
    a['after_s'] = pad(same & (t > s))
    a['eps'] = np.full((P, 1), EPS)
    a['rep'] = pad((i % NS == t))
    a['causal_s'] = pad(np.where(same & (s <= t), 0.0, NEG))
    a['ones'] = np.ones((P, P))
    pos = np.concatenate([np.arange(SEQ), PAST + np.arange(NS) % DS]).astype(np.float32)
    inv = (np.float32(1.0) / (np.float32(10000.0) ** np.linspace(0.0, 1.0, 64, dtype=np.float32))).astype(np.float32)
    ang = inv[:, None] * pos[None, :]
    a['cos'] = np.concatenate([np.cos(ang)] * 2, 0)
    a['sin'] = np.concatenate([-np.sin(ang), np.sin(ang)], 0)
    return {k: np.asarray(v, np.float32) for k, v in a.items()}


def onehot_arrays():
    a = {'oh': one_hot(255 - np.arange(384))}
    c = np.arange(P)
    n = np.arange(NS)
    for t in range(DS):
        a[f'oh{t}'] = np.concatenate([one_hot(P + t - c), one_hot(t - n % DS)], 1)
        a[f'row{t}'] = np.broadcast_to((np.arange(P) % DS == t), (NBUCKET, P))
    return {k: np.asarray(v, np.float32) for k, v in a.items()}


class Counter:

    def __init__(self, sem, known):
        self.sem, self.known, self.count, self.values = sem, known, 0, {}

    def fresh(self):
        self.count = 0

    def next(self, key=None, by=1):
        self.count += by
        if key is not None:
            assert key not in self.values, key
            self.values[key] = self.count
        return by

    def at(self, key):
        return self.known[key] if self.known is not None else 1


class Bank:

    def __init__(self, ap, filled, drained, known):
        self.ap, self.filled, self.drained, self.known = ap, filled, drained, known
        self.uses, self.values = 0, {}

    def fresh(self):
        self.uses = 0

    def claim(self, key):
        assert key not in self.values, key
        self.uses += 1
        self.values[key] = self.uses
        return self.uses - 1

    def at(self, key):
        return self.known[key] if self.known is not None else 1


class Known:

    def __init__(self):
        self.tables = None
        self.made = {}

    def table(self, name):
        return None if self.tables is None else self.tables[name]

    def learned(self):
        k = Known()
        k.tables = {n: dict(s.values) for n, s in self.made.items()}
        return k


IN_NAMES = ['x_prompt', 'x_sample', 'cache_k', 'cache_v', 'cache_kidx', 'state_dn_conv', 'state_dn', 'state_ret',
            'state_ffn_conv', 'page_table', 'norm_mix', 'w_in', 'dn_conv_w', 'dn_a_log', 'dn_dt_bias', 'dn_norm',
            'ret_norm', 'rel_bias', 'w_branch', 'w_o', 'norm_ffn', 'w_up', 'ffn_conv_w', 'w_down', 'norm_final']
OUT_SHAPES = [
    ('y_prompt', (1, SEQ, D)), ('y_sample', (DB, DS, D)),
    ('p_dn_conv', (DEPTH, 1, 3, 1536)), ('p_dn', (DEPTH, 1, H, P, P)), ('p_ret', (DEPTH, 1, H, P, P)),
    ('p_k', (DEPTH, 1, SEQ, H, P)), ('p_v', (DEPTH, 1, SEQ, H, P)), ('p_kidx', (DEPTH, 1, SEQ, 64)),
    ('p_ffn_conv', (DEPTH, 1, 2, 2 * DFF)),
    ('s_dn_conv', (DEPTH, DB, 3, 1536)), ('s_dn', (DEPTH, DB, H, P, P)), ('s_ret', (DEPTH, DB, H, P, P)),
    ('s_k', (DEPTH, DB, DS, H, P)), ('s_v', (DEPTH, DB, DS, H, P)), ('s_kidx', (DEPTH, DB, DS, 64)),
    ('s_ffn_conv', (DEPTH, DB, 2, 2 * DFF))]

UNITS = ['iq', 'ik'] + [f'{n}{i}' for n in ('rq', 'rk', 'rv', 'rg', 'aq', 'z', 'ak', 'av') for i in range(2)] \
    + [f'dn{i}' for i in range(6)] \
    + [f'{w}{n}{d}' for n in range(3) for d in range(4) for w in ('gate', 'br')] \
    + [f'wo{i}' for i in range(4)] \
    + [x for f in range(2) for x in [f'up{f}_{j}' for j in range(FH)] + [f'down{f}_{c}' for c in range(KD)]]
UIDX = {u: i for i, u in enumerate(UNITS)}
NRAW, NSPLIT = 3, 3
TILES = []
for _u in UNITS:
    if _u.startswith('gate'):
        TILES += [(_u, 0), ('br' + _u[4:], 0), (_u, 1), ('br' + _u[4:], 1)]
    elif not _u.startswith('br'):
        TILES += [(_u, 0), (_u, 1)]
TIDX = {t: i for i, t in enumerate(TILES)}
UP_K = 6
KPAGES, VPAGES = 6, 4
NPAGES = DB * NPG
LAST = 2 * FT // 4
ROUNDS_S = TOPK_S // 8
LEVELS = (1, 2, 4, 8, 16, 32, 64)
PAR0 = dict(f0=0, f1=FT * 2, mix=FT * 4, ffn=FT * 4 + 8, dnn=FT * 4 + 16, retn=FT * 4 + 17)
PAR0_N = FT * 4 + 21
PAR1 = dict(f2=0, dc=FT * 2, fin=FT * 2 + 48)
PAR1_N = FT * 2 + 56


def flat(ap):
    return ap.rearrange("p a b -> p (a b)")


class Program:

    def __init__(self, nc, io, consts, onehots, scratch_x, scratch_b, known):
        self.nc, self.io, self.known, self.learn = nc, io, known, Known()
        self.scratch_x, self.scratch_b = scratch_x, scratch_b
        self.consts, self.onehots = consts, onehots
        self.ctx = ExitStack()
        self.sems = []

    def sb(self, name, shape, dt=F32, ctx=None):
        return (ctx or self.ctx).enter_context(self.nc.sbuf_tensor(name, shape, dt))

    def sem(self, name):
        s = self.ctx.enter_context(self.nc.semaphore(name))
        self.sems.append(s)
        return s

    def counter(self, name):
        s = Counter(self.sem(name), self.known.table(name))
        self.learn.made[name] = s
        return s

    def bank(self, name, ap):
        s = Bank(ap, self.sem(name + "_filled"), self.sem(name + "_drained"), self.known.table(name))
        self.learn.made[name] = s
        return s

    def eps(self):
        return self.const('eps')

    def clear_semaphores(self):
        self.nc.all_engine_barrier()
        for s in self.sems:
            self.nc.sync.sem_clear(s)
        self.nc.all_engine_barrier()


def allocate(g, layout):
    sb, c = g.sb, g.ctx
    g.C = sb("consts", [P, layout['_n']])
    g.const = lambda n, p=P: g.C[0:p, layout[n][0]:layout[n][0] + layout[n][1]]
    g.PJ = [g.bank(f"big{i}", c.enter_context(g.nc.psum_tensor(f"big{i}", [P, 2, 512], F32))) for i in range(2)]
    g.X = [g.bank(f"aux{i}", c.enter_context(g.nc.psum_tensor(f"aux{i}", [P, 512], F32))) for i in range(4)]
    g.bias_near = sb("bias_near", [P, H, 2 * P])
    g.bias_s = sb("bias_s", [P, P + NS])
    g.uhi, g.ulo = sb("uhi", [P, KD, NT], F32R), sb("ulo", [P, KD, NT], F32R)
    g.w_raw = [sb(f"w_raw{i}", [P, 2048]) for i in range(NRAW)]
    g.w_hi = [sb(f"w_hi{i}", [P, KD * P], F32R) for i in range(NSPLIT)]
    g.w_lo = [sb(f"w_lo{i}", [P, KD * P], F32R) for i in range(NSPLIT)]
    g.par = sb("par", [P, PAR0_N + PAR1_N])
    g.dn_prev, g.dn_last = sb("dn_prev", [P, 12, DB * 3]), sb("dn_last", [P, 12, 3 + DB * 3])
    g.ffn_prev, g.ffn_last = sb("ffn_prev", [P, 2 * FT, DB * 2]), sb("ffn_last", [P, 2 * FT, 2 + DB * 2])
    g.small = sb("small", [P, 5, 12])
    g.lrow = sb("lrow", [P, 2, H])
    g.gate = sb("gate", [P, 8, 5, H])
    g.stat = sb("stat", [P, 64])
    g.mx = sb("mx", [P, 8])
    g.ptab = sb("ptab", [1, DB * NPG], I32)
    g.x = sb("x", [P, KD, NT])
    with ExitStack() as r:
        g.xsq = [sb(f"xsq{i}", [P, NT], ctx=r) for i in range(2)]
        g.xsum = sb("xsum", [P, NT], ctx=r)
        g.par_rows = [sb(f"par_rows{i}", [P, P], ctx=r) for i in range(2)]
        g.dn_rows = sb("dn_rows", [DB * 3, 1536], ctx=r)
        g.ffn_rows = sb("ffn_rows", [DB * 2, 2 * DFF], ctx=r)
        g.rstd0 = sb("rstd0", [P, NT], ctx=r)
        g.ytok = [sb(f"ytok{i}", [P, D], ctx=r) for i in range(2)]
    with ExitStack() as r:
        g.oh_sb = sb("oh_sb", [NBUCKET, 384 + 4 * 160 + 4 * P], ctx=r)
        g.rb = sb("rb", [NBUCKET, 3, H], ctx=r)
        g.rbrow = sb("rbrow", [NBUCKET, 4, P], ctx=r)
        g.brow = sb("brow", [P, H, 383], ctx=r)
        g.xtok = sb("xtok", [P, 5, D], ctx=r)
    outs = c.enter_context(ExitStack())
    g.out_dn, g.out_ret = g.x[:, 0:H, :], g.x[:, H:2 * H, :]
    g.out_att = sb("out_att", [P, H, NT], ctx=outs)
    att = c.enter_context(ExitStack())
    g.s_pT = sb("s_pT", [P, NPG + 1, P], ctx=att)
    g.sel_s = flat(g.s_pT[0:NS, :, :])[:, 0:NEWK]
    g.s_ak = sb("s_ak", [P, H, NS], ctx=att)
    g.s_v = sb("s_v", [NS, 512], ctx=att)
    sel = c.enter_context(ExitStack())
    g.sel = sb("sel", [P, 128 + 256 + 384 + 512], ctx=sel)
    g.selat = [0, 128, 384, 768]
    with ExitStack() as r:
        g.rqk = sb("rqk", [P, 8, NT], ctx=r)
        g.rv = sb("rv", [P, H, NT], ctx=r)
        g.rraw = sb("rraw", [P, NT], ctx=r)
        g.rswap = sb("rswap", [P, NT], ctx=r)
        with ExitStack() as r2:
            g.iq, g.ik = sb("iq", [P, 2, NT], ctx=r2), sb("ik", [P, NT], ctx=r2)
            g.iqs = sb("iqs", [64, H, NS], ctx=r2)
            g.kidx = [sb(f"kidx{i}", [P, NPG, 64], ctx=r2) for i in range(2)]
            g.kidxT = sb("kidxT", [64, PAST], ctx=r2)
            g.wrow = sb("wrow", [P, DB, H * DS], ctx=r2)
            g.relu_p = [sb(f"relu_p{i}", [P, 512], ctx=r2) for i in range(2)]
            g.sprod = sb("sprod", [P, NPG, H * DS], ctx=r2)
            g.scoreT = sb("scoreT", [P, NPG, NS], ctx=r2)
            g.relu_s = sb("relu_s", [NS, H * NS], ctx=r2)
            g.smallT = sb("smallT", [12, NT], ctx=r2)
            g.kidx_tok = sb("kidx_tok", [P, 5, 64], ctx=r2)
        g.r_kd, g.r_v, g.r_qk, g.r_qd, g.r_S = (sb(f"r_{n}", [P, 512], ctx=r) for n in ("kd", "v", "qk", "qd", "S"))
        g.r_sin = [sb(f"r_sin{i}", [P, 512], ctx=r) for i in range(2)]
    g.r_sout, g.r_kdm = [g.rraw[:, 0:512], g.r_S[:, :]], [g.rswap[0:NS, 0:512], g.r_qk[0:NS, :]]
    with ExitStack() as r:
        g.akv = sb("akv", [P, 8, NT], ctx=r)
        g.vtok = sb("vtok", [P, 5, 512], ctx=r)
        g.ktok = [sb(f"ktok{i}", [P, 512], ctx=r) for i in range(2)]
        g.logit = [sb(f"logit{i}", [P, 512], ctx=r) for i in range(2)]
        g.prob = [sb(f"prob{i}", [P, 512], ctx=r) for i in range(2)]
        g.probT = [sb(f"probT{i}", [P, 512], ctx=r) for i in range(2)]
    sel.close()
    with ExitStack() as r:
        g.qkv = sb("qkv", [P, 12, NT], ctx=r)
        g.d_pad = [sb(f"d_pad{i}", [P, DW], ctx=r) for i in range(2)]
        g.d_conv = [sb(f"d_conv{i}", [P, DW], ctx=r) for i in range(2)]
        with ExitStack() as r2:
            g.kpage = [sb(f"kpage{i}", [P, 512], ctx=r2) for i in range(KPAGES)]
            g.kT = [sb(f"kT{i}", [P, 512], ctx=r2) for i in range(2)]
            g.s_q = sb("s_q", [P, H, DB * (NS + DS)], ctx=r2)
            g.s_log = sb("s_log", [P, NEWK], ctx=r2)
        g.d_dec, g.d_eg, g.d_mt, g.d_lm, g.d_t, g.d_tt, g.d_y, g.d_kd, g.d_vb, g.d_kb, g.d_S = (
            sb("d_" + n, [P, 512], ctx=r) for n in ("dec", "eg", "mt", "lm", "t", "tt", "y", "kd", "vb", "kb", "S"))
    att.close()
    g.vpage = [t[:, 0:512] for t in (*g.d_conv, *g.d_pad)]
    g.d_kc, g.d_qd, g.d_w = g.d_mt, g.d_y, g.d_lm
    g.d_sq, g.d_rs = ([a[:, 0:NT], b[:, 0:NT]] for a, b in zip(g.d_pad, g.d_conv))
    g.s_o = [t[:, 0:512] for t in g.d_pad]
    g.s_new = flat(g.s_ak)
    g.d_sin = [g.d_pad[0][:, 0:512], g.d_pad[1][:, 0:512]]
    g.d_sout, g.d_kdm = [g.d_conv[0][:, 0:512], g.d_S[:, :]], [g.d_conv[1][0:NS, 0:512], g.d_kb[0:NS, :]]
    with ExitStack() as r:
        g.bhi = [sb(f"bhi{i}", [P, H, NT], F32R, ctx=r) for i in range(2)]
        g.blo = [sb(f"blo{i}", [P, H, NT], F32R, ctx=r) for i in range(2)]
        g.m = sb("m", [P, KD, NT], ctx=r)
        g.sig = [sb(f"sig{i}", [P, NT], ctx=r) for i in range(2)]
    outs.close()
    g.hhi, g.hlo = (sb(n, [P, FH, NT], F32R) for n in ("hhi", "hlo"))
    g.f_pad = [sb(f"f_pad{i}", [P, SW]) for i in range(2)]
    g.f_conv = [sb(f"f_conv{i}", [P, SW]) for i in range(2)]
    g.f_act = sb("f_act", [P, NT])
    g.f_sq, g.f_rs = g.f_pad[0][:, 0:NT], g.f_pad[1][:, 0:NT]


def setup(g, oh_at):
    nc, io = g.nc, g.io
    const, ident = g.const, g.const('ident')
    in_ready, steps_a, steps_v = (g.counter(n) for n in ("set_in", "set_act", "set_vec"))
    x_in, wr = g.counter("set_x"), g.counter("set_wr")
    oh = lambda n: g.oh_sb[:, oh_at[n][0]:oh_at[n][0] + oh_at[n][1]]
    with nc.Block() as block:
        @block.sync
        def _(sp):
            sp.dma_start(g.C[:, :], g.consts).then_inc(in_ready.sem, in_ready.next(by=16))
            sp.dma_start(g.oh_sb[:, :], g.onehots).then_inc(in_ready.sem, in_ready.next(by=16))
            sp.dma_start(g.rb[:, 0, :], io['rel_bias']).then_inc(in_ready.sem, in_ready.next(by=16))
            sp.dma_start(g.rb[:, 1, :], io['rel_bias'][31:32, :].to_broadcast([NBUCKET, H])).then_inc(
                    in_ready.sem, in_ready.next(by=16))
            sp.dma_start(g.ptab[:, :], io['page_table'].rearrange("b n -> (b n)").unsqueeze(0)).then_inc(
                    in_ready.sem, in_ready.next('all', 16))
            sp.dma_start(g.xtok[:, 0:4, :], io['x_prompt'].rearrange("a (c p) n -> p (a c) n", p=P)).then_inc(
                    x_in.sem, x_in.next(by=16))
            sp.dma_start(g.xtok[0:NS, 4, :], io['x_sample'].rearrange("b t n -> (b t) n")).then_inc(
                    x_in.sem, x_in.next('all', 16))
            sp.wait_ge(steps_a.sem, steps_a.at('brow'))
            sp.dma_start(g.scratch_b[0:P * H * 383].rearrange("(h p n) -> p h n", h=H, p=P), g.brow[:, :, :]).then_inc(
                    wr.sem, wr.next('brow', 16))
            sp.wait_ge(wr.sem, wr.at('brow'))
            for h in range(H):
                src = bass.AP(g.scratch_b.tensor, h * P * 383 + 127, [[382, P], [1, 2 * P]])
                sp.dma_start(g.bias_near[:, h, :], src).then_inc(wr.sem, wr.next(by=16))
            sp.wait_ge(steps_a.sem, steps_a.at('xset'))
            sp.dma_start(g.scratch_x, flat(g.x[:, :, :])).then_inc(wr.sem, wr.next('end', 16))
            sp.wait_ge(wr.sem, wr.at('end'))

        @block.vector
        def _(ve):
            ve.wait_ge(in_ready.sem, in_ready.at('all'))
            ve.tensor_tensor(g.rb[:, 2, :], g.rb[:, 0, :], g.rb[:, 1, :], ALU.subtract).then_inc(
                    steps_v.sem, steps_v.next())
            ve.wait_ge(steps_v.sem, steps_v.count)
            ve.tensor_copy(g.rbrow[:, :, :], g.rb[:, 2, :].unsqueeze(2).to_broadcast([NBUCKET, H, P])).then_inc(
                    steps_v.sem, steps_v.next('rb'))
            ve.wait_ge(steps_v.sem, steps_v.count)
            ve.wait_ge(g.X[3].filled, g.X[3].at(('brow', 3)))
            rows = [oh(f'row{t}') for t in range(DS)]
            for t in range(DS):
                ve.tensor_tensor(g.rbrow[:, t, :].rearrange("p (h n) -> p h n", h=H),
                                      g.rb[:, 2, :].unsqueeze(2).to_broadcast([NBUCKET, H, NS]),
                                      rows[t].rearrange("p (h n) -> p h n", h=H), ALU.mult).then_inc(
                        steps_v.sem, steps_v.next(('row', t)))
                ve.wait_ge(steps_v.sem, steps_v.count)

        @block.tensor
        def _(pe):
            pe.wait_ge(steps_v.sem, steps_v.at('rb'))
            for h in range(H):
                pe.wait_ge(g.X[h].drained, g.X[h].claim(('brow', h)))
                x = g.X[h].ap
                mm = pe.matmul(x[:, 0:383], g.rbrow[:, h, :], oh('oh')[:, 0:383], start=True, stop=True)
                mm.then_inc(g.X[h].filled, 1)
            pe.wait_ge(g.X[0].drained, g.X[0].claim('bias_s'))
            x = g.X[0].ap
            for t in range(DS):
                pe.wait_ge(steps_v.sem, steps_v.at(('row', t)))
                mm = pe.matmul(x[:, 0:160], g.rbrow[:, t, :], oh(f'oh{t}'), start=(t == 0), stop=(t == DS - 1))
            mm.then_inc(g.X[0].filled, 1)
            pe.wait_ge(x_in.sem, x_in.at('all'))
            for c in range(5):
                n = P if c < 4 else NS
                for half in range(2):
                    b = g.X[2 + half]
                    pe.wait_ge(b.drained, b.claim(('x', c, half)))
                    x = b.ap
                    for k in range(4):
                        mm = pe.transpose(x[:, k * P:k * P + n], g.xtok[0:n, c, (half * 4 + k) * P:(half * 4 + k + 1) * P],
                                          ident[0:n, 0:n])
                    mm.then_inc(b.filled, 1)

        @block.scalar
        def _(ac):
            for h in range(H):
                ac.wait_ge(g.X[h].filled, g.X[h].at(('brow', h)))
                x = g.X[h].ap
                ac.activation(g.brow[:, h, :], x[:, 0:383], ACT.Copy).then_inc(g.X[h].drained, 1)
                ac.wait_ge(g.X[h].drained, g.X[h].at(('brow', h)))
            ac.activation(g.stat[:, 0:1], g.eps(), ACT.Copy).then_inc(steps_a.sem, steps_a.next('brow'))
            ac.wait_ge(steps_a.sem, steps_a.count)
            ac.wait_ge(g.X[0].filled, g.X[0].at('bias_s'))
            x = g.X[0].ap
            ac.activation(g.bias_s[:, :], x[:, 0:160], ACT.Copy).then_inc(g.X[0].drained, 1)
            ac.wait_ge(g.X[0].drained, g.X[0].at('bias_s'))
            for c in range(5):
                n = P if c < 4 else NS
                for half in range(2):
                    b = g.X[2 + half]
                    ac.wait_ge(b.filled, b.at(('x', c, half)))
                    x = b.ap
                    ac.activation(g.x[:, half * 4:half * 4 + 4, c * P:c * P + n],
                                          x[:, :].rearrange("p (k n) -> p k n", k=4)[:, :, 0:n], ACT.Copy).then_inc(
                            b.drained, 1)
                    ac.wait_ge(b.drained, b.at(('x', c, half)))
            ac.activation(g.stat[:, 1:2], g.eps(), ACT.Copy).then_inc(steps_a.sem, steps_a.next('xset'))
            ac.wait_ge(steps_a.sem, steps_a.count)


def halves(ap):
    return ap.rearrange("p (a b) -> p a b", a=2)


def head_view(ap, n):
    return ap[:, 0:H * n].rearrange("p (h n) -> p h n", h=H)


def chunk_of(c):
    return (slice(c * P, c * P + P), P) if c < 4 else (slice(SEQ, NT), NS)


def layer_program(g, layer):
    nc, io, const = g.nc, g.io, g.const
    ident, ones = const('ident'), const('ones')
    S = lambda n: g.counter(n)
    w_in_raw = [S(f"w_loaded{i}") for i in range(NRAW)]
    w_hi, w_lo = S("w_hi_made"), S("w_lo_made")
    x_in, rows_in, state_in = S("x_loaded"), S("rows_loaded"), S("conv_states_loaded")
    kidx_in = [S(f"kidx_loaded{i}") for i in range(2)]
    rs_in = [S(f"ret_state_loaded{i}") for i in range(2)]
    ds_in = [S(f"dn_state_loaded{i}") for i in range(2)]
    k_in = [S(f"k_page_loaded{i}") for i in range(KPAGES)]
    v_in = [S(f"v_page_loaded{i}") for i in range(VPAGES)]
    act_steps, vec_steps, pool_steps = S("act_steps"), S("vec_steps"), S("pool_steps")
    act_out, vec_out, pe_out, pool_out = S("act_made"), S("vec_made"), S("pe_made"), S("pool_made")
    st_idx, st_kv, st_k = S("kidx_stored"), S("v_stored"), [S(f"ktok_stored{i}") for i in range(2)]
    st_state, st_dn = S("state_stored"), S("dn_rows_stored")
    st_rs = [S(f"ret_sample_state_stored{i}") for i in range(2)]
    st_ds = [S(f"dn_sample_state_stored{i}") for i in range(2)]
    st_ffn = [S(f"ffn_rows_stored{i}") for i in range(4)]
    PJ, X = g.PJ, g.X
    at_layer = lambda name: io[name][bass.ds(layer, 1)]

    def last_use(t):
        u, i = t
        if u.startswith('down') and i == 0:
            return pe_out.sem, pe_out.at(('used', u))
        bank, key = PJ[1], None
        if u == 'ik':
            bank, key = (PJ[0], 'ik') if i == 0 else (PJ[1], 'small')
        elif u.startswith('gate'):
            bank, key = PJ[0], ('gate', int(u[4]), int(u[5]), i)
        elif u.startswith('br'):
            key = ('br', int(u[2]), int(u[3]), i)
        elif u.startswith('up'):
            bank, key = PJ[i], ('up', *map(int, u[2:].split('_')), i)
        elif u.startswith('down'):
            f, c = map(int, u[4:].split('_'))
            bank, key = PJ[c % 2], ('down', f, c)
        elif u == 'iq':
            bank, key = PJ[i], f'iq{i}'
        elif u[0] == 'z':
            bank, key = PJ[0], ('z', 2 * int(u[1]) + i)
        else:
            bank, key = PJ[i], (u[:-1], 2 * int(u[-1]) + i)
        return bank.filled, bank.at(key)
    raw, hi, lo = g.w_raw, g.w_hi, g.w_lo
    gC, gG, gBeta, gEK, gBE, gTmp, gA, gB = (g.gate[:, i] for i in range(8))

    def unit_pieces(u):
        t = raw[UIDX[u] % NRAW]
        win = at_layer('w_in').rearrange("a (k p) n -> p (a k) n", p=P)

        def cols(src, w, n_k=KD, at=0, width=256):
            return (t[:, 0:n_k * width].rearrange("p (k n) -> p k n", k=n_k)[:, :, at:at + w], src)
        if u == 'ik':
            ik = win[:, :, COL['ik']:COL['ik'] + 64]
            return [cols(ik, 64), cols(ik, 64, at=64), cols(win[:, :, COL['b']:COL['b'] + 8], 8, at=128),
                    cols(win[:, :, COL['iw']:COL['iw'] + 4], 4, at=136), cols(win[:, :, 0:116], 116, at=140)]
        if u == 'iq':
            return [cols(win[:, :, COL['iq']:COL['iq'] + 256], 256)]
        if u.startswith('gate'):
            c = COL['gate'] + int(u[4]) * D + int(u[5]) * 256
            return [cols(win[:, :, c:c + 256], 256)]
        if u.startswith('br'):
            n, d = int(u[2]), int(u[3])
            src = at_layer('w_branch').rearrange("a n (k p) m -> p (a n k) m", p=P)
            return [cols(src[:, n * H:n * H + H, d * 256:d * 256 + 256], 256, n_k=H)]
        if u.startswith('wo'):
            c = int(u[2]) * 256
            return [cols(at_layer('w_o').rearrange("a (k p) m -> p (a k) m", p=P)[:, :, c:c + 256], 256)]
        if u.startswith('up'):
            f, j = map(int, u[2:].split('_'))
            c = (f * FH + j) * P
            src = at_layer('w_up').rearrange("a (k p) m -> p (a k) m", p=P)
            return [cols(src[:, :, c:c + P], P), cols(src[:, :, DFF + c:DFF + c + P], P, at=P)]
        if u.startswith('down'):
            f, c = map(int, u[4:].split('_'))
            src = at_layer('w_down').rearrange("a (k p) m -> p (a k) m", p=P)
            return [cols(src[:, f * FH:f * FH + FH, c * P:c * P + P], P, n_k=FH, width=P)]
        name, i = (u[:-1], int(u[-1]))
        return [cols(win[:, :, COL[name] + i * 256:COL[name] + i * 256 + 256], 256)]

    def unit_size(u):
        return 1024 if u.startswith('br') else FH * P if u.startswith('down') else 2048

    def tile_of(t):
        u, i = t
        x = raw[UIDX[u] % NRAW]
        if u.startswith('down'):
            return x[:, 0:FH * P].rearrange("p (k n) -> p k n", n=P)[:, UP_K:FH] if i \
                else x[:, 0:UP_K * P].rearrange("p (k n) -> p k n", n=P)
        x = x[:, 0:unit_size(u)].rearrange("p (k n) -> p k n", n=256)
        return x[:, :, i * P:i * P + P]

    def split_view(bufs, t):
        n_k, n = tile_of(t).shape[1:]
        return bufs[TIDX[t] % NSPLIT][:, 0:n_k * n].rearrange("p (k n) -> p k n", n=n)

    def load_unit(q, i):
        if i >= len(UNITS):
            return
        u = UNITS[i]
        if i >= NRAW:
            q.wait_ge(w_lo.sem, w_lo.at((UNITS[i - NRAW], 1)))
        loaded = w_in_raw[i % NRAW]
        pieces = unit_pieces(u)
        for n, (dst, src) in enumerate(pieces):
            q.dma_start(dst, src).then_inc(loaded.sem, loaded.next(u if n == len(pieces) - 1 else None, 16))

    @g.block.sync
    def _(sp):
        r0, r1 = g.par_rows
        fw = at_layer('ffn_conv_w').rearrange("a i (t p) -> (a i t) p", p=P)
        for t, base, n, src in (
                (r0, PAR0['f0'], 4 * FT, fw[0:4 * FT]), (r1, PAR1['f2'], 2 * FT, fw[4 * FT:6 * FT]),
                (r0, PAR0['mix'], 8, at_layer('norm_mix').rearrange("a (k p) -> (a k) p", p=P)),
                (r0, PAR0['ffn'], 8, at_layer('norm_ffn').rearrange("a (k p) -> (a k) p", p=P)),
                (r0, PAR0['dnn'], 1, at_layer('dn_norm')),
                (r0, PAR0['retn'], 4, at_layer('ret_norm').rearrange("a h p -> (a h) p")),
                (r1, PAR1['dc'], 48, at_layer('dn_conv_w').rearrange("a i (t p) -> (a i t) p", p=P)),
                (r1, PAR1['fin'], 8, io['norm_final'].rearrange("(k p) -> k p", p=P))):
            sp.dma_start(t[base:base + n, :], src).then_inc(rows_in.sem, rows_in.next(by=16))
        sp.dma_start(g.lrow[:, 0, :], at_layer('dn_a_log').to_broadcast([P, H])).then_inc(
                rows_in.sem, rows_in.next(by=16))
        sp.dma_start(g.lrow[:, 1, :], at_layer('dn_dt_bias').to_broadcast([P, H])).then_inc(
                rows_in.sem, rows_in.next('all', 16))
        for i in range(NRAW):
            load_unit(sp, i)
        sp.dma_start(g.dn_rows[:, :], at_layer('state_dn_conv').rearrange("a b i n -> (a b i) n")).then_inc(
                state_in.sem, state_in.next(by=16))
        sp.dma_start(g.ffn_rows[:, :], at_layer('state_ffn_conv').rearrange("a b i n -> (a b i) n")).then_inc(
                state_in.sem, state_in.next('all', 16))
        n_phys = io['cache_k'].shape[1]
        pools = {n: io[n].rearrange("l n p h d -> (l n) p (h d)") for n in ('cache_k', 'cache_v')}
        pools['cache_kidx'] = io['cache_kidx'].rearrange("l n p d -> (l n) p d")

        def page(pool, b, pg):
            e = b * NPG + pg
            phys = sp.value_load(g.ptab[0:1, e:e + 1], min_val=0, max_val=n_phys - 1)
            return pools[pool][bass.ds(phys + layer * n_phys, 1)].rearrange("a p n -> (a p) n")
        for b in range(DB):
            if b >= 2:
                sp.wait_ge(X[1].filled, X[1].at(('kidxT', b - 2)))
            elif b == 0:
                sp.wait_ge(vec_out.sem, vec_out.at(('u', KD - 1)))
            for pg in range(NPG):
                sp.dma_start(g.kidx[b % 2][:, pg, :], page('cache_kidx', b, pg)).then_inc(
                        kidx_in[b % 2].sem, kidx_in[b % 2].next(b if pg == NPG - 1 else None, 16))
        for b in range(DB):
            if b >= 2:
                sp.wait_ge(X[b % 2].drained, X[b % 2].at(('rS', 4, b - 2)))
            elif b == 0:
                sp.wait_ge(X[2].filled, X[2].at(('s_score', 1)))
                sp.wait_ge(vec_out.sem, vec_out.at('index_done'))
                sp.wait_ge(st_idx.sem, st_idx.at('all'))
            sp.dma_start(head_view(g.r_sin[b % 2], P), at_layer('state_ret').rearrange(
                "a b h k v -> k (a b) h v")[:, b]).then_inc(rs_in[b % 2].sem, rs_in[b % 2].next(b, 16))
        sp.wait_ge(PJ[1].drained, PJ[1].at(('ao', 3)))
        sp.wait_ge(st_kv.sem, st_kv.at('v'))
        sp.wait_ge(st_k[0].sem, st_k[0].at(4))
        sp.wait_ge(st_k[1].sem, st_k[1].at(3))
        for i in range(NPAGES):
            if i >= KPAGES:
                m = i - KPAGES
                sp.wait_ge(X[m % 2].filled, X[m % 2].at(('sk', m)))
            sp.dma_start(g.kpage[i % KPAGES][:, :], page('cache_k', *divmod(i, NPG))).then_inc(
                k_in[i % KPAGES].sem, k_in[i % KPAGES].next(i, 16))
        sp.wait_ge(vec_out.sem, vec_out.at(('l2', 7)))
        for i in range(NPAGES):
            if i >= VPAGES:
                sp.wait_ge(pe_out.sem, pe_out.at(('v', i - VPAGES)))
            sp.dma_start(g.vpage[i % VPAGES], page('cache_v', *divmod(i, NPG))).then_inc(
                v_in[i % VPAGES].sem, v_in[i % VPAGES].next(i, 16))
        for ps in range(2):
            for b in range(DB):
                n = ps * DB + b
                if n >= 2:
                    if n < DB + 2:
                        sp.wait_ge(pe_out.sem, pe_out.at(('ds', n - 2)))
                    else:
                        sp.wait_ge(X[b % 2].drained, X[b % 2].at(('dS', 4, b - 2)))
                else:
                    sp.wait_ge(X[n % 2].filled, X[n % 2].at(('s_oT', n)))
                sp.dma_start(head_view(g.d_sin[n % 2], P), at_layer('state_dn').rearrange(
                    "a b h k v -> k (a b) h v")[:, b]).then_inc(ds_in[n % 2].sem, ds_in[n % 2].next(n, 16))
        sp.wait_ge(act_out.sem, act_out.at(('bsplit', 2)))
        sp.wait_ge(vec_out.sem, vec_out.at(('bsplit', 2)))
        sp.dma_start(flat(g.x[:, :, :]), g.scratch_x).then_inc(x_in.sem, x_in.next('again', 16))
        for c in range(KD):
            sp.wait_ge(PJ[c % 2].drained, PJ[c % 2].at(('down', 1, c)))
            sp.dma_start(g.scratch_x[:, c * NT:c * NT + NT], g.x[:, c, :]).then_inc(
                x_in.sem, x_in.next('stored' if c == KD - 1 else None, 16))
        sp.wait_ge(x_in.sem, x_in.at('stored'))

    @g.block.gpsimd
    def _(po):

        for t in TILES:
            po.wait_ge(w_hi.sem, w_hi.at(t))
            po.tensor_tensor(split_view(lo, t), tile_of(t), split_view(hi, t).bitcast(F32), ALU.subtract).then_inc(
                w_lo.sem, w_lo.next(t))

    @g.block.tensor
    def _(pe):
        def mm3(out, wh, wl, xh, xl, start, stop):
            pe.matmul(out, wh, xh, start=start, stop=False)
            pe.matmul(out, wh, xl, start=False, stop=False)
            return pe.matmul(out, wl, xh, start=False, stop=stop)

        def dense_tile(key, slot, u, i, ah, al, ready=None, between=None):
            pe.wait_ge(w_lo.sem, w_lo.at((u, i)))
            wh, wl = split_view(hi, (u, i)), split_view(lo, (u, i))
            n_k = wh.shape[1]
            pe.wait_ge(PJ[slot].drained, PJ[slot].claim(key))
            out = PJ[slot].ap
            for half in range(2):
                if half == 1 and between is not None:
                    between()
                for k in range(n_k):
                    if half == 0 and ready is not None:
                        ready(k)
                    cs = slice(half * HT, half * HT + HT)
                    mm = mm3(out[:, half, 0:HT], wh[:, k, :], wl[:, k, :], ah[:, k, cs], al[:, k, cs],
                             k == 0, k == n_k - 1)
            mm.then_inc(PJ[slot].filled, 1)

        def column_sums(key, slot, sources):
            pe.wait_ge(PJ[slot].drained, PJ[slot].claim(key))
            out = PJ[slot].ap
            n = len(sources)
            for k, (wait, ap) in enumerate(sources):
                wait()
                for half in range(2):
                    mm = pe.matmul(out[:, half, 0:HT], ones, ap[:, half * HT:half * HT + HT],
                                   start=(k == 0), stop=(k == n - 1))
                if k < n - 1:
                    mm.then_inc(pe_out.sem, pe_out.next((key, k)))
            mm.then_inc(PJ[slot].filled, 1)

        def turn(bank, key, n, m, srcs, pitch):
            pe.wait_ge(bank.drained, bank.claim(key))
            x = bank.ap
            for i, s in enumerate(srcs):
                mm = pe.transpose(x[0:m, i * pitch:i * pitch + n], s, ident[0:n, 0:n])
            mm.then_inc(bank.filled, 1)

        column_sums('rms0', 0, [((lambda: pe.wait_ge(vec_out.sem, vec_out.at('squares'))), g.xsum)])
        pe.wait_ge(rows_in.sem, rows_in.at('all'))
        turn(X[0], 'par0', PAR0_N, P, [g.par_rows[0][0:PAR0_N, :]], PAR0_N)
        turn(X[1], 'par1', PAR1_N, P, [g.par_rows[1][0:PAR1_N, :]], PAR1_N)

        def dense_unit(u, keys, first_ready=None):
            for i, key in enumerate(keys):
                dense_tile(key, i, u, i, g.uhi, g.ulo, first_ready if i == 0 else None)

        def u_ready(k):
            pe.wait_ge(vec_out.sem, vec_out.at(('u', k)))
        dense_unit('iq', ['iq0', 'iq1'], u_ready)
        dense_tile('ik', 0, 'ik', 0, g.uhi, g.ulo)
        dense_tile('small', 1, 'ik', 1, g.uhi, g.ulo)
        pe.wait_ge(state_in.sem, state_in.at('all'))
        turn(X[2], 'dn_prev', 24, P, [g.dn_rows[:, t * P:t * P + P] for t in range(12)], 24)
        turn(X[3], 'ffn_prev0', 16, P, [g.ffn_rows[:, t * P:t * P + P] for t in range(FT)], 16)
        turn(X[0], 'ffn_prev1', 16, P, [g.ffn_rows[:, t * P:t * P + P] for t in range(FT, 2 * FT)], 16)
        pe.wait_ge(PJ[1].drained, PJ[1].at('small'))
        pe.wait_ge(X[1].drained, X[1].claim('small'))
        for c in range(5):
            cs, n = chunk_of(c)
            mm = pe.transpose(X[1].ap[0:n, c * 12:c * 12 + 12], g.smallT[:, cs], ident[0:12, 0:12])
        mm.then_inc(X[1].filled, 1)
        pe.wait_ge(PJ[0].drained, PJ[0].at('ik'))
        pe.wait_ge(X[0].drained, X[0].claim('kidx_tok'))
        x = X[0].ap
        for c in range(5):
            cs, n = chunk_of(c)
            mm = pe.transpose(x[0:n, c * 64:c * 64 + 64], g.ik[0:64, cs], ident[0:64, 0:64])
        mm.then_inc(X[0].filled, 1)
        pe.wait_ge(X[1].drained, X[1].at('small'))
        pe.wait_ge(X[2].drained, X[2].claim('wrow'))
        x = X[2].ap
        for h in range(H):
            mm = pe.matmul(x[:, h * NS:h * NS + NS], g.small[0:NS, 4, 8 + h:9 + h].to_broadcast([NS, P]),
                           ident[0:NS, 0:NS], start=True, stop=True)
        mm.then_inc(X[2].filled, 1)
        pe.wait_ge(act_out.sem, act_out.at('iqs'))

        def prompt_scores(i):
            qb, h = i // H + 1, i % H
            n, b0, bank = (qb + 1) * P, 64 * (h % 2), X[2 + i % 2]
            pe.wait_ge(bank.drained, bank.claim(('is', qb, h)))
            mm = pe.matmul(bank.ap[:, 0:n], g.iq[b0:b0 + 64, h // 2, qb * P:qb * P + P], g.ik[b0:b0 + 64, 0:n],
                           start=True, stop=True)
            mm.then_inc(bank.filled, 1)

        def turn_index_keys(b):
            pe.wait_ge(kidx_in[b % 2].sem, kidx_in[b % 2].at(b))
            for q in range(2):
                turn(X[q], ('kidxT' if q else 'kidxT0', b), P, 64, [g.kidx[b % 2][:, q * 4 + j, :] for j in range(4)], P)

        def sample_scores(b):
            pe.wait_ge(X[1].drained, X[1].at(('kidxT', b)))
            bank = X[2 + b % 2]
            pe.wait_ge(bank.drained, bank.claim(('sT', b)))
            for pg in range(NPG):
                mm = pe.matmul(bank.ap[:, pg * 16:pg * 16 + 16].rearrange("p (h t) -> p h t", h=H),
                               g.kidxT[:, pg * P:pg * P + P], g.iqs[:, :, b * DS:b * DS + DS], start=True, stop=True)
            mm.then_inc(bank.filled, 1)

        for t in range(16):
            nm, h = ('rq', 'rk', 'rv', 'rg')[t // H], t % H
            dense_tile((nm, h), h % 2, f'{nm}{h // 2}', h % 2, g.uhi, g.ulo,
                       between=(lambda: prompt_scores(t)) if t < 12 else None)
            if t % 2:
                turn_index_keys(t // 2)
            elif t:
                sample_scores(t // 2 - 1)
        sample_scores(DB - 1)
        pe.wait_ge(X[0].drained, X[0].claim('s_new'))
        x = X[0].ap
        for h in range(H):
            mm = pe.matmul(x[0:NS, h * NS:h * NS + NS], g.iqs[:, h, :], g.ik[0:64, SEQ:NT], start=True, stop=True)
        mm.then_inc(X[0].filled, 1)
        pe.wait_ge(vec_out.sem, vec_out.at('scoreT'))
        for q in range(2):
            turn(X[1 + q], ('s_score', q), P, NS, [g.scoreT[:, q * 4 + j, :] for j in range(4)], P)

        for c in range(5):
            cs, n = chunk_of(c)
            if c == 0:
                pe.wait_ge(vec_out.sem, vec_out.at(('rk', 3)))
                pe.wait_ge(PJ[1].drained, PJ[1].at(('rv', 3)))
            turn(X[0], ('rkT', c), P, n, [g.rqk[:, 4 + h, cs] for h in range(H)], P)
            turn(X[1], ('rvT', c), P, n, [g.rv[:, h, cs] for h in range(H)], P)
            pe.wait_ge(X[2].drained, X[2].claim(('rqk', c)))
            x = X[2].ap
            for h in range(H):
                mm = pe.matmul(x[0:n, h * n:h * n + n], g.rqk[:, 4 + h, cs], g.rqk[:, h, cs], start=True, stop=True)
            mm.then_inc(X[2].filled, 1)
            if c < 4:
                dense_tile(('aq', c), c % 2, f'aq{c // 2}', c % 2, g.uhi, g.ulo)
            pe.wait_ge(vec_out.sem, vec_out.at(('r_in', c)))
            pe.wait_ge(X[1].drained, X[1].at(('rvT', c)))
            pe.wait_ge(X[3].drained, X[3].claim(('ro', c)))
            x = X[3].ap
            kd, v, qk, qd = g.r_kd, g.r_v, g.r_qk, g.r_qd
            if c < 4:
                for h in range(H):
                    hs = slice(h * P, h * P + P)
                    pe.matmul(x[:, hs], g.r_S[:, hs], qd[:, hs], start=True, stop=False)
                    mm = pe.matmul(x[:, hs], v[:, hs], qk[:, hs], start=False, stop=True)
                mm.then_inc(X[3].filled, 1)
                pe.wait_ge(X[0].drained, X[0].claim(('rS', c)))
                x = X[0].ap
                for h in range(H):
                    hs = slice(h * P, h * P + P)
                    mm = pe.matmul(x[:, hs], kd[:, hs], v[:, hs], start=True, stop=True)
                mm.then_inc(X[0].filled, 1)
            else:
                for h in range(H):
                    pe.matmul(x[:, h * n:h * n + n], v[0:n, h * P:h * P + P], qk[0:n, h * n:h * n + n],
                              start=(h == 0), stop=False, skip_group_check=True)
                for b in range(DB):
                    pe.wait_ge(rs_in[b % 2].sem, rs_in[b % 2].at(b))
                    for h in range(H):
                        o = h * n + b * DS
                        mm = pe.matmul(x[:, o:o + DS], g.r_sin[b % 2][:, h * P:h * P + P], qd[:, o:o + DS],
                                       start=False, stop=(b == DB - 1), skip_group_check=True)
                    if b == DB - 1:
                        mm.then_inc(X[3].filled, 1)
                    pe.wait_ge(vec_out.sem, vec_out.at(('kdm', b)))
                    bank = X[b % 2]
                    pe.wait_ge(bank.drained, bank.claim(('rS', c, b)))
                    y = bank.ap
                    for h in range(H):
                        hs = slice(h * P, h * P + P)
                        mm = pe.matmul(y[:, hs], g.r_kdm[b % 2][:, hs], v[0:n, hs], start=True, stop=True)
                    mm.then_inc(bank.filled, 1)
        pe.wait_ge(X[3].drained, X[3].at(('ro', 4)))
        for h in range(H):
            column_sums(('rmean', h), 0, [((lambda: None), g.rv[:, h, :])])
            dense_tile(('z', h), 0, f'z{h // 2}', h % 2, g.uhi, g.ulo)
            column_sums(('rvar', h), 1, [((lambda h=h: pe.wait_ge(act_out.sem, act_out.at(('rsq', h)))), g.rswap)])

        for nm in ('ak', 'av'):
            for i in range(2):
                dense_unit(f'{nm}{i}', [(nm, 2 * i), (nm, 2 * i + 1)])
        pe.wait_ge(PJ[1].drained, PJ[1].at(('av', 3)))
        for c in range(5):
            cs, n = chunk_of(c)
            turn(X[0], ('kT', c), P, n, [g.akv[:, h, cs] for h in range(H)], P)
            turn(X[1], ('vT', c), P, n, [g.akv[:, 4 + h, cs] for h in range(H)], P)
        steps = [(qb, h) for qb in range(4) for h in range(H)]

        def logits(i):
            qb, h = steps[i]
            n = (qb + 1) * P
            pe.wait_ge(X[i % 2].drained, X[i % 2].claim(('qk', i)))
            mm = pe.matmul(X[i % 2].ap[:, 0:n], g.out_att[:, h, qb * P:qb * P + P], g.akv[:, h, 0:n],
                           start=True, stop=True)
            mm.then_inc(X[i % 2].filled, 1)

        logits(0)
        for i in range(len(steps) + 2):
            if i + 1 < len(steps):
                logits(i + 1)
            if 0 < i <= len(steps):
                j = i - 1
                pe.wait_ge(act_out.sem, act_out.at(('prob', j)))
                turn(X[2 + j % 2], ('pT', j), P, P, [g.prob[j % 2][:, t * P:t * P + P] for t in range(steps[j][0] + 1)], P)
            if i > 1:
                j = i - 2
                qb, h = steps[j]
                pe.wait_ge(X[2 + j % 2].drained, X[2 + j % 2].at(('pT', j)))
                if j == 0:
                    pe.wait_ge(X[1].drained, X[1].at(('vT', 4)))
                if h == 0:
                    pe.wait_ge(PJ[qb % 2].drained, PJ[qb % 2].claim(('ao', qb)))
                for t in range(qb + 1):
                    mm = pe.matmul(PJ[qb % 2].ap[:, 0, h * P:h * P + P], g.vtok[:, t, h * P:h * P + P],
                                   g.probT[j % 2][:, t * P:t * P + P], start=(t == 0), stop=(t == qb))
                if h == H - 1:
                    mm.then_inc(PJ[qb % 2].filled, 1)

        def turn_keys(i):
            pe.wait_ge(k_in[i % KPAGES].sem, k_in[i % KPAGES].at(i))
            turn(X[i % 2], ('sk', i), P, P, [g.kpage[i % KPAGES][:, h * P:h * P + P] for h in range(H)], P)

        def key_page(i):
            b, pg = divmod(i, NPG)
            if i + 1 < NPAGES:
                turn_keys(i + 1)
            bank, c0 = X[2 + pg // 4], pg % 4 * P
            if b == 0 and pg % 4 == 0:
                pe.wait_ge(bank.drained, bank.claim(('slog', pg // 4)))
            pe.wait_ge(X[i % 2].drained, X[i % 2].at(('sk', i)))
            for h in range(H):
                mm = pe.matmul(bank.ap[h * NS:h * NS + NS, c0:c0 + P], g.s_q[:, h, b * NS:b * NS + NS],
                               g.kT[i % 2][:, h * P:h * P + P], start=(b == 0 and pg % 4 == 0), stop=(b == DB - 1),
                               skip_group_check=True)
            if b == DB - 1 and pg % 4 == 3:
                mm.then_inc(bank.filled, 1)

        turn_keys(0)
        pe.wait_ge(vec_out.sem, vec_out.at('s_q'))
        for t in range(12):
            def keys(half):
                for i in range(NPAGES * (2 * t + half) // 24, NPAGES * (2 * t + half + 1) // 24):
                    key_page(i)
            dense_tile(('dn', t), t % 2, f'dn{t // 2}', t % 2, g.uhi, g.ulo, between=lambda: keys(0))
            keys(1)

        pe.wait_ge(vec_out.sem, vec_out.at('sel_s'))
        pe.wait_ge(X[0].drained, X[0].claim(('srep', 0)))
        x = X[0].ap
        mm = pe.matmul(x[:, 0:512], const('rep', NS), g.sel_s[:, 0:512], start=True, stop=True)
        mm.then_inc(X[0].filled, 1)
        pe.wait_ge(X[1].drained, X[1].claim(('srep', 1)))
        x = X[1].ap
        mm = pe.matmul(x[:, 0:512], const('rep', NS), g.sel_s[:, 512:1024], start=True, stop=True)
        mm.then_inc(X[1].filled, 1)
        pe.wait_ge(X[0].drained, X[0].claim(('srep', 2)))
        x = X[0].ap
        mm = pe.matmul(x[:, 0:NS], const('rep', NS), g.sel_s[:, 1024:NEWK], start=True, stop=True)
        mm.then_inc(X[0].filled, 1)
        pe.wait_ge(X[1].drained, X[1].claim('snew'))
        x = X[1].ap
        for h in range(H):
            mm = pe.matmul(x[h * NS:h * NS + NS, 0:NS], g.out_att[:, h, SEQ:NT], g.s_ak[:, h, :], start=True, stop=True)
        mm.then_inc(X[1].filled, 1)
        for t in range(8):
            column_sums(('l2', t), t % 2, [((lambda t=t: pe.wait_ge(act_out.sem, act_out.at(('l2sq', t)))), g.d_sq[t % 2])])
        pe.wait_ge(X[3].drained, X[3].claim('gsum'))
        x = X[3].ap
        pe.wait_ge(act_out.sem, act_out.at('conv_done'))
        pe.wait_ge(vec_out.sem, vec_out.at('g'))
        G16 = gG[:, 0:4, :].rearrange("p c h -> p (c h)")
        pe.matmul(x[:, 0:16], const('triu'), G16, start=True, stop=True)
        pe.matmul(x[0:NS, 16:20], const('triu_s', NS)[:, 0:NS], gG[0:NS, 4, :], start=True, stop=True)
        pe.matmul(x[:, 20:36], const('after'), G16, start=True, stop=True)
        mm = pe.matmul(x[0:NS, 36:40], const('after_s', NS)[:, 0:NS], gG[0:NS, 4, :], start=True, stop=True)
        mm.then_inc(X[3].filled, 1)
        pe.wait_ge(vec_out.sem, vec_out.at('s_prob'))
        for q in range(2):
            turn(X[2 + q], ('spT', q), P, P, [g.s_log[:, (q * 4 + j) * P:(q * 4 + j + 1) * P] for j in range(4)], P)
        turn(X[0], 'spT_new', P, NS, [g.s_log[:, PAST:NEWK]], P)
        pe.wait_ge(X[0].drained, X[0].at('spT_new'))
        pe.wait_ge(X[1].drained, X[1].claim('s_new'))
        for h in range(H):
            hs = slice(h * NS, h * NS + NS)
            mm = pe.matmul(X[1].ap[hs, 0:P], g.s_pT[0:NS, NPG, hs], g.s_v[:, h * P:h * P + P], start=True, stop=True)
        mm.then_inc(X[1].filled, 1)
        pe.wait_ge(PJ[0].drained, PJ[0].claim('so'))

        def value_page(i):
            b, pg = divmod(i, NPG)
            pe.wait_ge(v_in[i % VPAGES].sem, v_in[i % VPAGES].at(i))
            for h in range(H):
                hs = slice(h * NS, h * NS + NS)
                mm = pe.matmul(PJ[0].ap[hs, b // 4, b % 4 * P:b % 4 * P + P], g.s_pT[:, pg, hs],
                               g.vpage[i % VPAGES][:, h * P:h * P + P], start=(pg == 0), stop=(pg == NPG - 1),
                               skip_group_check=True)
            if i == NPAGES - 1:
                mm.then_inc(PJ[0].filled, 1)
            else:
                mm.then_inc(pe_out.sem, pe_out.next(('v', i)))

        for c in range(5):
            if c == 4:
                pe.wait_ge(vec_out.sem, vec_out.at('s_o'))
                for i in range(2):
                    turn(X[i], ('s_oT', i), P, P, [g.s_o[i][:, j * P:j * P + P] for j in range(4)], P)
            cs, n = chunk_of(c)
            tri = const('triu') if c < 4 else const('triu_s', NS)[:, 0:NS]
            q, k, v = (g.qkv[:, 4 * i:4 * i + 4, cs] for i in range(3))
            for bank, key, src, rhs in ((X[1], 'grow', gG, tri), (X[0], 'betarow', gBeta, ident[0:n, 0:n])):
                pe.wait_ge(bank.drained, bank.claim((key, c)))
                x = bank.ap
                for h in range(H):
                    mm = pe.matmul(x[:, h * n:h * n + n], src[0:n, c, h:h + 1].to_broadcast([n, P]), rhs,
                                   start=True, stop=True)
                mm.then_inc(bank.filled, 1)
            if c == 0:
                pe.wait_ge(vec_out.sem, vec_out.at(('l2', 7)))
            for bank, key, a, b in ((X[2], 'kk', k, k), (X[3], 'kq', k, q)):
                pe.wait_ge(bank.drained, bank.claim((key, c)))
                x = bank.ap
                for h in range(H):
                    mm = pe.matmul(x[0:n, h * n:h * n + n], a[:, h, :], b[:, h, :], start=True, stop=True)
                mm.then_inc(bank.filled, 1)
            turn(X[1], ('dvT', c), P, n, [v[:, h, :] for h in range(H)], P)
            levels = LEVELS if c < 4 else LEVELS[:2]
            pages = iter(range(c * 16, c * 16 + 16 if c < 4 else 0))
            if c < 4:
                value_page(next(pages))
                value_page(next(pages))
            for s in levels:
                if s == levels[1]:
                    turn(X[1], ('dkT', c), P, n, [k[:, h, :] for h in range(H)], P)
                pe.wait_ge(vec_out.sem, vec_out.at(('lm', c, s)))
                if s != levels[0]:
                    before = levels[levels.index(s) - 1]
                    pe.wait_ge(X[3].drained, X[3].at(('TY', c, before)))
                pe.wait_ge(X[2].drained, X[2].claim(('Y', c, s)))
                x = X[2].ap
                for h in range(H):
                    hs = slice(h * n, h * n + n)
                    mm = pe.matmul(x[0:n, hs], g.d_lm[0:n, hs], g.d_t[0:n, hs], start=True, stop=True)
                mm.then_inc(X[2].filled, 1)
                if c < 4:
                    value_page(next(pages))
                pe.wait_ge(X[2].drained, X[2].at(('Y', c, s)))
                if s != levels[0]:
                    pe.wait_ge(X[0].drained, X[0].at(('YT', c, before)))
                if s != levels[-1]:
                    pe.wait_ge(X[3].drained, X[3].claim(('TY', c, s)))
                    x = X[3].ap
                    for h in range(H):
                        hs = slice(h * n, h * n + n)
                        mm = pe.matmul(x[0:n, hs], g.d_tt[0:n, hs], g.d_y[0:n, hs], start=True, stop=True)
                    mm.then_inc(X[3].filled, 1)
                pe.wait_ge(X[0].drained, X[0].claim(('YT', c, s)))
                x = X[0].ap
                for h in range(H):
                    hs = slice(h * n, h * n + n)
                    mm = pe.matmul(x[0:n, hs], g.d_y[0:n, hs], g.d_tt[0:n, hs], start=True, stop=True)
                mm.then_inc(X[0].filled, 1)
                if c < 4:
                    value_page(next(pages))
            pe.wait_ge(X[0].drained, X[0].at(('YT', c, levels[-1])))
            pe.wait_ge(X[1].drained, X[1].claim(('kc', c)))
            x = X[1].ap
            for h in range(H):
                mm = pe.matmul(x[:, h * n:h * n + n], g.d_kb[0:n, h * P:h * P + P], g.d_tt[0:n, h * n:h * n + n],
                               start=True, stop=True)
            mm.then_inc(X[1].filled, 1)
            pe.wait_ge(X[1].drained, X[1].at(('kc', c)))
            pe.wait_ge(vec_out.sem, vec_out.at(('qd', c)))
            qk = g.d_dec
            if c < 4:
                pe.wait_ge(X[2].drained, X[2].claim(('dw', c)))
                x = X[2].ap
                for h in range(H):
                    hs = slice(h * P, h * P + P)
                    pe.matmul(x[:, hs], g.d_tt[:, hs], g.d_vb[:, hs], start=True, stop=False)
                    mm = pe.matmul(x[:, hs], g.d_kc[:, hs], g.d_S[:, hs], start=False, stop=True)
                mm.then_inc(X[2].filled, 1)
                pe.wait_ge(X[3].drained, X[3].claim(('do', c)))
                for h in range(H):
                    hs = slice(h * P, h * P + P)
                    pe.matmul(X[3].ap[:, hs], g.d_S[:, hs], g.d_qd[:, hs], start=(h == 0), stop=False,
                              skip_group_check=True)
                pe.wait_ge(X[2].drained, X[2].at(('dw', c)))
                pe.wait_ge(X[0].drained, X[0].claim(('dS', c)))
                for h in range(H):
                    hs = slice(h * P, h * P + P)
                    mm = pe.matmul(X[0].ap[:, hs], g.d_kd[:, hs], g.d_w[:, hs], start=True, stop=True)
                mm.then_inc(X[0].filled, 1)
                for h in range(H):
                    hs = slice(h * P, h * P + P)
                    mm = pe.matmul(X[3].ap[:, hs], g.d_w[:, hs], qk[:, hs], start=False, stop=True,
                                   skip_group_check=True)
                mm.then_inc(X[3].filled, 1)
            else:
                pe.wait_ge(X[2].drained, X[2].claim(('dw', c)))
                x = X[2].ap
                for h in range(H):
                    pe.matmul(x[:, h * n:h * n + n], g.d_vb[0:n, h * P:h * P + P], g.d_tt[0:n, h * n:h * n + n],
                              start=(h == 0), stop=False, skip_group_check=True)
                pe.wait_ge(X[3].drained, X[3].claim(('do', c)))
                y = X[3].ap
                for b in range(DB):
                    pe.wait_ge(ds_in[b % 2].sem, ds_in[b % 2].at(b))
                    for h in range(H):
                        o = h * n + b * DS
                        mm = pe.matmul(x[:, o:o + DS], g.d_sin[b % 2][:, h * P:h * P + P], g.d_kc[:, o:o + DS],
                                       start=False, stop=(b == DB - 1), skip_group_check=True)
                    if b == DB - 1:
                        mm.then_inc(X[2].filled, 1)
                    for h in range(H):
                        o = h * n + b * DS
                        mm = pe.matmul(y[:, o:o + DS], g.d_sin[b % 2][:, h * P:h * P + P], g.d_qd[:, o:o + DS],
                                       start=(b == 0 and h == 0), stop=False, skip_group_check=True)
                    mm.then_inc(pe_out.sem, pe_out.next(('ds', b)))
                pe.wait_ge(X[2].drained, X[2].at(('dw', c)))
                turn(X[1], 'dwT', P, n, [g.d_eg[:, 128 + h * n:128 + h * n + n] for h in range(H)], P)
                pe.wait_ge(X[1].drained, X[1].at('dwT'))
                for h in range(H):
                    mm = pe.matmul(y[:, h * n:h * n + n], g.d_w[0:n, h * P:h * P + P], qk[0:n, h * n:h * n + n],
                                   start=False, stop=True, skip_group_check=True)
                mm.then_inc(X[3].filled, 1)
                for b in range(DB):
                    pe.wait_ge(vec_out.sem, vec_out.at(('dkdm', b)))
                    pe.wait_ge(X[b % 2].drained, X[b % 2].claim(('dS', c, b)))
                    x = X[b % 2].ap
                    for h in range(H):
                        hs = slice(h * P, h * P + P)
                        mm = pe.matmul(x[:, hs], g.d_kdm[b % 2][:, hs], g.d_w[0:n, hs], start=True, stop=True)
                    mm.then_inc(X[b % 2].filled, 1)
        pe.wait_ge(X[3].drained, X[3].at(('do', 4)))
        for h in range(H):
            column_sums(('dvar', h), h % 2, [((lambda h=h: pe.wait_ge(act_out.sem, act_out.at(('dsq', h)))), g.d_sq[h % 2])])
        for i in range(3):
            turn(X[i], ('dn_last', i), P, 27, [g.dn_last[:, 4 * i + j, :] for j in range(4)], P)

        for n in range(3):
            for d in range(4):
                ug, ub = f'gate{n}{d}', f'br{n}{d}'
                for i in range(2):
                    dense_tile(('gate', n, d, i), 0, ug, i, g.uhi, g.ulo)
                    if d == 0 and i == 0:
                        pe.wait_ge(act_out.sem, act_out.at(('bsplit', n)))
                        pe.wait_ge(vec_out.sem, vec_out.at(('bsplit', n)))
                    dense_tile(('br', n, d, i), 1, ub, i, g.bhi[n % 2], g.blo[n % 2])

        def m_ready(k):
            pe.wait_ge(act_out.sem, act_out.at(('msplit', k)))
            pe.wait_ge(vec_out.sem, vec_out.at(('msplit', k)))
        for i in range(4):
            dense_unit(f'wo{i}', [('wo', 2 * i), ('wo', 2 * i + 1)], m_ready if i == 0 else None)
        column_sums('rms1', 0, [((lambda k=k: pe.wait_ge(act_out.sem, act_out.at(('hsq', k)))), g.f_sq if k % 2 == 0 else g.f_rs)
                                for k in range(KD)])

        for f in range(2):
            for j in range(FH):
                for i in range(2):
                    dense_tile(('up', f, j, i), i, f'up{f}_{j}', i, g.uhi, g.ulo,
                               (lambda k: pe.wait_ge(vec_out.sem, vec_out.at(('hn', k)))) if (f, j, i) == (0, 0, 0)
                               else None)
            for c in range(KD):
                u, slot = f'down{f}_{c}', PJ[c % 2]
                pe.wait_ge(slot.drained, slot.claim(('down', f, c)))
                for i in range(2):
                    pe.wait_ge(w_lo.sem, w_lo.at((u, i)))
                    wh, wl = split_view(hi, (u, i)), split_view(lo, (u, i))
                    for k in range(i * UP_K, FH if i else UP_K):
                        if c == 0:
                            pe.wait_ge(vec_out.sem, vec_out.at(('hff', f, k)))
                        for half in range(2):
                            cs = slice(half * HT, half * HT + HT)
                            mm = mm3(slot.ap[:, half, 0:HT], wh[:, k - i * UP_K, :], wl[:, k - i * UP_K, :],
                                     g.hhi[:, k, cs], g.hlo[:, k, cs], k == 0, k == FH - 1)
                    if i == 0:
                        mm.then_inc(pe_out.sem, pe_out.next(('used', u)))
                    else:
                        mm.then_inc(slot.filled, 1)
                for i in range(LAST * c // KD, LAST * (c + 1) // KD) if f else ():
                    if i == 0:
                        pe.wait_ge(act_out.sem, act_out.at('ffn_last'))
                    turn(X[i % 4], ('ffn_last', i), P, 18, [g.ffn_last[:, 4 * i + j, :] for j in range(4)], P)

    @g.block.scalar
    def _(ac):
        C = ACT.Copy

        def act(out, in_, f=C, **kw):
            return ac.activation(out, in_, f, **kw)

        def prep(n):
            if n >= len(TILES):
                return
            u, i = TILES[n]
            if n >= NSPLIT:
                ac.wait_ge(*last_use(TILES[n - NSPLIT]))
            if i == 0:
                ac.wait_ge(w_in_raw[UIDX[u] % NRAW].sem, w_in_raw[UIDX[u] % NRAW].at(u))
            act(split_view(hi, (u, i)), tile_of((u, i))).then_inc(w_hi.sem, w_hi.next((u, i)))
            if n and TILES[n - 1][1] == 1:
                load_unit(ac, UIDX[TILES[n - 1][0]] + NRAW)

        def next_tile(u, i):
            prep(TIDX[u, i] + NSPLIT)

        def rsqrt(out, bank, key, scale, made):
            ac.wait_ge(bank.filled, bank.at(key))
            x = bank.ap
            act(halves(out), x[:, :, 0:HT], ACT.Ln, scale=scale, bias=g.eps()).then_inc(bank.drained, 1)
            ac.wait_ge(bank.drained, bank.at(key))
            act(out, out, ACT.Exp, scale=-0.5).then_inc(act_out.sem, act_out.next(made))
            ac.wait_ge(act_out.sem, act_out.count)

        def rsqrt_pair(outs, keys, scale, made, between=()):
            for i in range(2):
                ac.wait_ge(PJ[i].filled, PJ[i].at(keys[i]))
                act(halves(outs[i]), PJ[i].ap[:, :, 0:HT], ACT.Ln, scale=scale, bias=g.eps()).then_inc(PJ[i].drained, 1)
            for square, t in between:
                square(t)
            for i in range(2):
                ac.wait_ge(PJ[i].drained, PJ[i].at(keys[i]))
                act(outs[i], outs[i], ACT.Exp, scale=-0.5).then_inc(act_out.sem, act_out.next(made[i]))
            ac.wait_ge(act_out.sem, act_out.count)

        def copy_out(bank, key, pairs, **kw):
            ac.wait_ge(bank.filled, bank.at(key))
            x = bank.ap
            pairs = pairs(x)
            for dst, src in pairs[:-1]:
                act(dst, src, **kw).then_inc(act_steps.sem, act_steps.next())
                ac.wait_ge(act_steps.sem, act_steps.count)
            act(*pairs[-1], **kw).then_inc(bank.drained, 1)
            ac.wait_ge(bank.drained, bank.at(key))

        for k in range(KD):
            if k >= 2:
                ac.wait_ge(vec_out.sem, vec_out.at(('sq', k - 2)))
            act(g.xsq[k % 2][:, :], g.x[:, k, :], ACT.Square).then_inc(act_out.sem, act_out.next(('sq', k)))
        copy_out(X[0], 'par0', lambda x: [(g.par[:, 0:PAR0_N], x[:, 0:PAR0_N])])
        copy_out(X[1], 'par1', lambda x: [(g.par[:, PAR0_N:PAR0_N + PAR1_N], x[:, 0:PAR1_N])])
        rsqrt(g.rstd0[:, :], PJ[0], 'rms0', 1.0 / D, 'rstd0')
        prep(0)
        for k in range(KD):
            ac.wait_ge(vec_out.sem, vec_out.at(('uf', k)))
            act(g.uhi[:, k, :], g.x[:, k, :]).then_inc(act_out.sem, act_out.next(('uh', k)))
        prep(1)
        prep(2)
        ac.wait_ge(vec_out.sem, vec_out.at(('u', KD - 1)))
        for i in range(2):
            copy_out(PJ[i], f'iq{i}', lambda x: [(halves(g.iq[:, i, :]), x[:, :, 0:HT])])
            next_tile('iq', i)
        copy_out(PJ[0], 'ik', lambda x: [(halves(g.ik[:, :]), x[:, :, 0:HT])])
        next_tile('ik', 0)
        copy_out(PJ[1], 'small', lambda x: [(halves(g.smallT[:, :]), x[0:12, :, 0:HT])])
        next_tile('ik', 1)
        copy_out(X[2], 'dn_prev', lambda x: [(g.dn_prev[:, :, :], x[:, 0:288].rearrange("p (t n) -> p t n", t=12))])
        for i, b in ((0, X[3]), (1, X[0])):
            copy_out(b, f'ffn_prev{i}', lambda x: [(g.ffn_prev[:, i * FT:i * FT + FT, :],
                                                    x[:, 0:FT * 16].rearrange("p (t n) -> p t n", t=FT))])
        act(g.gate[:, 7, 0, :], g.lrow[:, 0, :], ACT.Exp).then_inc(act_out.sem, act_out.next('states'))
        ac.wait_ge(act_out.sem, act_out.count)
        ac.wait_ge(vec_out.sem, vec_out.at('small_zero'))
        copy_out(X[1], 'small', lambda x: [(g.small[:, 0:4, :], x[:, 0:48].rearrange("p (c n) -> p c n", c=4)),
                                           (g.small[0:NS, 4, :], x[0:NS, 48:60])])
        for h in range(H):
            act(g.iqs[:, h, :], g.iq[64 * (h % 2):64 * (h % 2) + 64, h // 2, SEQ:NT]).then_inc(
                    act_out.sem, act_out.next('iqs' if h == H - 1 else None))
            ac.wait_ge(act_out.sem, act_out.count)
        copy_out(X[0], 'kidx_tok', lambda x: [(g.kidx_tok[:, 0:4, :], x[:, 0:256].rearrange("p (c n) -> p c n", c=4)),
                                              (g.kidx_tok[0:NS, 4, :], x[0:NS, 256:320])])
        ac.dma_start(at_layer('p_kidx').rearrange("a b (c p) n -> p (a b c) n", p=P), g.kidx_tok[:, 0:4, :]).then_inc(
                st_idx.sem, st_idx.next(by=16))
        ac.dma_start(at_layer('s_kidx').rearrange("a b t n -> (a b t) n"), g.kidx_tok[0:NS, 4, :]).then_inc(
                st_idx.sem, st_idx.next('all', 16))
        copy_out(X[2], 'wrow', lambda x: [(g.wrow[:, :, :].rearrange("p b (h t) -> p b h t", h=H),
                                           x[:, 0:P].rearrange("p (h b t) -> p b h t", h=H, b=DB))])

        prev = None
        for t in range(16):
            nm, h = ('rq', 'rk', 'rv', 'rg')[t // H], t % H
            if t < 12:
                n = (t // H + 2) * P
                if t >= 2:
                    ac.wait_ge(vec_out.sem, vec_out.at(('score', t - 2)))
                copy_out(X[2 + t % 2], ('is', t // H + 1, h), lambda x: [(g.relu_p[t % 2][:, 0:n], x[:, 0:n])], f=ACT.Relu)
            b, key = PJ[h % 2], (nm, h)
            if nm in ('rq', 'rk'):
                if prev is not None:
                    ac.wait_ge(vec_out.sem, vec_out.at(prev))
                sc = SCALE if nm == 'rq' else 1.0
                copy_out(b, key, lambda x: [(halves(g.rraw[:, :]), x[:, :, 0:HT]),
                                            (halves(g.rswap[0:64, :]), x[64:P, :, 0:HT]),
                                            (halves(g.rswap[64:P, :]), x[0:64, :, 0:HT])], scale=sc)
                prev = key
            elif nm == 'rv':
                copy_out(b, key, lambda x: [(halves(g.rv[:, h, :]), x[:, :, 0:HT])])
            else:
                copy_out(b, key, lambda x: [(halves(g.out_ret[:, h, :]), x[:, :, 0:HT])], f=ACT.Silu)
            if t % 2:
                seq = t // 2
                if seq:
                    ac.wait_ge(X[2 + (seq - 1) % 2].filled, X[2 + (seq - 1) % 2].at(('sT', seq - 1)))
                copy_out(X[0], ('kidxT0', seq), lambda x: [(g.kidxT[:, 0:512], x[0:64, :])])
                copy_out(X[1], ('kidxT', seq), lambda x: [(g.kidxT[:, 512:1024], x[0:64, :])])
            next_tile(f'{nm}{h // 2}', h % 2)
        copy_out(X[0], 's_new', lambda x: [(g.relu_s[:, :], x[0:NS, 0:P])], f=ACT.Relu)
        for q in range(2):
            copy_out(X[1 + q], ('s_score', q), lambda x: [(g.sel_s[:, q * 512:q * 512 + 512], x[0:NS, :])])

        ac.wait_ge(vec_out.sem, vec_out.at('index_done'))
        ac.wait_ge(st_idx.sem, st_idx.at('all'))
        for c in range(5):
            cs, n = chunk_of(c)
            if c:
                ac.wait_ge(X[0].filled, X[0].at(('rS', c - 1)))
            copy_out(X[1], ('rvT', c), lambda x: [(g.r_v[0:n, :], x[0:n, :])])
            if c < 4:
                copy_out(PJ[c % 2], ('aq', c), lambda x: [(halves(g.out_att[:, c, :]), x[:, :, 0:HT])], scale=SCALE)
                next_tile(f'aq{c // 2}', c % 2)
            if c == 4:
                for b in range(DB):
                    ac.wait_ge(X[b % 2].drained, X[b % 2].at(('rS', 4, b)))
                    ac.dma_start(at_layer('s_ret').rearrange("a b h k v -> k (a b) h v")[:, b],
                                 head_view(g.r_sout[b % 2], P)).then_inc(st_rs[b % 2].sem, st_rs[b % 2].next(b, 16))
            copy_out(X[3], ('ro', c), lambda x: [(g.rv[:, :, cs], head_view(x, n))])
            if c == 3:
                ac.wait_ge(vec_out.sem, vec_out.at(('r_state', 3)))
                ac.dma_start(at_layer('p_ret').rearrange("a b h k v -> k (a b h) v"),
                                          head_view(g.r_S, P)).then_inc(st_state.sem, st_state.next('ret', 16))
        for h in range(H):
            ac.wait_ge(vec_out.sem, vec_out.at(('rxc', h)))
            if h:
                ac.wait_ge(PJ[1].filled, PJ[1].at(('rvar', h - 1)))
            act(g.rswap[:, :], g.rraw[:, :], ACT.Square).then_inc(act_out.sem, act_out.next(('rsq', h)))
            copy_out(PJ[0], ('z', h), lambda x: [(halves(g.out_dn[:, h, :]), x[:, :, 0:HT])], f=ACT.Silu)
            next_tile(f'z{h // 2}', h % 2)
            rsqrt(g.rswap[:, :], PJ[1], ('rvar', h), 1.0 / P, ('rrs', h))
            ac.wait_ge(vec_out.sem, vec_out.at(('rout', h)))

        ac.wait_ge(st_state.sem, st_state.at('ret'))
        for i in range(2):
            ac.wait_ge(st_rs[i].sem, st_rs[i].at(DB - 2 + i))
        for nm in ('ak', 'av'):
            for h in range(H):
                dst = g.akv[:, h + (4 if nm == 'av' else 0), :]
                copy_out(PJ[h % 2], (nm, h), lambda x: [(halves(dst), x[:, :, 0:HT])])
                next_tile(f'{nm}{h // 2}', h % 2)
        for c in range(5):
            cs, n = chunk_of(c)
            if c >= 2:
                ac.wait_ge(st_k[c % 2].sem, st_k[c % 2].at(c - 2))
            copy_out(X[0], ('kT', c), lambda x: [(g.ktok[c % 2][0:n, :], x[0:n, :])])
            copy_out(X[1], ('vT', c), lambda x: [(g.vtok[0:n, c, :], x[0:n, :])])
            for nm, sig, src, key in (('k', st_k[c % 2], g.ktok[c % 2][0:n, :], c),
                                      ('v', st_kv, g.vtok[0:n, c, :], 'v' if c == 4 else None)):
                if c < 4:
                    dst = at_layer(f'p_{nm}').rearrange("a b (c p) h d -> (a b c) p (h d)", p=P)[c]
                else:
                    dst = at_layer(f's_{nm}').rearrange("a b t h d -> (a b t) (h d)")
                ac.dma_start(dst, src).then_inc(sig.sem, sig.next(key, 16))
        act(g.s_ak[:, :, :], g.akv[:, 0:4, SEQ:NT]).then_inc(act_steps.sem, act_steps.next())
        ac.wait_ge(act_steps.sem, act_steps.count)
        act(g.s_v[:, :], g.vtok[0:NS, 4, :]).then_inc(act_out.sem, act_out.next('s_kv'))
        ac.wait_ge(act_out.sem, act_out.count)
        steps = [(qb, h) for qb in range(4) for h in range(H)]
        for i in range(len(steps) + 2):
            if i < len(steps):
                n = (steps[i][0] + 1) * P
                ac.wait_ge(vec_out.sem, vec_out.at(('nmax', i)))
                if i >= 2:
                    ac.wait_ge(X[2 + i % 2].filled, X[2 + i % 2].at(('pT', i - 2)))
                act(g.prob[i % 2][:, 0:n], g.logit[i % 2][:, 0:n], ACT.Exp, bias=g.stat[:, 4 + i % 2:5 + i % 2],
                    accum_out=g.stat[:, 6 + i % 2:7 + i % 2]).then_inc(act_out.sem, act_out.next(('exp', i)))
            if 0 < i <= len(steps):
                j = i - 1
                p = g.prob[j % 2][:, 0:(steps[j][0] + 1) * P]
                ac.wait_ge(act_out.sem, act_out.at(('exp', j)))
                ac.wait_ge(vec_out.sem, vec_out.at(('recip', j)))
                act(p, p, scale=g.stat[:, 10 + j % 2:11 + j % 2]).then_inc(act_out.sem, act_out.next(('prob', j)))
            if i > 1:
                j = i - 2
                qb, h = steps[j]
                n = (qb + 1) * P
                copy_out(X[2 + j % 2], ('pT', j), lambda x: [(g.probT[j % 2][:, 0:n], x[:, 0:n])])
                if h == H - 1:
                    copy_out(PJ[qb % 2], ('ao', qb), lambda x: [(g.out_att[:, :, qb * P:qb * P + P],
                                                                 head_view(x[:, 0, :], P))])

        ac.wait_ge(st_kv.sem, st_kv.at('v'))
        ac.wait_ge(st_k[0].sem, st_k[0].at(4))
        ac.wait_ge(st_k[1].sem, st_k[1].at(3))

        def even_pages(half):
            for i in range(NPAGES * half // 24 + 1, NPAGES * (half + 1) // 24 + 1):
                if i % 2 == 0 and i < NPAGES:
                    copy_out(X[0], ('sk', i), lambda x: [(g.kT[0][:, :], x[:, :])])

        def seqs(ap, base, w):
            return ap[:, base:base + DB * w].rearrange("p (b w) -> p b w", b=DB)

        def silu_of(t):
            ac.wait_ge(vec_out.sem, vec_out.at(('conv', t)))
            y = g.d_conv[t % 2]
            act(g.qkv[:, t, 0:SEQ], y[:, 0:SEQ], ACT.Silu).then_inc(act_steps.sem, act_steps.next())
            ac.wait_ge(act_steps.sem, act_steps.count)
            act(g.qkv[:, t, SEQ:NT].rearrange("p (b t) -> p b t", b=DB), seqs(y, 515, 7)[:, :, 0:4], ACT.Silu).then_inc(
                    act_out.sem, act_out.next(('silu', t)))
            ac.wait_ge(act_out.sem, act_out.count)
        ac.wait_ge(vec_out.sem, vec_out.at('d_pads'))
        copy_out(X[0], ('sk', 0), lambda x: [(g.kT[0][:, :], x[:, :])])
        for t in range(12):
            even_pages(2 * t)
            pad = g.d_pad[t % 2]
            if t >= 2:
                ac.wait_ge(vec_out.sem, vec_out.at(('conv', t - 2)))
            copy_out(PJ[t % 2], ('dn', t), lambda x: [
                (pad[:, 3:3 + HT], x[:, 0, 0:HT]), (pad[:, 3 + HT:3 + SEQ], x[:, 1, 0:SEQ - HT]),
                (seqs(pad, 515, 7)[:, :, 3:7], x[:, 1, SEQ - HT:HT].rearrange("p (b t) -> p b t", b=DB))])
            act(seqs(pad, 515, 7)[:, :, 0:3], g.dn_prev[:, t, :].rearrange("p (b i) -> p b i", b=DB)).then_inc(
                    act_out.sem, act_out.next(('pad', t)))
            ac.wait_ge(act_out.sem, act_out.count)
            act(g.dn_last[:, t, 0:3], pad[:, SEQ:SEQ + 3]).then_inc(act_steps.sem, act_steps.next())
            ac.wait_ge(act_steps.sem, act_steps.count)
            act(g.dn_last[:, t, 3:27].rearrange("p (b i) -> p b i", b=DB), seqs(pad, 515, 7)[:, :, 4:7]).then_inc(
                    act_steps.sem, act_steps.next())
            ac.wait_ge(act_steps.sem, act_steps.count)
            even_pages(2 * t + 1)
            next_tile(f'dn{t // 2}', t % 2)
            if t:
                silu_of(t - 1)
        silu_of(11)
        for q in range(2):
            copy_out(X[q], ('srep', q), lambda x: [(g.s_log[:, q * 512:q * 512 + 512], x[:, :])])
        copy_out(X[0], ('srep', 2), lambda x: [(g.s_log[:, PAST:NEWK], x[:, 0:NS])])
        ac.wait_ge(vec_out.sem, vec_out.at('g_arg'))
        act(gBeta, g.small[:, :, 0:4], ACT.Sigmoid).then_inc(act_out.sem, act_out.next('beta'))
        ac.wait_ge(act_out.sem, act_out.count)
        act(gA, gTmp, ACT.Abs).then_inc(act_steps.sem, act_steps.next())
        ac.wait_ge(act_steps.sem, act_steps.count)
        act(gA, gA, ACT.Exp, scale=-1.0).then_inc(act_steps.sem, act_steps.next())
        ac.wait_ge(act_steps.sem, act_steps.count)
        act(gA, gA, ACT.Ln, bias=1.0).then_inc(act_out.sem, act_out.next('conv_done'))
        ac.wait_ge(act_out.sem, act_out.count)

        def l2_square(t):
            if t >= 2:
                ac.wait_ge(PJ[t % 2].filled, PJ[t % 2].at(('l2', t - 2)))
            act(g.d_sq[t % 2], g.qkv[:, t, :], ACT.Square).then_inc(act_out.sem, act_out.next(('l2sq', t)))
        l2_square(0)
        l2_square(1)
        for t in range(0, 8, 2):
            if t == 2:
                ac.wait_ge(vec_out.sem, vec_out.at('s_nmax'))
                act(g.s_log[:, :], g.s_log[:, :], ACT.Exp, bias=g.stat[:, 8:9], accum_out=g.stat[:, 9:10]).then_inc(
                        act_out.sem, act_out.next('s_exp'))
                ac.wait_ge(act_out.sem, act_out.count)
            if t >= 2:
                ac.wait_ge(vec_out.sem, vec_out.at(('l2', t - 1)))
            rsqrt_pair(g.d_rs, [('l2', t), ('l2', t + 1)], 1.0, [('l2rs', t), ('l2rs', t + 1)],
                       [(l2_square, t + 2), (l2_square, t + 3)] if t < 6 else ())
        ac.wait_ge(X[3].filled, X[3].at('gsum'))
        x = X[3].ap
        v16 = lambda at: x[:, at:at + 16].rearrange("p (c h) -> p c h", c=4)
        act(gC[:, 0:4, :], v16(0)).then_inc(act_steps.sem, act_steps.next())
        ac.wait_ge(act_steps.sem, act_steps.count)
        act(gC[0:NS, 4, :], x[0:NS, 16:20]).then_inc(act_steps.sem, act_steps.next())
        ac.wait_ge(act_steps.sem, act_steps.count)
        act(gEK[:, 0:4, :], v16(20), ACT.Exp).then_inc(act_steps.sem, act_steps.next())
        ac.wait_ge(act_steps.sem, act_steps.count)
        act(gEK[0:NS, 4, :], x[0:NS, 36:40], ACT.Exp).then_inc(X[3].drained, 1)
        ac.wait_ge(X[3].drained, X[3].at('gsum'))
        act(gBE[:, 0:4, :], gC[:, 0:4, :], ACT.Exp).then_inc(act_steps.sem, act_steps.next())
        ac.wait_ge(act_steps.sem, act_steps.count)
        act(gBE[0:NS, 4, :], gC[0:NS, 4, :], ACT.Exp).then_inc(act_out.sem, act_out.next('gexp'))
        ac.wait_ge(act_out.sem, act_out.count)
        for q in range(2):
            copy_out(X[2 + q], ('spT', q), lambda x: [(g.s_pT[:, q * 4:q * 4 + 4, :],
                                                       x[:, :].rearrange("p (g n) -> p g n", g=4))])
        copy_out(X[0], 'spT_new', lambda x: [(g.s_pT[0:NS, NPG, :], x[0:NS, 0:P])])
        copy_out(X[1], 's_new', lambda x: [(g.s_new, x[:, 0:P])])
        for c in range(5):
            if c == 4:
                for i in range(2):
                    copy_out(X[i], ('s_oT', i), lambda x: [
                        (g.out_att[:, :, SEQ + b * DS:SEQ + b * DS + DS],
                         head_view(x[:, (b % 4) * P:(b % 4) * P + P], NS)[:, :, b * DS:b * DS + DS])
                        for b in range(4 * i, 4 * i + 4)])
            cs, n = chunk_of(c)
            ac.wait_ge(vec_out.sem, vec_out.at(('dif', c)))
            act(g.d_dec[0:n, 0:4 * n], g.d_dec[0:n, 0:4 * n], ACT.Exp).then_inc(act_out.sem, act_out.next(('dec', c)))
            ac.wait_ge(act_out.sem, act_out.count)
            if c:
                ac.wait_ge(X[0].drained, X[0].at(('dS', c - 1)))
            copy_out(X[1], ('grow', c), lambda x: [(g.d_eg[:, 0:4 * n], x[:, 0:4 * n])], f=ACT.Exp)
            for s in (LEVELS if c < 4 else LEVELS[:2]):
                copy_out(X[2], ('Y', c, s), lambda x: [(g.d_y[0:n, 0:4 * n], x[0:n, 0:4 * n])])
            copy_out(X[1], ('kc', c), lambda x: [(g.d_kc[:, 0:4 * n], x[:, 0:4 * n])])
            if c < 4:
                copy_out(X[2], ('dw', c), lambda x: [(g.d_w[:, :], x[:, :])])
            else:
                copy_out(X[2], ('dw', c), lambda x: [(g.d_eg[:, 128:256], x[:, 0:P])])
                copy_out(X[1], 'dwT', lambda x: [(g.d_w[0:NS, :], x[0:NS, :])])
            copy_out(X[3], ('do', c), lambda x: [(g.qkv[:, 8:12, cs], head_view(x, n))])
            if c == 3:
                ac.wait_ge(vec_out.sem, vec_out.at(('d_state', 3)))
                ac.dma_start(at_layer('p_dn').rearrange("a b h k v -> k (a b h) v"),
                                          head_view(g.d_S, P)).then_inc(st_state.sem, st_state.next('dn', 16))
        for b in range(DB):
            ac.wait_ge(X[b % 2].drained, X[b % 2].at(('dS', 4, b)))
            ac.dma_start(at_layer('s_dn').rearrange("a b h k v -> k (a b) h v")[:, b],
                                      head_view(g.d_sout[b % 2], P)).then_inc(st_ds[b % 2].sem, st_ds[b % 2].next(b, 16))

        def out_square(h):
            if h == 1:
                ac.wait_ge(st_ds[0].sem, st_ds[0].at(DB - 2))
            if h >= 2:
                ac.wait_ge(PJ[h % 2].filled, PJ[h % 2].at(('dvar', h - 2)))
            act(g.d_sq[h % 2], g.qkv[:, 8 + h, :], ACT.Square).then_inc(act_out.sem, act_out.next(('dsq', h)))
        out_square(0)
        out_square(1)
        for h in range(0, H, 2):
            if h:
                ac.wait_ge(vec_out.sem, vec_out.at(('dout', h - 1)))
            rsqrt_pair(g.d_rs, [('dvar', h), ('dvar', h + 1)], 1.0 / P, [('drs', h), ('drs', h + 1)],
                       [(out_square, h + 2), (out_square, h + 3)] if h < H - 2 else ())
        for i, st in enumerate((g.d_t, g.d_tt, g.d_y)):
            copy_out(X[i], ('dn_last', i), lambda x: [(st[0:27, :], x[0:27, :])])
            ac.dma_start(at_layer('p_dn_conv').rearrange("a b i n -> (a b i) n")[:, i * 512:i * 512 + 512],
                                   st[0:3, :]).then_inc(st_dn.sem, st_dn.next(by=16))
            ac.dma_start(at_layer('s_dn_conv').rearrange("a b i n -> (a b i) n")[:, i * 512:i * 512 + 512],
                                   st[3:27, :]).then_inc(st_dn.sem, st_dn.next(i, 16))

        ac.wait_ge(vec_out.sem, vec_out.at(('dout', 3)))
        ac.wait_ge(st_state.sem, st_state.at('dn'))
        for i in range(2):
            ac.wait_ge(st_ds[i].sem, st_ds[i].at(DB - 2 + i))
        ac.wait_ge(st_dn.sem, st_dn.at(2))
        outs = (g.out_dn, g.out_ret, g.out_att)

        def bsplit(n):
            if n == 2:
                ac.wait_ge(PJ[1].filled, PJ[1].at(('br', 0, 3, 1)))
            act(g.bhi[n % 2][:, :, :], outs[n][:, :, :]).then_inc(act_out.sem, act_out.next(('bsplit', n)))
            ac.wait_ge(act_out.sem, act_out.count)
        bsplit(0)
        bsplit(1)
        i = 0
        for n in range(3):
            if n == 1:
                bsplit(2)
            for d in range(4):
                for j in range(2):
                    if i >= 2:
                        ac.wait_ge(vec_out.sem, vec_out.at(('mul', i - 2)))
                    copy_out(PJ[0], ('gate', n, d, j), lambda x: [(halves(g.sig[i % 2][:, :]), x[:, :, 0:HT])],
                             f=ACT.Sigmoid)
                    i += 1
                    next_tile(f'gate{n}{d}', j)
                    next_tile(f'br{n}{d}', j)
        for k in range(KD):
            ac.wait_ge(vec_out.sem, vec_out.at(('m', k)))
            act(g.uhi[:, k, :], g.m[:, k, :]).then_inc(act_out.sem, act_out.next(('msplit', k)))
            ac.wait_ge(act_out.sem, act_out.count)
        for i in range(4):
            next_tile(f'wo{i}', 0)
            next_tile(f'wo{i}', 1)
        for k in range(KD):
            ac.wait_ge(vec_out.sem, vec_out.at(('h', k)))
            if k >= 2:
                ac.wait_ge(pe_out.sem, pe_out.at(('rms1', k - 2)))
            act(g.f_sq if k % 2 == 0 else g.f_rs, g.x[:, k, :], ACT.Square).then_inc(
                    act_out.sem, act_out.next(('hsq', k)))
            ac.wait_ge(act_out.sem, act_out.count)
        rsqrt(g.f_act[:, :], PJ[0], 'rms1', 1.0 / D, 'rstd1')
        for k in range(KD):
            ac.wait_ge(vec_out.sem, vec_out.at(('hf', k)))
            act(g.uhi[:, k, :], g.f_conv[k % 2][:, 0:NT]).then_inc(act_out.sem, act_out.next(('hh', k)))
            ac.wait_ge(act_out.sem, act_out.count)

        ac.wait_ge(vec_out.sem, vec_out.at('f_pads'))
        for f in range(2):
            for j in range(FH):
                for i in range(2):
                    pad, t = g.f_pad[i], f * FH + j + i * FT
                    if (f, j) != (0, 0):
                        ac.wait_ge(vec_out.sem, vec_out.at(('fconv', *divmod(f * FH + j - 1, FH), i)))
                    copy_out(PJ[i], ('up', f, j, i), lambda x: [
                        (pad[:, 2:2 + HT], x[:, 0, 0:HT]), (pad[:, 2 + HT:2 + SEQ], x[:, 1, 0:SEQ - HT]),
                        (seqs(pad, 514, 6)[:, :, 2:6], x[:, 1, SEQ - HT:HT].rearrange("p (b t) -> p b t", b=DB))])
                    act(seqs(pad, 514, 6)[:, :, 0:2], g.ffn_prev[:, t, :].rearrange("p (b i) -> p b i", b=DB)).then_inc(
                            act_out.sem, act_out.next(('fpad', f, j, i)))
                    ac.wait_ge(act_out.sem, act_out.count)
                    act(g.ffn_last[:, t, 0:2], pad[:, SEQ:SEQ + 2]).then_inc(act_steps.sem, act_steps.next())
                    ac.wait_ge(act_steps.sem, act_steps.count)
                    act(g.ffn_last[:, t, 2:18].rearrange("p (b i) -> p b i", b=DB), seqs(pad, 514, 6)[:, :, 4:6]).then_inc(
                            act_steps.sem, act_steps.next())
                    ac.wait_ge(act_steps.sem, act_steps.count)
                    next_tile(f'up{f}_{j}', i)
                ac.wait_ge(vec_out.sem, vec_out.at(('fconv', f, j, 0)))
                if (f, j) != (0, 0):
                    ac.wait_ge(vec_out.sem, vec_out.at(('hff', *divmod(f * FH + j - 1, FH))))
                y = g.f_conv[0]
                act(g.f_act[:, 0:SEQ], y[:, 0:SEQ], ACT.Silu).then_inc(act_steps.sem, act_steps.next())
                ac.wait_ge(act_steps.sem, act_steps.count)
                act(g.f_act[:, SEQ:NT].rearrange("p (b t) -> p b t", b=DB), seqs(y, 514, 6)[:, :, 0:4], ACT.Silu).then_inc(
                        act_out.sem, act_out.next(('fsilu', f, j)))
                ac.wait_ge(act_out.sem, act_out.count)
                ac.wait_ge(vec_out.sem, vec_out.at(('hprod', f, j)))
                if f == 1 and j == 0:
                    ac.wait_ge(PJ[1].filled, PJ[1].at(('down', 0, 7)))
                act(g.hhi[:, j, :], g.f_act[:, :]).then_inc(act_out.sem, act_out.next(('hhi', f, j)))
                ac.wait_ge(act_out.sem, act_out.count)
            if f == 1:
                act(g.stat[:, 0:1], g.eps()).then_inc(act_out.sem, act_out.next('ffn_last'))
                ac.wait_ge(vec_out.sem, vec_out.at(('hff', 1, FH - 1)))
            for c in range(KD):
                next_tile(f'down{f}_{c}', 0)
                next_tile(f'down{f}_{c}', 1)
                for i in range(LAST * c // KD, LAST * (c + 1) // KD) if f else ():
                    st = (*g.f_pad, *g.f_conv)[i % 4]
                    if i >= 4:
                        ac.wait_ge(st_ffn[i % 4].sem, st_ffn[i % 4].at(i - 4))
                    copy_out(X[i % 4], ('ffn_last', i), lambda x: [(st[0:18, 0:512], x[0:18, :])])
                    for nm, lo_, hi_ in (('p_ffn_conv', 0, 2), ('s_ffn_conv', 2, 18)):
                        dst = at_layer(nm).rearrange("a b i n -> (a b i) n")[:, i * 512:i * 512 + 512]
                        ac.dma_start(dst, st[lo_:hi_, 0:512]).then_inc(
                            st_ffn[i % 4].sem, st_ffn[i % 4].next(i if hi_ == 18 else None, 16))
        for i in range(LAST - 4, LAST):
            ac.wait_ge(st_ffn[i % 4].sem, st_ffn[i % 4].at(i))

    @g.block.vector
    def _(ve):
        tt, stt, ts = ve.tensor_tensor, ve.scalar_tensor_tensor, ve.tensor_scalar
        par = lambda n, i=0: g.par[:, (PAR0[n] if n in PAR0 else PAR0_N + PAR1[n]) + i:][:, 0:1]

        def bcast(ap, n):
            return ap.unsqueeze(2).to_broadcast([ap.shape[0], ap.shape[1], n])

        def over_heads(ap):
            return ap.unsqueeze(1).to_broadcast([ap.shape[0], H, ap.shape[1]])

        ve.memset(g.small[:, 4, :], 0.0).then_inc(vec_out.sem, vec_out.next('small_zero'))
        ve.wait_ge(vec_out.sem, vec_out.count)
        for k in range(KD):
            ve.wait_ge(act_out.sem, act_out.at(('sq', k)))
            if k == 0:
                ve.tensor_copy(g.xsum[:, :], g.xsq[0][:, :]).then_inc(vec_out.sem, vec_out.next(('sq', k)))
            else:
                tt(g.xsum[:, :], g.xsum[:, :], g.xsq[k % 2][:, :], ALU.add).then_inc(
                    vec_out.sem, vec_out.next(('sq', k) if k < KD - 1 else 'squares'))
            ve.wait_ge(vec_out.sem, vec_out.count)
        ve.wait_ge(X[0].drained, X[0].at('par0'))
        ve.wait_ge(act_out.sem, act_out.at('rstd0'))
        for k in range(KD):
            stt(g.x[:, k, :], g.x[:, k, :], par('mix', k), g.rstd0[:, :], ALU.mult, ALU.mult).then_inc(
                    vec_out.sem, vec_out.next(('uf', k)))
            ve.wait_ge(vec_out.sem, vec_out.count)
            if k:
                ve.wait_ge(act_out.sem, act_out.at(('uh', k - 1)))
                tt(g.ulo[:, k - 1, :], g.x[:, k - 1, :], g.uhi[:, k - 1, :].bitcast(F32), ALU.subtract).then_inc(
                        vec_out.sem, vec_out.next(('u', k - 1)))
                ve.wait_ge(vec_out.sem, vec_out.count)
        ve.wait_ge(act_out.sem, act_out.at(('uh', KD - 1)))
        tt(g.ulo[:, KD - 1, :], g.x[:, KD - 1, :], g.uhi[:, KD - 1, :].bitcast(F32), ALU.subtract).then_inc(
                vec_out.sem, vec_out.next(('u', KD - 1)))
        ve.wait_ge(vec_out.sem, vec_out.count)

        ve.wait_ge(X[1].drained, X[1].at('small'))
        w = g.gate[:, 6]
        ts(w, g.small[:, :, 8:12], 1.0 / 16.0, None, ALU.mult).then_inc(vec_steps.sem, vec_steps.next())
        ve.wait_ge(vec_steps.sem, vec_steps.count)
        ve.tensor_copy(g.sel[:, 0:P], const('causal')).then_inc(vec_steps.sem, vec_steps.next())
        ve.wait_ge(vec_steps.sem, vec_steps.count)
        def choose_rounds(sc, first, last):
            mx = g.mx[0:sc.shape[0], :]
            for _ in range(first, last):
                ve.max(mx, sc).then_inc(vec_steps.sem, vec_steps.next())
                ve.wait_ge(vec_steps.sem, vec_steps.count)
                ve.match_replace(sc, mx, sc, TAKEN).then_inc(vec_steps.sem, vec_steps.next())
                ve.wait_ge(vec_steps.sem, vec_steps.count)

        def chosen(sc, key=None):
            ts(sc, sc, TAKEN / 1.5, NEG, ALU.is_gt, ALU.mult).then_inc(vec_out.sem, vec_out.next(key))
            ve.wait_ge(vec_out.sem, vec_out.count)

        def choose_prompt(qb):
            sc = g.sel[:, g.selat[qb]:g.selat[qb] + (qb + 1) * P]
            choose_rounds(sc, 0, TOPK_P // 8)
            chosen(sc)

        def prompt_scores(i):
            qb, h = i // H + 1, i % H
            n = (qb + 1) * P
            sc = g.sel[:, g.selat[qb]:g.selat[qb] + n]
            ve.wait_ge(X[2 + i % 2].drained, X[2 + i % 2].at(('is', qb, h)))
            r = g.relu_p[i % 2][:, 0:n]
            if h == 0:
                ts(sc, r, w[:, qb, h:h + 1], None, ALU.mult).then_inc(vec_out.sem, vec_out.next(('score', i)))
            else:
                stt(sc, r, w[:, qb, h:h + 1], sc, ALU.mult, ALU.add).then_inc(vec_out.sem, vec_out.next(('score', i)))
            ve.wait_ge(vec_out.sem, vec_out.count)
            if h == H - 1:
                tt(sc[:, n - P:n], sc[:, n - P:n], const('causal'), ALU.add).then_inc(vec_steps.sem, vec_steps.next())
                ve.wait_ge(vec_steps.sem, vec_steps.count)

        def sample_scores(b):
            bank = X[2 + b % 2]
            ve.wait_ge(bank.filled, bank.at(('sT', b)))
            stt(g.sprod[:, :, :], bank.ap[:, 0:P].rearrange("p (g n) -> p g n", g=NPG), 0.0,
                g.wrow[:, b, :].unsqueeze(1).to_broadcast([P, NPG, 16]), ALU.max, ALU.mult).then_inc(bank.drained, 1)
            ve.wait_ge(bank.drained, bank.at(('sT', b)))
            ve.tensor_reduce(g.scoreT[:, :, b * DS:b * DS + DS],
                             g.sprod[:, :, :].rearrange("p g (h t) -> p g t h", h=H), AX.X, ALU.add).then_inc(
                vec_out.sem, vec_out.next('scoreT' if b == DB - 1 else None))
            ve.wait_ge(vec_out.sem, vec_out.count)

        ve.wait_ge(X[2].drained, X[2].at('wrow'))
        for t in range(16):
            if t < 12:
                prompt_scores(t)
            if t < 8:
                nm, h = ('rq', 'rk')[t // H], t % H
                ve.wait_ge(PJ[h % 2].drained, PJ[h % 2].at((nm, h)))
                dst = g.rqk[:, t, :]
                tt(dst, g.rraw[:, :], const('cos'), ALU.mult).then_inc(vec_steps.sem, vec_steps.next())
                tt(g.rswap[:, :], g.rswap[:, :], const('sin'), ALU.mult).then_inc(vec_steps.sem, vec_steps.next())
                ve.wait_ge(vec_steps.sem, vec_steps.count)
                tt(dst, dst, g.rswap[:, :], ALU.add).then_inc(vec_out.sem, vec_out.next((nm, h)))
                ve.wait_ge(vec_out.sem, vec_out.count)
            if t and t % 2 == 0:
                sample_scores(t // 2 - 1)
            if t in (8, 12):
                choose_prompt(1 if t == 8 else 2)
        sample_scores(DB - 1)
        ve.wait_ge(X[0].drained, X[0].at('s_new'))
        new = g.sel_s[:, PAST:NEWK]
        ws = g.small[0:NS, 4, 8:12]
        for h in range(H):
            r = g.relu_s[:, h * NS:h * NS + NS]
            if h == 0:
                ts(new, r, ws[:, h:h + 1], None, ALU.mult).then_inc(vec_steps.sem, vec_steps.next())
                ve.wait_ge(vec_steps.sem, vec_steps.count)
            else:
                stt(new, r, ws[:, h:h + 1], new, ALU.mult, ALU.add).then_inc(vec_steps.sem, vec_steps.next())
                ve.wait_ge(vec_steps.sem, vec_steps.count)
        tt(new, new, const('causal_s', NS)[:, 0:NS], ALU.add).then_inc(vec_out.sem, vec_out.next('index_done'))
        ve.wait_ge(vec_out.sem, vec_out.count)

        ve.wait_ge(X[2].filled, X[2].at(('s_score', 1)))
        ve.wait_ge(st_idx.sem, st_idx.at('all'))
        ve.memset(g.r_S[:, :], 0.0).then_inc(vec_steps.sem, vec_steps.next())
        ve.wait_ge(vec_steps.sem, vec_steps.count)
        gt = [float(np.exp(np.log1p(-2.0 ** (-5.0 - h)) * P)) for h in range(H)]
        gt_s = [float(np.exp(np.log1p(-2.0 ** (-5.0 - h)) * DS)) for h in range(H)]
        for c in range(5):
            cs, n = chunk_of(c)
            rk_, rq_, dc = ('r_k', 'r_q', 'r_decay') if c < 4 else ('rs_k', 'rs_q', 'rs_decay')
            ve.wait_ge(X[0].filled, X[0].at(('rkT', c)))
            x = X[0].ap
            tt(head_view(g.r_kd[0:n, :], P), head_view(x[0:n, :], P), bcast(const(rk_, n), P), ALU.mult).then_inc(
                    X[0].drained, 1)
            ve.wait_ge(X[0].drained, X[0].at(('rkT', c)))
            tt(head_view(g.r_qd, n), g.rqk[:, 0:4, cs], head_view(const(rq_), n), ALU.mult).then_inc(
                    vec_steps.sem, vec_steps.next())
            ve.wait_ge(vec_steps.sem, vec_steps.count)
            ve.wait_ge(X[2].filled, X[2].at(('rqk', c)))
            x = X[2].ap
            tt(g.r_qk[0:n, 0:4 * n], x[0:n, 0:4 * n], const(dc, n), ALU.mult).then_inc(X[2].drained, 1)
            ve.wait_ge(X[2].drained, X[2].at(('rqk', c)))
            ve.engine_nop().then_inc(vec_out.sem, vec_out.next(('r_in', c)))
            ve.wait_ge(vec_out.sem, vec_out.count)
            if c < 4:
                ve.wait_ge(X[0].filled, X[0].at(('rS', c)))
                x = X[0].ap
                for h in range(H):
                    hs = slice(h * P, h * P + P)
                    ins = stt(g.r_S[:, hs], g.r_S[:, hs], gt[h], x[:, hs], ALU.mult, ALU.add)
                    if h < H - 1:
                        ins.then_inc(vec_steps.sem, vec_steps.next())
                        ve.wait_ge(vec_steps.sem, vec_steps.count)
                    else:
                        ins.then_inc(X[0].drained, 1)
                        ve.wait_ge(X[0].drained, X[0].at(('rS', c)))
                ve.engine_nop().then_inc(vec_out.sem, vec_out.next(('r_state', c)))
                ve.wait_ge(vec_out.sem, vec_out.count)
            else:
                def masked(b):
                    ts(g.r_kdm[b % 2], g.r_kd[0:NS, :], const('seq_of', NS)[:, b:b + 1], None, ALU.mult).then_inc(
                        vec_out.sem, vec_out.next(('kdm', b)))
                masked(0)
                for b in range(DB):
                    ve.wait_ge(X[b % 2].filled, X[b % 2].at(('rS', c, b)))
                    if b < DB - 1:
                        masked(b + 1)
                    if b == 1:
                        ve.wait_ge(st_state.sem, st_state.at('ret'))
                    if b >= 2:
                        ve.wait_ge(st_rs[b % 2].sem, st_rs[b % 2].at(b - 2))
                    x = X[b % 2].ap
                    for h in range(H):
                        hs = slice(h * P, h * P + P)
                        ins = stt(g.r_sout[b % 2][:, hs], g.r_sin[b % 2][:, hs], gt_s[h], x[:, hs], ALU.mult, ALU.add)
                        if h < H - 1:
                            ins.then_inc(vec_steps.sem, vec_steps.next())
                        else:
                            ins.then_inc(X[b % 2].drained, 1)
        ve.wait_ge(st_rs[0].sem, st_rs[0].at(DB - 2))
        for h in range(H):
            ve.wait_ge(PJ[0].filled, PJ[0].at(('rmean', h)))
            x = PJ[0].ap
            stt(halves(g.rraw[:, :]), x[:, :, 0:HT], -1.0 / P, halves(g.rv[:, h, :]), ALU.mult, ALU.add).then_inc(
                    PJ[0].drained, 1)
            ve.wait_ge(PJ[0].drained, PJ[0].at(('rmean', h)))
            ve.engine_nop().then_inc(vec_out.sem, vec_out.next(('rxc', h)))
            ve.wait_ge(vec_out.sem, vec_out.count)
            choose_rounds(g.sel_s, 3 * h, 3 * h + 3)
            ve.wait_ge(act_out.sem, act_out.at(('rrs', h)))
            stt(g.rraw[:, :], g.rraw[:, :], par('retn', h), g.rswap[:, :], ALU.mult, ALU.mult).then_inc(
                    vec_steps.sem, vec_steps.next())
            ve.wait_ge(vec_steps.sem, vec_steps.count)
            tt(g.out_ret[:, h, :], g.out_ret[:, h, :], g.rraw[:, :], ALU.mult).then_inc(
                    vec_out.sem, vec_out.next(('rout', h)))
            ve.wait_ge(vec_out.sem, vec_out.count)

        choose_prompt(3)
        choose_rounds(g.sel_s, 3 * H, ROUNDS_S - 10)
        steps = [(qb, h) for qb in range(4) for h in range(H)]
        for i in range(len(steps) + 1):
            if i < len(steps):
                qb, h = steps[i]
                n = (qb + 1) * P
                ve.wait_ge(X[i % 2].filled, X[i % 2].at(('qk', i)))
                x = X[i % 2].ap
                L = g.logit[i % 2]
                tt(L[:, 0:n], x[:, 0:n], g.sel[:, g.selat[qb]:g.selat[qb] + n], ALU.add).then_inc(X[i % 2].drained, 1)
                ve.wait_ge(X[i % 2].drained, X[i % 2].at(('qk', i)))
                m = min(n, 2 * P)
                tt(L[:, n - m:n], L[:, n - m:n], g.bias_near[:, h, 2 * P - m:2 * P], ALU.add).then_inc(
                        vec_steps.sem, vec_steps.next())
                ve.wait_ge(vec_steps.sem, vec_steps.count)
                ve.tensor_reduce(g.stat[:, 4 + i % 2:5 + i % 2], L[:, 0:n], AX.X, ALU.max, negate=True).then_inc(
                        vec_out.sem, vec_out.next(('nmax', i)))
                ve.wait_ge(vec_out.sem, vec_out.count)
            if i:
                j = i - 1
                n = (steps[j][0] + 1) * P
                ve.wait_ge(act_out.sem, act_out.at(('exp', j)))
                r = g.stat[:, 10 + j % 2:11 + j % 2]
                ve.reciprocal(r, g.stat[:, 6 + j % 2:7 + j % 2]).then_inc(vec_out.sem, vec_out.next(('recip', j)))

        ve.wait_ge(PJ[1].drained, PJ[1].at(('ao', 3)))
        ve.wait_ge(st_kv.sem, st_kv.at('v'))
        ve.wait_ge(st_k[0].sem, st_k[0].at(4))
        ve.wait_ge(st_k[1].sem, st_k[1].at(3))

        def odd_pages(half):
            for i in range(NPAGES * half // 24 + 1, NPAGES * (half + 1) // 24 + 1):
                if i % 2:
                    ve.wait_ge(X[1].filled, X[1].at(('sk', i)))
                    ve.tensor_copy(g.kT[1][:, :], X[1].ap[:, :]).then_inc(X[1].drained, 1)
                    ve.wait_ge(X[1].drained, X[1].at(('sk', i)))

        ve.wait_ge(X[2].drained, X[2].at(('s_score', 1)))
        ve.memset(g.s_q[:, :, :], 0.0).then_inc(vec_steps.sem, vec_steps.next())
        ve.wait_ge(vec_steps.sem, vec_steps.count)
        ve.tensor_copy(g.s_q[:, :, :].rearrange("p h (b n) -> p h b n", b=DB)[:, :, :, 0:DS],
                       g.out_att[:, :, SEQ:NT].rearrange("p h (b t) -> p h b t", b=DB)).then_inc(
            vec_out.sem, vec_out.next('s_q'))
        ve.wait_ge(vec_out.sem, vec_out.count)
        ve.memset(g.d_pad[0][:, 0:3], 0.0).then_inc(vec_steps.sem, vec_steps.next())
        ve.wait_ge(vec_steps.sem, vec_steps.count)
        ve.memset(g.d_pad[1][:, 0:3], 0.0).then_inc(vec_out.sem, vec_out.next('d_pads'))
        ve.wait_ge(vec_out.sem, vec_out.count)
        for t in range(12):
            odd_pages(2 * t)
            odd_pages(2 * t + 1)
            if t < 10:
                choose_rounds(g.sel_s, ROUNDS_S - 10 + t, ROUNDS_S - 9 + t)
            ve.wait_ge(act_out.sem, act_out.at(('pad', t)))
            if t >= 2:
                ve.wait_ge(act_out.sem, act_out.at(('silu', t - 2)))
            src, y = g.d_pad[t % 2], g.d_conv[t % 2][:, 0:DW - 3]
            ts(y, src[:, 0:DW - 3], par('dc', t), None, ALU.mult).then_inc(vec_steps.sem, vec_steps.next())
            ve.wait_ge(vec_steps.sem, vec_steps.count)
            for i in range(1, 4):
                stt(y, src[:, i:i + DW - 3], par('dc', i * 12 + t), y, ALU.mult, ALU.add).then_inc(
                        vec_out.sem, vec_out.next(('conv', t) if i == 3 else None))
                ve.wait_ge(vec_out.sem, vec_out.count)
        chosen(g.sel_s, 'sel_s')
        ve.wait_ge(X[0].drained, X[0].at(('srep', 2)))
        ve.wait_ge(X[1].drained, X[1].at(('srep', 1)))
        L = g.s_log
        for q in range(2):
            ve.wait_ge(X[2 + q].filled, X[2 + q].at(('slog', q)))
            x = X[2 + q].ap
            tt(L[:, q * 512:q * 512 + 512], L[:, q * 512:q * 512 + 512], x[:, :], ALU.add).then_inc(
                    X[2 + q].drained, 1)
            ve.wait_ge(X[2 + q].drained, X[2 + q].at(('slog', q)))
        ve.wait_ge(X[1].filled, X[1].at('snew'))
        x = X[1].ap
        tt(L[:, PAST:NEWK], L[:, PAST:NEWK], x[:, 0:NS], ALU.add).then_inc(X[1].drained, 1)
        ve.wait_ge(X[1].drained, X[1].at('snew'))
        tt(L[:, PAST - P:NEWK], L[:, PAST - P:NEWK], g.bias_s[:, :], ALU.add).then_inc(
                vec_steps.sem, vec_steps.next())
        ve.wait_ge(vec_steps.sem, vec_steps.count)
        ve.tensor_reduce(g.stat[:, 8:9], L[:, :], AX.X, ALU.max, negate=True).then_inc(
                vec_out.sem, vec_out.next('s_nmax'))
        ve.wait_ge(vec_out.sem, vec_out.count)
        tt(gTmp, g.small[:, :, 4:8], g.lrow[:, 1, :].unsqueeze(1).to_broadcast([P, 5, H]), ALU.add).then_inc(
                vec_out.sem, vec_out.next('g_arg'))
        ve.wait_ge(vec_out.sem, vec_out.count)
        ve.wait_ge(act_out.sem, act_out.at('conv_done'))
        stt(gTmp, gTmp, 0.0, gA, ALU.max, ALU.add).then_inc(vec_steps.sem, vec_steps.next())
        ve.wait_ge(vec_steps.sem, vec_steps.count)
        stt(gG, gTmp, -1.0, g.gate[:, 7, 0, :].unsqueeze(1).to_broadcast([P, 5, H]), ALU.mult, ALU.mult).then_inc(
                vec_out.sem, vec_out.next('g'))
        ve.wait_ge(vec_out.sem, vec_out.count)
        for t in range(8):
            if t == 4:
                ve.wait_ge(act_out.sem, act_out.at('s_exp'))
                ve.reciprocal(g.stat[:, 12:13], g.stat[:, 9:10]).then_inc(vec_steps.sem, vec_steps.next())
                ve.wait_ge(vec_steps.sem, vec_steps.count)
                ts(L[:, :], L[:, :], g.stat[:, 12:13], None, ALU.mult).then_inc(vec_out.sem, vec_out.next('s_prob'))
                ve.wait_ge(vec_out.sem, vec_out.count)
            ve.wait_ge(act_out.sem, act_out.at(('l2rs', t)))
            q = g.qkv[:, t, :]
            stt(q, q, SCALE if t < 4 else 1.0, g.d_rs[t % 2], ALU.mult, ALU.mult).then_inc(
                    vec_out.sem, vec_out.next(('l2', t)))
            ve.wait_ge(vec_out.sem, vec_out.count)
        ve.wait_ge(act_out.sem, act_out.at('gexp'))
        ve.wait_ge(X[0].filled, X[0].at('spT_new'))
        stt(gBE[:, 0:4, :], gBE[:, 0:4, :], -1.0, gBeta[:, 0:4, :], ALU.mult, ALU.mult).then_inc(
                vec_steps.sem, vec_steps.next())
        ve.wait_ge(vec_steps.sem, vec_steps.count)
        stt(gBE[0:NS, 4, :], gBE[0:NS, 4, :], -1.0, gBeta[0:NS, 4, :], ALU.mult, ALU.mult).then_inc(
                vec_steps.sem, vec_steps.next())
        ve.wait_ge(vec_steps.sem, vec_steps.count)
        ve.memset(g.d_S[:, :], 0.0).then_inc(vec_steps.sem, vec_steps.next())
        ve.wait_ge(vec_steps.sem, vec_steps.count)

        def block_part(c, n, li):
            tt(head_view(g.d_lm[0:n, :], n), head_view(g.d_mt[0:n, 0:4 * n], n),
               over_heads(const('level', n)[:, li * P:li * P + n]), ALU.mult).then_inc(
                vec_out.sem, vec_out.next(('lm', c, LEVELS[li])))
            ve.wait_ge(vec_out.sem, vec_out.count)

        for c in range(5):
            if c == 4:
                ve.wait_ge(PJ[0].filled, PJ[0].at('so'))
                for i in range(2):
                    inst = tt(g.s_o[i].rearrange("p (b n) -> p b n", b=4),
                              PJ[0].ap[:, i, :].rearrange("p (b n) -> p b n", b=4),
                              g.s_new.unsqueeze(1).to_broadcast([P, 4, P]), ALU.add)
                    if i == 0:
                        inst.then_inc(vec_steps.sem, vec_steps.next())
                        ve.wait_ge(vec_steps.sem, vec_steps.count)
                    else:
                        inst.then_inc(PJ[0].drained, 1)
                        ve.wait_ge(PJ[0].drained, PJ[0].at('so'))
                ve.engine_nop().then_inc(vec_out.sem, vec_out.next('s_o'))
            cs, n = chunk_of(c)
            tri = const('triu') if c < 4 else const('triu_s', NS)[:, 0:NS]
            t_, tT = g.d_t[0:n, 0:4 * n], g.d_tt[0:n, 0:4 * n]
            for y in (t_, tT):
                ve.tensor_copy(head_view(y, n), over_heads(ident[0:n, 0:n])).then_inc(vec_steps.sem, vec_steps.next())
                ve.wait_ge(vec_steps.sem, vec_steps.count)
            ve.wait_ge(X[1].filled, X[1].at(('grow', c)))
            x = X[1].ap
            for h in range(H):
                ts(g.d_dec[0:n, h * n:h * n + n], x[0:n, h * n:h * n + n], gC[0:n, c, h:h + 1], 0.0,
                        ALU.subtract, ALU.min).then_inc(vec_out.sem, vec_out.next(('dif', c) if h == 3 else None))
                ve.wait_ge(vec_out.sem, vec_out.count)
            ve.wait_ge(act_out.sem, act_out.at(('dec', c)))
            dec = head_view(g.d_dec[0:n, :], n)
            tt(dec, dec, over_heads(tri), ALU.mult).then_inc(vec_steps.sem, vec_steps.next())
            ve.wait_ge(vec_steps.sem, vec_steps.count)
            mt = g.d_mt[0:n, 0:4 * n]
            ve.wait_ge(X[2].filled, X[2].at(('kk', c)))
            x = X[2].ap
            tt(mt, g.d_dec[0:n, 0:4 * n], x[0:n, 0:4 * n], ALU.mult).then_inc(X[2].drained, 1)
            ve.wait_ge(X[2].drained, X[2].at(('kk', c)))
            ve.wait_ge(X[0].filled, X[0].at(('betarow', c)))
            x = X[0].ap
            tt(mt, mt, x[0:n, 0:4 * n], ALU.mult).then_inc(X[0].drained, 1)
            ve.wait_ge(X[0].drained, X[0].at(('betarow', c)))
            ve.wait_ge(X[3].filled, X[3].at(('kq', c)))
            x = X[3].ap
            tt(g.d_dec[0:n, 0:4 * n], g.d_dec[0:n, 0:4 * n], x[0:n, 0:4 * n], ALU.mult).then_inc(X[3].drained, 1)
            ve.wait_ge(X[3].drained, X[3].at(('kq', c)))
            levels = LEVELS if c < 4 else LEVELS[:2]
            for li, s in enumerate(levels):
                if li == 0:
                    block_part(c, n, 0)
                if s != levels[-1]:
                    ve.wait_ge(X[2].filled, X[2].at(('Y', c, s)))
                    block_part(c, n, li + 1)
                    ve.wait_ge(X[3].filled, X[3].at(('TY', c, s)))
                    x = X[3].ap
                    tt(t_, t_, x[0:n, 0:4 * n], ALU.subtract).then_inc(X[3].drained, 1)
                    ve.wait_ge(X[3].drained, X[3].at(('TY', c, s)))
                ve.wait_ge(X[0].filled, X[0].at(('YT', c, s)))
                x = X[0].ap
                tt(tT, tT, x[0:n, 0:4 * n], ALU.subtract).then_inc(X[0].drained, 1)
                ve.wait_ge(X[0].drained, X[0].at(('YT', c, s)))
                if li == 0:
                    ve.wait_ge(X[1].filled, X[1].at(('dvT', c)))
                    x = X[1].ap
                    tt(head_view(g.d_vb[0:n, :], P), head_view(x[0:n, :], P), bcast(gBeta[0:n, c, :], P), ALU.mult).then_inc(
                            X[1].drained, 1)
                    ve.wait_ge(X[1].drained, X[1].at(('dvT', c)))
                if li == 1:
                    ve.wait_ge(X[1].filled, X[1].at(('dkT', c)))
                    x = X[1].ap
                    tt(head_view(g.d_kd[0:n, :], P), head_view(x[0:n, :], P), bcast(gEK[0:n, c, :], P), ALU.mult).then_inc(
                            vec_steps.sem, vec_steps.next())
                    ve.wait_ge(vec_steps.sem, vec_steps.count)
                    tt(head_view(g.d_kb[0:n, :], P), head_view(x[0:n, :], P), bcast(gBE[0:n, c, :], P), ALU.mult).then_inc(
                            X[1].drained, 1)
                    ve.wait_ge(X[1].drained, X[1].at(('dkT', c)))
            ve.wait_ge(X[1].drained, X[1].at(('kc', c)))
            tt(head_view(g.d_qd, n), g.qkv[:, 0:4, cs], head_view(g.d_eg, n), ALU.mult).then_inc(
                    vec_out.sem, vec_out.next(('qd', c)))
            ve.wait_ge(vec_out.sem, vec_out.count)
            if c < 4:
                ve.wait_ge(X[0].filled, X[0].at(('dS', c)))
                x = X[0].ap
                for h in range(H):
                    hs = slice(h * P, h * P + P)
                    ins = stt(g.d_S[:, hs], g.d_S[:, hs], g.d_eg[:, h * P + P - 1:h * P + P], x[:, hs],
                              ALU.mult, ALU.add)
                    if h < H - 1:
                        ins.then_inc(vec_steps.sem, vec_steps.next())
                        ve.wait_ge(vec_steps.sem, vec_steps.count)
                    else:
                        ins.then_inc(X[0].drained, 1)
                        ve.wait_ge(X[0].drained, X[0].at(('dS', c)))
                ve.engine_nop().then_inc(vec_out.sem, vec_out.next(('d_state', c)))
                ve.wait_ge(vec_out.sem, vec_out.count)
            else:
                ve.wait_ge(X[1].drained, X[1].at('dwT'))
                def masked(b):
                    ts(g.d_kdm[b % 2], g.d_kd[0:NS, :], const('seq_of', NS)[:, b:b + 1], None, ALU.mult).then_inc(
                        vec_out.sem, vec_out.next(('dkdm', b)))
                masked(0)
                for b in range(DB):
                    ve.wait_ge(X[b % 2].filled, X[b % 2].at(('dS', c, b)))
                    if b < DB - 1:
                        masked(b + 1)
                    if b == 1:
                        ve.wait_ge(st_state.sem, st_state.at('dn'))
                    if b >= 2:
                        ve.wait_ge(st_ds[b % 2].sem, st_ds[b % 2].at(b - 2))
                    ve.wait_ge(ds_in[b % 2].sem, ds_in[b % 2].at(DB + b))
                    x = X[b % 2].ap
                    for h in range(H):
                        hs = slice(h * P, h * P + P)
                        e = h * NS + b * DS + DS - 1
                        ins = stt(g.d_sout[b % 2][:, hs], g.d_sin[b % 2][:, hs], g.d_eg[:, e:e + 1], x[:, hs],
                                  ALU.mult, ALU.add)
                        if h < H - 1:
                            ins.then_inc(vec_steps.sem, vec_steps.next())
                        else:
                            ins.then_inc(X[b % 2].drained, 1)
        for h in range(H):
            ve.wait_ge(act_out.sem, act_out.at(('drs', h)))
            o = g.qkv[:, 8 + h, :]
            stt(o, o, par('dnn'), g.d_rs[h % 2], ALU.mult, ALU.mult).then_inc(vec_steps.sem, vec_steps.next())
            ve.wait_ge(vec_steps.sem, vec_steps.count)
            tt(g.out_dn[:, h, :], g.out_dn[:, h, :], o, ALU.mult).then_inc(vec_out.sem, vec_out.next(('dout', h)))
            ve.wait_ge(vec_out.sem, vec_out.count)

        outs = (g.out_dn, g.out_ret, g.out_att)

        def bsplit(n):
            ve.wait_ge(act_out.sem, act_out.at(('bsplit', n)))
            tt(g.blo[n % 2][:, :, :], outs[n][:, :, :], g.bhi[n % 2][:, :, :].bitcast(F32), ALU.subtract).then_inc(
                    vec_out.sem, vec_out.next(('bsplit', n)))
            ve.wait_ge(vec_out.sem, vec_out.count)
        bsplit(0)
        bsplit(1)
        i = 0
        for n in range(3):
            if n == 1:
                bsplit(2)
            for d in range(4):
                for j in range(2):
                    k = 2 * d + j
                    ve.wait_ge(PJ[0].drained, PJ[0].at(('gate', n, d, j)))
                    ve.wait_ge(PJ[1].filled, PJ[1].at(('br', n, d, j)))
                    x = PJ[1].ap
                    s = g.sig[i % 2]
                    dst = g.m[:, k, :] if n == 0 else s[:, :]
                    tt(halves(dst), halves(s[:, :]), x[:, :, 0:HT], ALU.mult).then_inc(PJ[1].drained, 1)
                    ve.wait_ge(PJ[1].drained, PJ[1].at(('br', n, d, j)))
                    if n:
                        tt(g.m[:, k, :], g.m[:, k, :], s[:, :], ALU.add).then_inc(
                                vec_out.sem, vec_out.next(('mul', i)))
                        ve.wait_ge(vec_out.sem, vec_out.count)
                    else:
                        ve.engine_nop().then_inc(vec_out.sem, vec_out.next(('mul', i)))
                        ve.wait_ge(vec_out.sem, vec_out.count)
                    if n == 2:
                        ve.engine_nop().then_inc(vec_out.sem, vec_out.next(('m', k)))
                        ve.wait_ge(vec_out.sem, vec_out.count)
                    i += 1
        for k in range(KD):
            ve.wait_ge(act_out.sem, act_out.at(('msplit', k)))
            tt(g.ulo[:, k, :], g.m[:, k, :], g.uhi[:, k, :].bitcast(F32), ALU.subtract).then_inc(
                    vec_out.sem, vec_out.next(('msplit', k)))
            ve.wait_ge(vec_out.sem, vec_out.count)
        ve.wait_ge(x_in.sem, x_in.at('again'))
        for k in range(KD):
            ve.wait_ge(PJ[k % 2].filled, PJ[k % 2].at(('wo', k)))
            x = PJ[k % 2].ap
            tt(halves(g.x[:, k, :]), halves(g.x[:, k, :]), x[:, :, 0:HT], ALU.add).then_inc(PJ[k % 2].drained, 1)
            ve.wait_ge(PJ[k % 2].drained, PJ[k % 2].at(('wo', k)))
            ve.engine_nop().then_inc(vec_out.sem, vec_out.next(('h', k)))
            ve.wait_ge(vec_out.sem, vec_out.count)
        ve.wait_ge(act_out.sem, act_out.at('rstd1'))
        for k in range(KD + 1):
            if k < KD:
                stt(g.f_conv[k % 2][:, 0:NT], g.x[:, k, :], par('ffn', k), g.f_act[:, :], ALU.mult, ALU.mult).then_inc(
                        vec_out.sem, vec_out.next(('hf', k)))
                ve.wait_ge(vec_out.sem, vec_out.count)
            if k:
                j = k - 1
                ve.wait_ge(act_out.sem, act_out.at(('hh', j)))
                tt(g.ulo[:, j, :], g.f_conv[j % 2][:, 0:NT], g.uhi[:, j, :].bitcast(F32), ALU.subtract).then_inc(
                        vec_out.sem, vec_out.next(('hn', j)))
                ve.wait_ge(vec_out.sem, vec_out.count)
        ve.memset(g.f_pad[0][:, 0:2], 0.0).then_inc(vec_steps.sem, vec_steps.next())
        ve.wait_ge(vec_steps.sem, vec_steps.count)
        ve.memset(g.f_pad[1][:, 0:2], 0.0).then_inc(vec_out.sem, vec_out.next('f_pads'))
        ve.wait_ge(vec_out.sem, vec_out.count)

        for f in range(2):
            for j in range(FH):
                for i in range(2):
                    ve.wait_ge(act_out.sem, act_out.at(('fpad', f, j, i)))
                    src, y, t = g.f_pad[i], g.f_conv[i][:, 0:SW - 2], f * FH + j + i * FT
                    ts(y, src[:, 0:SW - 2], par('f0', t), None, ALU.mult).then_inc(vec_steps.sem, vec_steps.next())
                    ve.wait_ge(vec_steps.sem, vec_steps.count)
                    stt(y, src[:, 1:SW - 1], par('f0', 2 * FT + t), y, ALU.mult, ALU.add).then_inc(
                            vec_steps.sem, vec_steps.next())
                    ve.wait_ge(vec_steps.sem, vec_steps.count)
                    stt(y, src[:, 2:SW], par('f2', t), y, ALU.mult, ALU.add).then_inc(
                            vec_out.sem, vec_out.next(('fconv', f, j, i)))
                    ve.wait_ge(vec_out.sem, vec_out.count)
                ve.wait_ge(act_out.sem, act_out.at(('fsilu', f, j)))
                y = g.f_conv[1]
                tt(g.f_act[:, 0:SEQ], g.f_act[:, 0:SEQ], y[:, 0:SEQ], ALU.mult).then_inc(
                        vec_steps.sem, vec_steps.next())
                ve.wait_ge(vec_steps.sem, vec_steps.count)
                fs = g.f_act[:, SEQ:NT].rearrange("p (b t) -> p b t", b=DB)
                tt(fs, fs, y[:, 514:514 + 48].rearrange("p (b t) -> p b t", b=DB)[:, :, 0:4], ALU.mult).then_inc(
                        vec_out.sem, vec_out.next(('hprod', f, j)))
                ve.wait_ge(vec_out.sem, vec_out.count)
                ve.wait_ge(act_out.sem, act_out.at(('hhi', f, j)))
                tt(g.hlo[:, j, :], g.f_act[:, :], g.hhi[:, j, :].bitcast(F32), ALU.subtract).then_inc(
                        vec_out.sem, vec_out.next(('hff', f, j)))
                ve.wait_ge(vec_out.sem, vec_out.count)
            for c in range(KD):
                ve.wait_ge(PJ[c % 2].filled, PJ[c % 2].at(('down', f, c)))
                x = PJ[c % 2].ap
                tt(halves(g.x[:, c, :]), halves(g.x[:, c, :]), x[:, :, 0:HT], ALU.add).then_inc(PJ[c % 2].drained, 1)
                ve.wait_ge(PJ[c % 2].drained, PJ[c % 2].at(('down', f, c)))


def final(g):
    nc, io = g.nc, g.io
    ones, ident = g.const('ones'), g.const('ident')
    made, normed, squares = (g.counter(n) for n in ("fin_act", "fin_vec", "fin_pe"))
    stored = [g.counter(f"fin_stored{i}") for i in range(2)]
    PJ, X = g.PJ, g.X
    with nc.Block() as block:
        @block.sync
        def _(sp):
            for c in range(5):
                sp.wait_ge(made.sem, made.at(('y', c)))
                if c < 4:
                    dst = io['y_prompt'].rearrange("a (c p) n -> (a c) p n", p=P)[c]
                else:
                    dst = io['y_sample'].rearrange("b t n -> (b t) n")
                sp.dma_start(dst, g.ytok[c % 2][0:P if c < 4 else NS, :]).then_inc(
                        stored[c % 2].sem, stored[c % 2].next(c, 16))
            sp.wait_ge(stored[0].sem, stored[0].at(4))
            sp.wait_ge(stored[1].sem, stored[1].at(3))

        @block.scalar
        def _(ac):
            for k in range(KD):
                if k >= 2:
                    ac.wait_ge(squares.sem, squares.at(k - 2))
                ac.activation(g.xsq[k % 2][:, :], g.x[:, k, :], ACT.Square).then_inc(
                        made.sem, made.next(('sq', k)))
                ac.wait_ge(made.sem, made.count)
            ac.wait_ge(PJ[0].filled, PJ[0].at('rms_fin'))
            x = PJ[0].ap
            ac.activation(halves(g.rstd0[:, :]), x[:, :, 0:HT], ACT.Ln, scale=1.0 / D, bias=g.eps()).then_inc(
                    PJ[0].drained, 1)
            ac.wait_ge(PJ[0].drained, PJ[0].at('rms_fin'))
            ac.activation(g.rstd0[:, :], g.rstd0[:, :], ACT.Exp, scale=-0.5).then_inc(made.sem, made.next('rstd'))
            ac.wait_ge(made.sem, made.count)
            for c in range(5):
                n = P if c < 4 else NS
                if c >= 2:
                    ac.wait_ge(stored[c % 2].sem, stored[c % 2].at(c - 2))
                for half in range(2):
                    b = X[half]
                    ac.wait_ge(b.filled, b.at(('y', c, half)))
                    x = b.ap
                    ac.activation(g.ytok[c % 2][0:n, half * 512:half * 512 + 512], x[0:n, :], ACT.Copy).then_inc(
                            b.drained, 1)
                    ac.wait_ge(b.drained, b.at(('y', c, half)))
                ac.activation(g.stat[:, 0:1], g.eps(), ACT.Copy).then_inc(made.sem, made.next(('y', c)))
                ac.wait_ge(made.sem, made.count)

        @block.vector
        def _(ve):
            ve.wait_ge(made.sem, made.at('rstd'))
            for k in range(KD):
                gain = g.par[:, PAR0_N + PAR1['fin'] + k:PAR0_N + PAR1['fin'] + k + 1]
                ve.scalar_tensor_tensor(g.x[:, k, :], g.x[:, k, :], gain, g.rstd0[:, :], ALU.mult, ALU.mult).then_inc(
                        normed.sem, normed.next(k))
                ve.wait_ge(normed.sem, normed.count)

        @block.tensor
        def _(pe):
            pe.wait_ge(PJ[0].drained, PJ[0].claim('rms_fin'))
            out = PJ[0].ap
            for k in range(KD):
                pe.wait_ge(made.sem, made.at(('sq', k)))
                for half in range(2):
                    mm = pe.matmul(out[:, half, 0:HT], ones, g.xsq[k % 2][:, half * HT:half * HT + HT],
                                   start=(k == 0), stop=(k == KD - 1))
                if k < KD - 1:
                    mm.then_inc(squares.sem, squares.next(k))
            mm.then_inc(PJ[0].filled, 1)
            pe.wait_ge(normed.sem, normed.at(KD - 1))
            for c in range(5):
                cs, n = chunk_of(c)
                for half in range(2):
                    pe.wait_ge(X[half].drained, X[half].claim(('y', c, half)))
                    x = X[half].ap
                    for k in range(4):
                        mm = pe.transpose(x[0:n, k * P:k * P + P], g.x[:, half * 4 + k, cs], ident)
                    mm.then_inc(X[half].filled, 1)


def build(nc, io, consts, onehots, scratch_x, scratch_b, layout, onehot_at, known):
    g = Program(nc, io, consts, onehots, scratch_x, scratch_b, known)
    with g.ctx:
        allocate(g, layout)
        setup(g, onehot_at)
        g.clear_semaphores()
        for s in g.learn.made.values():
            s.fresh()
        with nc.Fori(0, DEPTH) as layer:
            with nc.Block() as g.block:
                layer_program(g, layer)
            g.clear_semaphores()
        for s in g.learn.made.values():
            s.fresh()
        final(g)
    return g.learn.learned()



def packed(arrays, rows):
    at, o = {}, 0
    for k, v in arrays.items():
        at[k] = (o, v.shape[1])
        o += v.shape[1]
    at['_n'] = o
    return np.concatenate([v[0:rows] for v in arrays.values()], 1), at


def kernel(**inputs):
    from concourse import bacc
    from concourse.bass_utils import run_bass_kernel_spmd

    consts, layout = packed(const_arrays(), P)
    onehots, onehot_at = packed(onehot_arrays(), NBUCKET)
    arrays = {f"in_{n}": np.ascontiguousarray(inputs[n]) for n in IN_NAMES}
    arrays["in_consts"], arrays["in_onehots"] = consts, onehots

    def program(known):
        nc = bacc.Bacc("TRN2", target_bir_lowering=False, num_devices=1)
        dram = {n: nc.dram_tensor(n, a.shape, mybir.dt.from_np(a.dtype), kind="ExternalInput").ap()
                for n, a in arrays.items()}
        io = {n: dram[f"in_{n}"] for n in IN_NAMES}
        for n, shape in OUT_SHAPES:
            io[n] = nc.dram_tensor(f"out_{n}", shape, F32, kind="ExternalOutput").ap()
        scratch_x = nc.dram_tensor("scratch_x", (P, KD * NT), F32, kind="Internal").ap()
        scratch_b = nc.dram_tensor("scratch_b", (P * H * 383,), F32, kind="Internal").ap()
        return nc, build(nc, io, dram["in_consts"], dram["in_onehots"], scratch_x, scratch_b, layout, onehot_at, known)

    _, counted = program(Known())
    nc, _ = program(counted)
    r = run_bass_kernel_spmd(nc, [arrays], core_ids=[0])
    return tuple(r.results[0][f"out_{n}"] for n, _ in OUT_SHAPES)
```
